# Optimizing a Trainium2 kernel written in Bass

```python
import jax, jax.numpy as jnp
from jax import lax
import numpy as np
import math
import jax
import jax.numpy as jnp

D_MODEL = 1024
BATCH = 1
SEQ = 512
DEPTH = 2

GRID_W = 64
CTX_LEN = 256
N_MIXERS = 4
D_FF = -(-8 * D_MODEL // (3 * 256)) * 256
DEEPNORM_ALPHA = (2 * DEPTH) ** 0.25
DEEPNORM_BETA = (8 * DEPTH) ** -0.25
LN_EPS = 1e-5
RMS_EPS = 1e-6
ROPE_BASE = 10000.0
CHUNK = 64
NEG_INF = -1e30

RET_HEADS = 4
RET_DK = D_MODEL // RET_HEADS
RET_DV = 2 * RET_DK
NA_HEADS = 16
NA_DH = D_MODEL // NA_HEADS
NA_WIN_ROWS = 8
NA_WIN_COLS = 16
NA_QBLOCK_W = 16
NA_BAND_W = NA_QBLOCK_W + NA_WIN_COLS
MLA_HEADS = 16
MLA_NOPE = 64
MLA_ROPE = 32
MLA_V = 64
MLA_Q_LORA = 512
MLA_KV_LORA = 256
MLA_QBLOCK = 128
HG_EXPAND = 128
HG_HEADS = D_MODEL // HG_EXPAND
HG_DI = D_MODEL // HG_HEADS
HG_FDIM = HG_HEADS * HG_EXPAND


def layer_norm(x, g, b):
    xf = x.astype(jnp.float32)
    xc = xf - jnp.mean(xf, -1, keepdims=True)
    var = jnp.mean(xc * xc, -1, keepdims=True)
    return (xc * lax.rsqrt(var + LN_EPS) * g.astype(jnp.float32) + b.astype(jnp.float32)).astype(x.dtype)

def rms_norm(x, g=None):
    xf = x.astype(jnp.float32)
    y = xf * lax.rsqrt(jnp.mean(xf * xf, -1, keepdims=True) + RMS_EPS)
    if g is not None:
        y = y * g.astype(jnp.float32)
    return y.astype(x.dtype)

def modulate(h, shift, scale):
    return h * (1 + scale) + shift

def axial_rope(n_tokens, rot_dim):
    t = jnp.arange(n_tokens)
    rows = (t // GRID_W).astype(jnp.float32)
    cols = (t % GRID_W).astype(jnp.float32)
    n_freq = rot_dim // 4
    inv = ROPE_BASE ** (-jnp.arange(n_freq, dtype=jnp.float32) / n_freq)
    ang = jnp.concatenate([rows[:, None] * inv, cols[:, None] * inv], -1)
    return jnp.cos(ang)[:, None, :], jnp.sin(ang)[:, None, :]

def apply_rope(x, cos, sin):
    x1, x2 = jnp.split(x.astype(jnp.float32), 2, axis=-1)
    return jnp.concatenate([x1 * cos - x2 * sin, x1 * sin + x2 * cos], -1).astype(x.dtype)

def chunk_gla(q, k, v, log_f, s0):
    B, H, L, dk = q.shape
    dv = v.shape[-1]
    n = L // CHUNK

    def to_chunks(a):
        return a.astype(jnp.float32).reshape(B, H, n, CHUNK, a.shape[-1]).transpose(2, 0, 1, 3, 4)

    mask = jnp.tril(jnp.ones((CHUNK, CHUNK), bool))

    def step(S, inp):
        qi, ki, vi, gi = inp
        b = jnp.cumsum(gi, axis=-2)
        b_last = b[..., -1:, :]
        q_d = qi * jnp.exp(b)
        att = jnp.where(mask, jnp.einsum('bhtk,bhsk->bhts', q_d, ki * jnp.exp(-b)), 0.0)
        o = jnp.einsum('bhts,bhsv->bhtv', att, vi) + jnp.einsum('bhtk,bhkv->bhtv', q_d, S)
        S_new = jnp.exp(b_last[..., 0, :])[..., None] * S + jnp.einsum('bhsk,bhsv->bhkv', ki * jnp.exp(b_last - b), vi)
        return S_new, o

    S_fin, oc = lax.scan(step, s0, (to_chunks(q), to_chunks(k), to_chunks(v), to_chunks(log_f)))
    return oc.transpose(1, 2, 0, 3, 4).reshape(B, H, L, dv), S_fin

def bidirectional_scan(ctx_terms, lat_terms):
    qc, kcf, kcb, vc, gcf, gcb = ctx_terms
    ql, klf, klb, vl, glf, glb = lat_terms
    B, H, _, dk = qc.shape
    s0 = jnp.zeros((B, H, dk, vc.shape[-1]), jnp.float32)
    flip = lambda t: jnp.flip(t, axis=2)
    o_cf, s_cf = chunk_gla(qc, kcf, vc, gcf, s0)
    o_cb, s_cb = chunk_gla(flip(qc), flip(kcb), flip(vc), flip(gcb), s0)
    o_lf, _ = chunk_gla(ql, klf, vl, glf, s_cf)
    o_lb, _ = chunk_gla(flip(ql), flip(klb), flip(vl), flip(glb), s_cb)
    return o_cf + flip(o_cb), o_lf + flip(o_lb)

def retention_mixer(a_ctx, a_lat, w_in, decay_param, w_out, want_ctx):
    B, L, _ = a_lat.shape
    hk, hv = RET_HEADS * RET_DK, RET_HEADS * RET_DV
    log_gamma = -jnp.exp(decay_param.astype(jnp.float32))

    def project(a, rope):
        n = a.shape[1]
        q, k, v, g = jnp.split(a @ w_in, [hk, 2 * hk, 2 * hk + hv], axis=-1)
        q = q.reshape(B, n, RET_HEADS, RET_DK)
        k = k.reshape(B, n, RET_HEADS, RET_DK)
        if rope is not None:
            q, k = apply_rope(q, *rope), apply_rope(k, *rope)
        k = k * RET_DK ** -0.5
        v = v.reshape(B, n, RET_HEADS, RET_DV)
        decay = lambda lg: jnp.broadcast_to(lg[None, :, None, None], (B, RET_HEADS, n, RET_DK))
        qh, kh, vh = (t.transpose(0, 2, 1, 3) for t in (q, k, v))
        return (qh, kh, kh, vh, decay(log_gamma[0]), decay(log_gamma[1])), g

    ctx_terms, g_ctx = project(a_ctx, None)
    lat_terms, g_lat = project(a_lat, axial_rope(L, RET_DK))
    o_ctx, o_lat = bidirectional_scan(ctx_terms, lat_terms)

    def readout(o, g):
        n = o.shape[2]
        y = rms_norm(o).transpose(0, 2, 1, 3).reshape(B, n, hv).astype(g.dtype)
        return (jax.nn.silu(g) * y) @ w_out

    return (readout(o_ctx, g_ctx) if want_ctx else None), readout(o_lat, g_lat)

def neighbourhood_mixer(a_ctx, a_lat, w_qkv, rpb, w_out, want_ctx):
    B, L, _ = a_lat.shape
    Lc = a_ctx.shape[1]
    rows = L // GRID_W
    wr = min(NA_WIN_ROWS, rows)
    scale = NA_DH ** -0.5
    q, k, v = jnp.split(a_lat @ w_qkv, 3, axis=-1)
    grid = lambda t: t.reshape(B, rows, GRID_W, NA_HEADS, NA_DH)
    q, k, v = grid(q * scale), grid(k), grid(v)
    qc, kc, vc = (t.reshape(B, Lc, NA_HEADS, NA_DH) for t in jnp.split(a_ctx @ w_qkv, 3, axis=-1))

    n_cb = GRID_W // NA_QBLOCK_W
    band0 = np.clip(np.arange(n_cb) * NA_QBLOCK_W - NA_WIN_COLS // 2, 0, GRID_W - NA_BAND_W)
    kcol = band0[:, None] + np.arange(NA_BAND_W)
    qcol = np.arange(GRID_W).reshape(n_cb, NA_QBLOCK_W)
    wstart = np.clip(qcol - NA_WIN_COLS // 2, 0, GRID_W - NA_WIN_COLS)
    kc3 = kcol[:, None, :]
    col_ok = (kc3 >= wstart[..., None]) & (kc3 < wstart[..., None] + NA_WIN_COLS)
    c_idx = np.clip(kc3 - qcol[..., None] + NA_WIN_COLS - 1, 0, 2 * NA_WIN_COLS - 2)

    def row(r):
        rs = jnp.clip(r - wr // 2, 0, rows - wr)
        qr = lax.dynamic_index_in_dim(q, r, axis=1, keepdims=False).reshape(B, n_cb, NA_QBLOCK_W, NA_HEADS, NA_DH)
        kb = lax.dynamic_slice_in_dim(k, rs, wr, axis=1)[:, :, kcol]
        vb = lax.dynamic_slice_in_dim(v, rs, wr, axis=1)[:, :, kcol]
        r_idx = rs + jnp.arange(wr) - r + NA_WIN_ROWS - 1
        bias = rpb[:, r_idx[None, None, :, None], c_idx[:, :, None, :]]
        s_lat = jnp.einsum('bnqhd,brnkhd->bhnqrk', qr, kb).astype(jnp.float32) + bias[None].astype(jnp.float32)
        s_lat = jnp.where(col_ok[:, :, None, :], s_lat, NEG_INF).reshape(B, NA_HEADS, n_cb, NA_QBLOCK_W, wr * NA_BAND_W)
        s_ctx = jnp.einsum('bnqhd,bchd->bhnqc', qr, kc).astype(jnp.float32)
        p = jax.nn.softmax(jnp.concatenate([s_lat, s_ctx], -1), -1).astype(v.dtype)
        p_lat = p[..., :wr * NA_BAND_W].reshape(B, NA_HEADS, n_cb, NA_QBLOCK_W, wr, NA_BAND_W)
        o = jnp.einsum('bhnqrk,brnkhd->bnqhd', p_lat, vb) + jnp.einsum('bhnqc,bchd->bnqhd', p[..., wr * NA_BAND_W:], vc)
        return o.reshape(B, GRID_W, NA_HEADS * NA_DH)

    o_lat = lax.map(row, jnp.arange(rows)).transpose(1, 0, 2, 3).reshape(B, L, NA_HEADS * NA_DH)
    y_ctx = None
    if want_ctx:
        s = jnp.einsum('bqhd,bkhd->bhqk', qc * scale, kc).astype(jnp.float32)
        p = jax.nn.softmax(s, -1).astype(vc.dtype)
        y_ctx = jnp.einsum('bhqk,bkhd->bqhd', p, vc).reshape(B, Lc, NA_HEADS * NA_DH) @ w_out
    return y_ctx, o_lat @ w_out

def mla_mixer(a_ctx, a_lat, w_down, q_norm, kv_norm, w_uq, w_ukv, w_out, want_ctx):
    B, L, _ = a_lat.shape
    scale = (MLA_NOPE + MLA_ROPE) ** -0.5

    def project(a, rope):
        n = a.shape[1]
        cq, ckv, kr = jnp.split(a @ w_down, [MLA_Q_LORA, MLA_Q_LORA + MLA_KV_LORA], axis=-1)
        q = (rms_norm(cq, q_norm) @ w_uq).reshape(B, n, MLA_HEADS, MLA_NOPE + MLA_ROPE)
        kv = (rms_norm(ckv, kv_norm) @ w_ukv).reshape(B, n, MLA_HEADS, MLA_NOPE + MLA_V)
        q_nope, q_rope = jnp.split(q, [MLA_NOPE], axis=-1)
        k_nope, v = jnp.split(kv, [MLA_NOPE], axis=-1)
        kr = kr[:, :, None, :]
        if rope is not None:
            q_rope, kr = apply_rope(q_rope, *rope), apply_rope(kr, *rope)
        q = jnp.concatenate([q_nope, q_rope], -1) * scale
        k = jnp.concatenate([k_nope, jnp.broadcast_to(kr, (B, n, MLA_HEADS, MLA_ROPE))], -1)
        return q, k, v

    qc, kc, vc = project(a_ctx, None)
    ql, kl, vl = project(a_lat, axial_rope(L, MLA_ROPE))
    k_all = jnp.concatenate([kc, kl], axis=1)
    v_all = jnp.concatenate([vc, vl], axis=1)

    def attend(qb, keys, vals):
        s = jnp.einsum('bqhd,bkhd->bhqk', qb, keys).astype(jnp.float32)
        p = jax.nn.softmax(s, -1).astype(vals.dtype)
        return jnp.einsum('bhqk,bkhd->bqhd', p, vals)

    nb = L // MLA_QBLOCK
    qblocks = ql.reshape(B, nb, MLA_QBLOCK, MLA_HEADS, MLA_NOPE + MLA_ROPE).transpose(1, 0, 2, 3, 4)
    o = lax.map(lambda qb: attend(qb, k_all, v_all), qblocks)
    o_lat = o.transpose(1, 0, 2, 3, 4).reshape(B, L, MLA_HEADS * MLA_V)
    y_ctx = attend(qc, kc, vc).reshape(B, -1, MLA_HEADS * MLA_V) @ w_out if want_ctx else None
    return y_ctx, o_lat @ w_out

def hgrn2_mixer(a_ctx, a_lat, w_in, lower_bounds, norm_g, w_out, layer_idx, want_ctx):
    B = a_lat.shape[0]
    lb_soft = jax.nn.softmax(lower_bounds.astype(jnp.float32), axis=0)
    lb = (jnp.cumsum(lb_soft, axis=0) - lb_soft[0])[layer_idx]

    def project(a):
        n = a.shape[1]
        q, f_f, f_b, i, g = jnp.split(a @ w_in, [HG_FDIM, 2 * HG_FDIM, 3 * HG_FDIM, 3 * HG_FDIM + HG_HEADS * HG_DI], axis=-1)
        heads = lambda t, d: t.reshape(B, n, HG_HEADS, d).transpose(0, 2, 1, 3)
        q = heads(jax.nn.silu(q), HG_EXPAND) * HG_EXPAND ** -0.5

        def gate(f):
            forget = lb + (1 - lb) * jax.nn.sigmoid(f.astype(jnp.float32))
            return heads(1 - forget, HG_EXPAND), heads(jnp.log(forget), HG_EXPAND)

        kf, gf = gate(f_f)
        kb, gb = gate(f_b)
        return (q, kf, kb, heads(i, HG_DI), gf, gb), g

    ctx_terms, g_ctx = project(a_ctx)
    lat_terms, g_lat = project(a_lat)
    o_ctx, o_lat = bidirectional_scan(ctx_terms, lat_terms)

    def readout(o, g):
        n = o.shape[2]
        y = rms_norm(o, norm_g).transpose(0, 2, 1, 3).reshape(B, n, HG_HEADS * HG_DI).astype(g.dtype)
        return (y * jax.nn.silu(g)) @ w_out

    return (readout(o_ctx, g_ctx) if want_ctx else None), readout(o_lat, g_lat)

def swiglu(a, w13, w2):
    gate, up = jnp.split(a @ w13, 2, axis=-1)
    return (jax.nn.silu(gate) * up) @ w2

def first_inputs(seed: int = 0) -> dict:
    key = jax.random.key(seed)
    ks = iter(jax.random.split(key, 32))
    nrm = lambda shape, std: std * jax.random.normal(next(ks), shape, jnp.float32)
    D, F, beta = D_MODEL, D_FF, DEEPNORM_BETA
    ret_decay_base = jnp.log(-jnp.log1p(-(2.0 ** (-5.0 - jnp.arange(RET_HEADS, dtype=jnp.float32)))))
    return {
        'x': nrm((BATCH, SEQ, D), 1.0),
        'c': nrm((BATCH, D), 1.0),
        'ctx': nrm((BATCH, CTX_LEN, D), 1.0),
        'c_ctx': nrm((D,), 1.0),
        'ada_w': nrm((DEPTH, D, 6 * D), D ** -0.5),
        'ada_b': nrm((DEPTH, 6 * D), 0.01),
        'ln_g': 1.0 + nrm((DEPTH, 2, D), 0.01),
        'ln_b': nrm((DEPTH, 2, D), 0.01),
        'ffn_w13': nrm((DEPTH, D, 2 * F), D ** -0.5),
        'ffn_w2': nrm((DEPTH, F, D), beta * F ** -0.5),
        'ret_w_in': nrm((D, 2 * RET_HEADS * RET_DK + 2 * RET_HEADS * RET_DV), D ** -0.5),
        'ret_decay': ret_decay_base[None, :] + nrm((2, RET_HEADS), 0.01),
        'ret_w_out': nrm((RET_HEADS * RET_DV, D), beta * (RET_HEADS * RET_DV) ** -0.5),
        'na_w_qkv': nrm((D, 3 * NA_HEADS * NA_DH), D ** -0.5),
        'na_rpb': nrm((NA_HEADS, 2 * NA_WIN_ROWS - 1, 2 * NA_WIN_COLS - 1), 0.02),
        'na_w_out': nrm((NA_HEADS * NA_DH, D), beta * (NA_HEADS * NA_DH) ** -0.5),
        'mla_w_down': nrm((D, MLA_Q_LORA + MLA_KV_LORA + MLA_ROPE), D ** -0.5),
        'mla_q_norm': 1.0 + nrm((MLA_Q_LORA,), 0.01),
        'mla_kv_norm': 1.0 + nrm((MLA_KV_LORA,), 0.01),
        'mla_w_uq': nrm((MLA_Q_LORA, MLA_HEADS * (MLA_NOPE + MLA_ROPE)), MLA_Q_LORA ** -0.5),
        'mla_w_ukv': nrm((MLA_KV_LORA, MLA_HEADS * (MLA_NOPE + MLA_V)), MLA_KV_LORA ** -0.5),
        'mla_w_out': nrm((MLA_HEADS * MLA_V, D), beta * (MLA_HEADS * MLA_V) ** -0.5),
        'hg_w_in': nrm((D, 3 * HG_FDIM + 2 * HG_HEADS * HG_DI), D ** -0.5),
        'hg_lower_bounds': nrm((DEPTH, HG_FDIM), 0.1),
        'hg_norm_g': 1.0 + nrm((HG_DI,), 0.01),
        'hg_w_out': nrm((HG_HEADS * HG_DI, D), beta * (HG_HEADS * HG_DI) ** -0.5),
    }

def first_block(x, c, ctx, c_ctx, ada_w, ada_b, ln_g, ln_b, ffn_w13, ffn_w2,
              ret_w_in, ret_decay, ret_w_out,
              na_w_qkv, na_rpb, na_w_out,
              mla_w_down, mla_q_norm, mla_kv_norm, mla_w_uq, mla_w_ukv, mla_w_out,
              hg_w_in, hg_lower_bounds, hg_norm_g, hg_w_out):
    h_lat, h_ctx = x, ctx
    cond_lat = jax.nn.silu(c)[:, None, :]
    cond_ctx = jax.nn.silu(c_ctx)[None, None, :]
    for i in range(DEPTH):
        want_ctx = i < DEPTH - 1
        m_lat = jnp.split(cond_lat @ ada_w[i] + ada_b[i], 6, axis=-1)
        m_ctx = jnp.split(cond_ctx @ ada_w[i] + ada_b[i], 6, axis=-1)
        a_lat = modulate(h_lat, m_lat[0], m_lat[1])
        a_ctx = modulate(h_ctx, m_ctx[0], m_ctx[1])
        kind = i % N_MIXERS
        if kind == 0:
            y_ctx, y_lat = retention_mixer(a_ctx, a_lat, ret_w_in, ret_decay, ret_w_out, want_ctx)
        elif kind == 1:
            y_ctx, y_lat = neighbourhood_mixer(a_ctx, a_lat, na_w_qkv, na_rpb, na_w_out, want_ctx)
        elif kind == 2:
            y_ctx, y_lat = mla_mixer(a_ctx, a_lat, mla_w_down, mla_q_norm, mla_kv_norm, mla_w_uq, mla_w_ukv, mla_w_out, want_ctx)
        else:
            y_ctx, y_lat = hgrn2_mixer(a_ctx, a_lat, hg_w_in, hg_lower_bounds, hg_norm_g, hg_w_out, i, want_ctx)
        h_lat = layer_norm(DEEPNORM_ALPHA * h_lat + m_lat[2] * y_lat, ln_g[i, 0], ln_b[i, 0])
        f_lat = swiglu(modulate(h_lat, m_lat[3], m_lat[4]), ffn_w13[i], ffn_w2[i])
        h_lat = layer_norm(DEEPNORM_ALPHA * h_lat + m_lat[5] * f_lat, ln_g[i, 1], ln_b[i, 1])
        if want_ctx:
            h_ctx = layer_norm(DEEPNORM_ALPHA * h_ctx + m_ctx[2] * y_ctx, ln_g[i, 0], ln_b[i, 0])
            f_ctx = swiglu(modulate(h_ctx, m_ctx[3], m_ctx[4]), ffn_w13[i], ffn_w2[i])
            h_ctx = layer_norm(DEEPNORM_ALPHA * h_ctx + m_ctx[5] * f_ctx, ln_g[i, 1], ln_b[i, 1])
    return h_lat


DEPTH_2 = 1

HEAD_DIM = 64
SCALE = HEAD_DIM ** -0.5
NEG_INF_2 = -1e30
EPS = 1e-6
A_GROUPS = ((128, 1), (512, 4), (2048, 16))
A_HEADS_PER_GROUP = 4
A_HEADS = A_HEADS_PER_GROUP * len(A_GROUPS)
A_WIDTH = A_HEADS * HEAD_DIM
A_OUT = A_HEADS_PER_GROUP * HEAD_DIM
A_BLOCK = max(w // d for w, d in A_GROUPS)
LRU_WIDTH = D_MODEL // 2
LRU_BLOCKS = 8
LRU_BLOCK_DIM = LRU_WIDTH // LRU_BLOCKS
CONV_WIDTH = 4
LRU_C = 8.0
C_HEADS = 8
C_WIDTH = C_HEADS * HEAD_DIM
MOBA_BLOCK = 256
MOBA_TOPK = 3
MOBA_Q_CHUNK = 32
REL_BUCKETS = 32
REL_MAX_DIST = 2048
REL_HEADS = A_HEADS + C_HEADS
FFN_HIDDEN = -(-8 * D_MODEL // (3 * 256)) * 256
IN_SIZES = (A_WIDTH, A_WIDTH, A_WIDTH, LRU_WIDTH, LRU_WIDTH, C_WIDTH, C_WIDTH, C_WIDTH, 3 * D_MODEL)
IN_COLS = sum(IN_SIZES)


def rms_norm_2(x, g):
    xf = x.astype(jnp.float32)
    y = xf * lax.rsqrt(jnp.mean(xf * xf, axis=-1, keepdims=True) + EPS)
    return (y * g.astype(jnp.float32)).astype(x.dtype)

def rel_bucket(dist):
    max_exact = REL_BUCKETS // 2
    d = jnp.maximum(dist, 0)
    df = jnp.maximum(d, 1).astype(jnp.float32)
    large = max_exact + (jnp.log(df / max_exact) / math.log(REL_MAX_DIST / max_exact)
                         * (REL_BUCKETS - max_exact)).astype(jnp.int32)
    large = jnp.minimum(large, REL_BUCKETS - 1)
    return jnp.where(d < max_exact, d, large)

def dilated_window_attention(q, k, v, dilation, n_back, bias_tab):
    B, S, H, E = q.shape
    L = S // dilation
    nb = -(-L // A_BLOCK)
    Lp = nb * A_BLOCK

    def to_sub(t):
        t = t.reshape(B, L, dilation, H, E).transpose(0, 2, 3, 1, 4)
        t = jnp.pad(t, ((0, 0), (0, 0), (0, 0), (0, Lp - L), (0, 0)))
        return t.reshape(B, dilation, H, nb, A_BLOCK, E)

    qb, kb, vb = to_sub(q), to_sub(k), to_sub(v)

    def with_prev(t):
        prev = jnp.pad(t, ((0, 0), (0, 0), (0, 0), (1, 0), (0, 0), (0, 0)))[:, :, :, :nb]
        return jnp.concatenate([prev, t], axis=4)

    kk, vv = with_prev(kb), with_prev(vb)
    qi = jnp.arange(A_BLOCK)[:, None] + A_BLOCK
    kj = jnp.arange(2 * A_BLOCK)[None, :]
    delta = qi - kj
    band = (delta >= 0) & (delta <= n_back)
    has_prev = (jnp.arange(nb)[:, None, None] > 0) | (kj >= A_BLOCK)[None]
    valid = band[None] & has_prev
    bias = bias_tab.astype(jnp.float32)[rel_bucket(delta * dilation)]
    bias = jnp.transpose(bias, (2, 0, 1))
    logits = jnp.einsum('bdhnqe,bdhnke->bdhnqk', qb, kk).astype(jnp.float32) * SCALE
    logits = logits + bias[None, None, :, None]
    logits = jnp.where(valid[None, None, None], logits, NEG_INF_2)
    m = jnp.max(logits, axis=-1, keepdims=True)
    p = jnp.exp(logits - m)
    den = jnp.sum(p, axis=-1, keepdims=True)
    o = jnp.einsum('bdhnqk,bdhnke->bdhnqe', p, vv.astype(jnp.float32)) / den
    lse = (m + jnp.log(den))[..., 0]
    o = o.reshape(B, dilation, H, Lp, E)[:, :, :, :L].transpose(0, 3, 1, 2, 4).reshape(B, S, H, E)
    lse = lse.reshape(B, dilation, H, Lp)[:, :, :, :L].transpose(0, 3, 1, 2).reshape(B, S, H)
    return o, lse

def rg_lru_branch(xb, gb, conv_w, conv_b, w_a, b_a, w_x, b_x, lam):
    B, S, W = xb.shape
    xp = jnp.pad(xb, ((0, 0), (CONV_WIDTH - 1, 0), (0, 0)))
    xc = conv_b
    for i in range(CONV_WIDTH):
        xc = xc + xp[:, i:i + S] * conv_w[i]
    xr = xc.reshape(B, S, LRU_BLOCKS, LRU_BLOCK_DIM)
    r = jax.nn.sigmoid((jnp.einsum('bsnd,nde->bsne', xr, w_a).reshape(B, S, W) + b_a).astype(jnp.float32))
    ig = jax.nn.sigmoid((jnp.einsum('bsnd,nde->bsne', xr, w_x).reshape(B, S, W) + b_x).astype(jnp.float32))
    log_a = -LRU_C * r * jax.nn.softplus(-lam.astype(jnp.float32))
    a = jnp.exp(log_a)
    bterm = jnp.sqrt(-jnp.expm1(2.0 * log_a)) * (ig * xc.astype(jnp.float32))

    def combine(left, right):
        a1, b1 = left
        a2, b2 = right
        return a1 * a2, a2 * b1 + b2

    _, h = lax.associative_scan(combine, (a, bterm), axis=1)
    return (h * jax.nn.gelu(gb.astype(jnp.float32))).astype(xb.dtype)

def moba_attention(q, k, v, bias_tab):
    B, S, H, E = q.shape
    f32 = jnp.float32
    nblk = -(-S // MOBA_BLOCK)
    Sp = nblk * MOBA_BLOCK
    pad = ((0, 0), (0, 0), (0, Sp - S), (0, 0))
    qh = q.transpose(0, 2, 1, 3)
    qb = jnp.pad(qh, pad).reshape(B, H, nblk, MOBA_BLOCK, E)
    kb = jnp.pad(k.transpose(0, 2, 1, 3), pad).reshape(B, H, nblk, MOBA_BLOCK, E)
    vb = jnp.pad(v.transpose(0, 2, 1, 3), pad).reshape(B, H, nblk, MOBA_BLOCK, E)
    tab = bias_tab.astype(f32)
    off = jnp.arange(MOBA_BLOCK)
    delta = off[:, None] - off[None, :]
    bias_own = jnp.transpose(tab[rel_bucket(delta)], (2, 0, 1))
    lg = jnp.einsum('bhnqe,bhnke->bhnqk', qb, kb).astype(f32) * SCALE + bias_own[None, :, None]
    lg = jnp.where(delta >= 0, lg, NEG_INF_2)
    m_own = jnp.max(lg, axis=-1)
    p = jnp.exp(lg - m_own[..., None])
    den_own = jnp.sum(p, axis=-1).reshape(B, H, Sp)[:, :, :S]
    num_own = jnp.einsum('bhnqk,bhnke->bhnqe', p, vb.astype(f32)).reshape(B, H, Sp, E)[:, :, :S]
    m_own = m_own.reshape(B, H, Sp)[:, :, :S]
    n_sel = min(MOBA_TOPK, nblk - 1)
    if n_sel == 0:
        out = num_own / den_own[..., None]
    else:
        kmean = jnp.mean(kb.astype(f32), axis=3)
        qpos = jnp.arange(S)
        qblk = qpos // MOBA_BLOCK
        gate = jnp.einsum('bhse,bhne->bhsn', qh.astype(f32), kmean)
        gate = jnp.where(jnp.arange(nblk)[None, :] < qblk[:, None], gate, NEG_INF_2)
        _, idx = lax.top_k(gate, n_sel)
        base = (jnp.arange(B)[:, None] * H + jnp.arange(H)[None, :]) * nblk
        fidx = idx + base[:, :, None, None]
        kflat = kb.reshape(B * H * nblk, MOBA_BLOCK, E)
        vflat = vb.reshape(B * H * nblk, MOBA_BLOCK, E)
        head = jnp.arange(H)[None, :, None, None, None]
        tab_t = tab.T
        nq = S // MOBA_Q_CHUNK

        def chunks(t):
            return jnp.moveaxis(t.reshape(B, H, nq, MOBA_Q_CHUNK, *t.shape[3:]), 2, 0)

        def step(args):
            qc, fi, bi, qp, m_o, d_o, n_o = args
            ks = jnp.take(kflat, fi, axis=0)
            vs = jnp.take(vflat, fi, axis=0)
            lgs = jnp.einsum('bhqe,bhqnke->bhqnk', qc, ks).astype(f32) * SCALE
            kpos = bi[..., None] * MOBA_BLOCK + jnp.arange(MOBA_BLOCK)
            lgs = lgs + tab_t[head, rel_bucket(qp[:, None, None] - kpos)]
            ok = bi < (qp // MOBA_BLOCK)[:, None]
            lgs = jnp.where(ok[..., None], lgs, NEG_INF_2)
            mm = jnp.maximum(jnp.max(lgs, axis=(-2, -1)), m_o)
            ps = jnp.exp(lgs - mm[..., None, None])
            c_o = jnp.exp(m_o - mm)
            den = d_o * c_o + jnp.sum(ps, axis=(-2, -1))
            num = n_o * c_o[..., None] + jnp.einsum('bhqnk,bhqnke->bhqe', ps, vs.astype(f32))
            return num / den[..., None]

        out = lax.map(step, (chunks(qh), chunks(fidx), chunks(idx), qpos.reshape(nq, MOBA_Q_CHUNK),
                             chunks(m_own), chunks(den_own), chunks(num_own)))
        out = jnp.moveaxis(out, 0, 2).reshape(B, H, S, E)
    return out.transpose(0, 2, 1, 3)

def hybrid_layer(x, rel_bias, g_mix, w_in, conv_w, conv_b, lru_wa, lru_ba, lru_wx, lru_bx, lru_lam,
                 p_a, p_b, p_c, w_out, g_ffn, w_gu, w_down):
    B, S, D = x.shape
    h = rms_norm_2(x, g_mix)
    z = h @ w_in
    offs = np.cumsum(IN_SIZES)[:-1].tolist()
    qa, ka, va, xb, gb, qc, kc, vc, gates = jnp.split(z, offs, axis=-1)
    qa = qa.reshape(B, S, A_HEADS, HEAD_DIM)
    ka = ka.reshape(B, S, A_HEADS, HEAD_DIM)
    va = va.reshape(B, S, A_HEADS, HEAD_DIM)
    outs, lses = [], []
    for g, (window, dilation) in enumerate(A_GROUPS):
        sl = slice(g * A_HEADS_PER_GROUP, (g + 1) * A_HEADS_PER_GROUP)
        o, lse = dilated_window_attention(qa[:, :, sl], ka[:, :, sl], va[:, :, sl],
                                          dilation, window // dilation, rel_bias[:, sl])
        outs.append(o)
        lses.append(lse)
    wts = jax.nn.softmax(jnp.stack(lses, axis=0), axis=0)
    o_a = jnp.sum(wts[..., None] * jnp.stack(outs, axis=0), axis=0).reshape(B, S, A_OUT).astype(x.dtype)
    o_b = rg_lru_branch(xb, gb, conv_w, conv_b, lru_wa, lru_ba, lru_wx, lru_bx, lru_lam)
    o_c = moba_attention(qc.reshape(B, S, C_HEADS, HEAD_DIM), kc.reshape(B, S, C_HEADS, HEAD_DIM),
                         vc.reshape(B, S, C_HEADS, HEAD_DIM), rel_bias[:, A_HEADS:])
    o_c = o_c.reshape(B, S, C_WIDTH).astype(x.dtype)
    gt = jax.nn.sigmoid(gates.astype(jnp.float32)).astype(x.dtype).reshape(B, S, 3, D)
    merged = gt[:, :, 0] * (o_a @ p_a) + gt[:, :, 1] * (o_b @ p_b) + gt[:, :, 2] * (o_c @ p_c)
    x = x + merged @ w_out
    u = rms_norm_2(x, g_ffn) @ w_gu
    gate, up = jnp.split(u, 2, axis=-1)
    return x + (jax.nn.silu(gate) * up) @ w_down

def second_inputs(seed: int = 0) -> dict:
    key = jax.random.key(seed)
    ks = jax.random.split(key, 24)
    f32 = jnp.float32

    def nrm(k, shape, scale):
        return jax.random.normal(k, shape, f32) * scale

    u = jax.random.uniform(ks[11], (DEPTH_2, LRU_WIDTH), f32, 0.9, 0.999)
    a = u ** (1.0 / LRU_C)
    return {
        "x": nrm(ks[0], (BATCH, SEQ, D_MODEL), 1.0),
        "rel_bias": nrm(ks[1], (REL_BUCKETS, REL_HEADS), 0.5),
        "g_mix": 1.0 + nrm(ks[2], (DEPTH_2, D_MODEL), 0.05),
        "w_in": nrm(ks[3], (DEPTH_2, D_MODEL, IN_COLS), D_MODEL ** -0.5),
        "conv_w": nrm(ks[4], (DEPTH_2, CONV_WIDTH, LRU_WIDTH), CONV_WIDTH ** -0.5),
        "conv_b": nrm(ks[5], (DEPTH_2, LRU_WIDTH), 0.02),
        "lru_wa": nrm(ks[6], (DEPTH_2, LRU_BLOCKS, LRU_BLOCK_DIM, LRU_BLOCK_DIM), LRU_BLOCK_DIM ** -0.5),
        "lru_ba": nrm(ks[7], (DEPTH_2, LRU_WIDTH), 0.02),
        "lru_wx": nrm(ks[8], (DEPTH_2, LRU_BLOCKS, LRU_BLOCK_DIM, LRU_BLOCK_DIM), LRU_BLOCK_DIM ** -0.5),
        "lru_bx": nrm(ks[9], (DEPTH_2, LRU_WIDTH), 0.02),
        "lru_lam": jnp.log(a) - jnp.log1p(-a),
        "p_a": nrm(ks[12], (DEPTH_2, A_OUT, D_MODEL), A_OUT ** -0.5),
        "p_b": nrm(ks[13], (DEPTH_2, LRU_WIDTH, D_MODEL), LRU_WIDTH ** -0.5),
        "p_c": nrm(ks[14], (DEPTH_2, C_WIDTH, D_MODEL), C_WIDTH ** -0.5),
        "w_out": nrm(ks[15], (DEPTH_2, D_MODEL, D_MODEL), D_MODEL ** -0.5),
        "g_ffn": 1.0 + nrm(ks[16], (DEPTH_2, D_MODEL), 0.05),
        "w_gu": nrm(ks[17], (DEPTH_2, D_MODEL, 2 * FFN_HIDDEN), D_MODEL ** -0.5),
        "w_down": nrm(ks[18], (DEPTH_2, FFN_HIDDEN, D_MODEL), FFN_HIDDEN ** -0.5),
        "g_final": 1.0 + nrm(ks[19], (D_MODEL,), 0.05),
    }

def second_block(x, rel_bias, g_mix, w_in, conv_w, conv_b, lru_wa, lru_ba, lru_wx, lru_bx, lru_lam,
              p_a, p_b, p_c, w_out, g_ffn, w_gu, w_down, g_final):
    for l in range(DEPTH_2):
        x = hybrid_layer(x, rel_bias, g_mix[l], w_in[l], conv_w[l], conv_b[l], lru_wa[l], lru_ba[l],
                         lru_wx[l], lru_bx[l], lru_lam[l], p_a[l], p_b[l], p_c[l], w_out[l],
                         g_ffn[l], w_gu[l], w_down[l])
    return rms_norm_2(x, g_final)


def setup_inputs(seed=0):
    out = dict(first_inputs(seed))
    for name, value in second_inputs(seed + 1).items():
        if name != "x":
            out[name + "_2"] = value
    return out


def reference(
    x, c, ctx, c_ctx, ada_w, ada_b, ln_g, ln_b, ffn_w13, ffn_w2, ret_w_in, ret_decay, ret_w_out,
    na_w_qkv, na_rpb, na_w_out, mla_w_down, mla_q_norm, mla_kv_norm, mla_w_uq, mla_w_ukv,
    mla_w_out, hg_w_in, hg_lower_bounds, hg_norm_g, hg_w_out, rel_bias_2, g_mix_2, w_in_2,
    conv_w_2, conv_b_2, lru_wa_2, lru_ba_2, lru_wx_2, lru_bx_2, lru_lam_2, p_a_2, p_b_2, p_c_2,
    w_out_2, g_ffn_2, w_gu_2, w_down_2, g_final_2,
):
    x = first_block(
        x, c, ctx, c_ctx, ada_w, ada_b, ln_g, ln_b, ffn_w13, ffn_w2, ret_w_in, ret_decay,
        ret_w_out, na_w_qkv, na_rpb, na_w_out, mla_w_down, mla_q_norm, mla_kv_norm, mla_w_uq,
        mla_w_ukv, mla_w_out, hg_w_in, hg_lower_bounds, hg_norm_g, hg_w_out,
    )
    return second_block(
        x, rel_bias_2, g_mix_2, w_in_2, conv_w_2, conv_b_2, lru_wa_2, lru_ba_2, lru_wx_2,
        lru_bx_2, lru_lam_2, p_a_2, p_b_2, p_c_2, w_out_2, g_ffn_2, w_gu_2, w_down_2, g_final_2,
    )


_drawn_inputs = setup_inputs


def setup_inputs(seed=0):
    import zlib

    import numpy as np

    out = dict(_drawn_inputs(seed))
    spreads = {}
    factors = {'ada_b': 4.115, 'na_rpb': 64.0, 'lru_ba_2': 46.386, 'lru_bx_2': 23.389}
    for name, (base, spread) in spreads.items():
        noise = np.random.default_rng([zlib.crc32(name.encode()), seed]).standard_normal(out[name].shape)
        drawn = base * np.exp(spread * noise) if base else spread * noise
        out[name] = jnp.asarray(drawn.astype(out[name].dtype))
    for name, factor in factors.items():
        out[name] = (out[name] * factor).astype(out[name].dtype)
    return out
```

```python
from collections import deque
from contextlib import ExitStack

import numpy as np
import concourse.bass as bass
from concourse import mybir
from concourse.alu_op_type import AluOpType as ALU

F32 = mybir.dt.float32
F32R = mybir.dt.float32r
ACT = mybir.ActivationFunctionType
AX = mybir.AxisListType.X

P = 128
D = 1024
KD = D // P
NCTX, NLAT = 256, 512
NTOK = NCTX + NLAT
CTX, LAT = 0, 1
TOKENS = {CTX: NCTX, LAT: NLAT}
START = {CTX: 0, LAT: NCTX}
BOTH, ONLY_LAT = (CTX, LAT), (LAT,)
FF = -(-8 * D // (3 * 256)) * 256
KF = FF // P
KMAX = 8
FF_CHUNKS = [(a, min(KMAX, KF - a)) for a in range(0, KF, KMAX)]
ALPHA = 4 ** 0.25
LN_EPS, RMS_EPS = 1e-5, 1e-6
NEG = -1e30
GRID = 64
ROWS = NLAT // GRID
RET_HEADS, RET_DK, RET_DV = 4, 256, 512
NA_HEADS, HEAD = 16, 64
QB, BAND, WIN = 16, 32, 16
BAND0 = [int(v) for v in np.clip(np.arange(GRID // QB) * QB - WIN // 2, 0, GRID - BAND)]
RPB_ROWS, RPB_COLS, RPB_WIDE = 15, 31, 64
REL = QB + BAND
GROUP_HEADS, DIL_GROUPS, MOBA_HEADS = 4, 3, 8
LRU_TILES = 4

VECS = {}


def _vec(name, n):
    VECS[name] = (sum(k for _, k in VECS.values()), n)


for _name, _n in (("ada_b", 2 * 48), ("ln_g", 4 * KD), ("ln_b", 4 * KD), ("g_mix", KD), ("g_ffn", KD),
                  ("g_final", KD), ("conv_w", 4 * LRU_TILES), ("conv_b", LRU_TILES), ("lru_ba", LRU_TILES),
                  ("lru_bx", LRU_TILES), ("lru_lam", LRU_TILES), ("cond", 2 * KD), ("decay", 8)):
    _vec(_name, _n)
NVEC = sum(k for _, k in VECS.values())


class Queue:

    def __init__(self, engine, sem):
        self.engine, self.sem, self.count, self.met = engine, sem, 0, {}

    def wait(self, tokens):
        for t in tokens:
            if t is None:
                continue
            if isinstance(t, list):
                self.wait(t)
                continue
            sem, value = t
            if self.met.get(id(sem), 0) < value:
                self.met[id(sem)] = value
                self.engine.wait_ge(sem, value)

    def put(self, build, *after):
        self.wait(after)
        self.count += 1
        build().then_inc(self.sem, 1)
        return self.sem, self.count

    def quiet(self, build, *after):
        self.wait(after)
        build()

    def dma(self, out, in_, slot, *after):
        self.wait(after)
        slot[1] += 16
        self.engine.dma_start(out, in_).then_inc(slot[0], 16)
        return slot[0], slot[1]


class Ring:

    def __init__(self, slots):
        self.slots, self.free, self.at = slots, [[] for _ in slots], 0

    def take(self):
        i = self.at % len(self.slots)
        assert self.free[i] is not None, "slot still in use"
        after, self.free[i] = self.free[i], None
        self.at += 1
        return i, self.slots[i], after

    def give(self, i, *tokens):
        self.free[i] = list(tokens)


def weight_plan(w):
    plan = []

    def add(name, *index):
        block = w[name]
        for i in index:
            block = block[i]
        plan.append((block, block.shape[-1] // P))

    def ffn(name13, name2):
        for c, (f0, n) in enumerate(FF_CHUNKS):
            for f in range(f0, f0 + n):
                add(name13, f)
                add(name13, KF + f)
            for o in range(KD):
                add(f"{name2}_{c}", o)

    def ret_out(h):
        for o in range(KD):
            add("ret_out", h, o)

    for h in range(RET_HEADS):
        for b in (2 * h, 2 * h + 1, 8 + 2 * h, 9 + 2 * h):
            add("ret_in", b)
        if h:
            ret_out(h - 1)
        for b in range(4):
            add("ret_in", 16 + 4 * h + b)
        for b in range(4):
            add("ret_in", 32 + 4 * h + b)
    ret_out(RET_HEADS - 1)
    ffn("w13_0", "w2_0")
    for pair in range(NA_HEADS // 2):
        for b in (pair, KD + pair, 2 * KD + pair):
            add("na_qkv", b)
    for o in range(KD):
        add("na_out", o)
    ffn("w13_1", "w2_1")
    for jp in range(2):
        for part in range(3):
            for g in range(DIL_GROUPS):
                add("in_2", 6 * part + 2 * g + jp)
        if jp == 0:
            for t in range(LRU_TILES):
                add("in_2", 18 + t)
                add("in_2", 22 + t)
    for pair in range(MOBA_HEADS // 2):
        for part in range(3):
            add("in_2", 26 + 4 * part + pair)
    for o in range(KD):
        for branch, name in enumerate(("p_a", "p_b", "p_c")):
            add("in_2", 38 + KD * branch + o)
            add(name, o)
    for o in range(KD):
        add("out_2", o)
    ffn("w13_2", "w2_2")
    return plan


def program(nc, a, w, out):
    stack = ExitStack()
    sems = []

    def sem(name):
        s = stack.enter_context(nc.semaphore(name))
        sems.append(s)
        return s

    def dma_slot(name):
        return [sem(name), 0]

    pe, act, dve, pool, sp = (Queue(engine, sem(f"done_{name}")) for name, engine in (
        ("pe", nc.tensor), ("act", nc.scalar), ("dve", nc.vector), ("pool", nc.gpsimd), ("sp", nc.sync)))
    V, S, G, T = nc.vector, nc.scalar, nc.gpsimd, nc.tensor

    class Map:
        def __init__(self, start, end):
            self.at, self.end = start, end

        def sb(self, name, shape, dt=F32):
            size = int(np.prod(shape[1:])) * 4
            at = (self.at + 31) // 32 * 32
            assert at + size <= self.end, f"{name}: {at + size} > {self.end}"
            self.at = at + size
            return nc.alloc_sbuf_tensor_at(name, list(shape), dt, offset=at)

    keep = Map((nc.sbuf_base + 31) // 32 * 32, nc.sbuf_usable_end)
    h_lat = keep.sb("h_lat", [P, KD, NLAT])
    x_lat = [keep.sb(f"x_lat_{s}", [P, KD, NLAT], F32R) for s in ("hi", "lo")]
    ctx_start = keep.at
    h_ctx = keep.sb("h_ctx", [P, KD, NCTX])
    x_ctx = [keep.sb(f"x_ctx_{s}", [P, KD, NCTX], F32R) for s in ("hi", "lo")]
    ctx_end = keep.at
    NRAW, NSPLIT, AHEAD = 3, 3, 2
    w_raw = keep.sb("w_raw", [P, NRAW, KMAX * P])
    w_hi = keep.sb("w_hi", [P, NSPLIT, KMAX * P], F32R)
    w_lo = keep.sb("w_lo", [P, NSPLIT, KMAX * P], F32R)
    tmp = keep.sb("tmp", [P, 2, NTOK])
    ident = keep.sb("ident", [P, P])
    ones = keep.sb("ones", [P, P])
    vec = keep.sb("vec", [P, NVEC])
    cond = keep.sb("cond", [P, 2 * KD])
    mod = [keep.sb(f"mod_{l}", [P, 48, 2]) for l in range(2)]
    log_gamma = keep.sb("log_gamma", [P, 8])
    small = keep.sb("small", [P, 96])
    PHASE = keep.at
    END = nc.sbuf_usable_end // 32 * 32

    banks = [stack.enter_context(nc.psum_tensor(f"bank{i}", [P, 512], F32)) for i in range(8)]
    lin = Ring(banks[0:4])
    att = Ring(banks[4:7])
    last = Ring(banks[7:8])

    def vc(name, i=0, n=1):
        c = VECS[name][0] + i
        return vec[:, c:c + n]

    def fence():
        return [(q.sem, q.count) for q in (pe, act, dve, pool) if q.count]

    const_sem = dma_slot("loaded_constants")
    for dst, src in ((vec[:, :], a["vec"]), (ident[:, :], a["ident"])):
        consts = sp.dma(dst, src, const_sem)
    x_sem = dma_slot("loaded_x")
    for dst, src in ((h_ctx, a["ctx"]), (h_lat, a["x"])):
        x_loaded = sp.dma(dst[:, :, :], src, x_sem)
    ones_set = pool.put(lambda: G.memset(ones[:, :], 1.0))

    plan = weight_plan(w)
    raw_sem = [dma_slot(f"loaded_w{i}") for i in range(NRAW)]
    raw_free = [[] for _ in range(NRAW)]
    raw_token, split_token, split_free = {}, {}, [[] for _ in range(NSPLIT)]
    state = {"fetched": 0, "split": 0, "taken": 0}

    def fetch(i):
        slot = i % NRAW
        block, kt = plan[i]
        raw_token[i] = sp.dma(w_raw[:, slot, 0:kt * P], block, raw_sem[slot], raw_free[slot])

    def split_weights(i):
        raw, to = i % NRAW, i % NSPLIT
        n = plan[i][1] * P
        src, hi, lo = w_raw[:, raw, 0:n], w_hi[:, to, 0:n], w_lo[:, to, 0:n]
        t_hi = act.put(lambda: S.activation(hi, src, ACT.Copy), raw_token[i], split_free[to])
        t_lo = dve.put(lambda: V.tensor_tensor(lo, src, hi.bitcast(F32), ALU.subtract), t_hi, split_free[to])
        raw_free[raw] = [t_lo]
        split_token[i] = t_lo

    def take_weights(kt):
        i = state["taken"]
        state["taken"] += 1
        assert plan[i][1] == kt, (i, plan[i][1], kt)
        while state["split"] <= min(i + AHEAD, len(plan) - 1):
            if state["fetched"] <= state["split"]:
                fetch(state["fetched"])
                state["fetched"] += 1
            split_weights(state["split"])
            state["split"] += 1
            if state["fetched"] < min(state["split"] + NRAW, len(plan)) :
                fetch(state["fetched"])
                state["fetched"] += 1
        while state["fetched"] < min(state["split"] + NRAW, len(plan)):
            fetch(state["fetched"])
            state["fetched"] += 1
        return i

    background = deque()
    trickle = deque()

    def advance(works):
        while works:
            try:
                next(works[0])
                return
            except StopIteration:
                works.popleft()

    def tick(n=1):
        for _ in range(n):
            advance(background)
        advance(trickle)

    def drain():
        while background:
            advance(background)

    def drain_trickle():
        while trickle:
            advance(trickle)

    class Split:

        def __init__(self, parts):
            self.parts, self.ready, self.read = parts, {}, []

        def ap(self, part, k, g):
            return self.parts[g][part][:, k, :]

    def linear(x, kt, groups, ticks=1):
        i = take_weights(kt)
        slot = i % NSPLIT
        taken = [lin.take() for _ in groups]
        outs = [bank[:, 0:TOKENS[g]] for (_, bank, _), g in zip(taken, groups)]
        pe.wait([after for _, _, after in taken] + [split_token[i]])
        done = 0
        for k in range(kt):
            hi, lo = (t[:, slot, k * P:(k + 1) * P] for t in (w_hi, w_lo))
            for n, (weights, part) in enumerate(((hi, 0), (hi, 1), (lo, 0))):
                for o, g in zip(outs, groups):
                    end = k == kt - 1 and n == 2
                    call = (lambda o=o, wt=weights, m=x.ap(part, k, g), s=(k == 0 and n == 0), e=end:
                            T.matmul(o, wt, m, start=s, stop=e))
                    if end:
                        token = pe.put(call, x.ready[k, g])
                    else:
                        pe.quiet(call, x.ready[k, g])
            while done < ticks * (k + 1) // kt and k < kt - 1:
                advance(background)
                done += 1
        split_free[slot] = [token]
        x.read = [token]
        tick(ticks - done)
        return [(idx, o, token) for (idx, _, _), o in zip(taken, outs)]

    tmp_ring = Ring([tmp[:, i, :] for i in range(2)])

    def put_split(x, k, g, src, ready, cols=slice(None), view=None, src_view=None):
        hi, lo = x.ap(0, k, g), x.ap(1, k, g)
        if view is not None:
            hi, lo = view(hi), view(lo)
        t_hi = act.put(lambda: S.activation(hi, src, ACT.Copy), ready, x.read)
        t_lo = dve.put(lambda: V.tensor_tensor(lo, src, hi.bitcast(F32), ALU.subtract), t_hi, x.read)
        x.ready.setdefault((k, g), [])
        x.ready[k, g] = x.ready[k, g] + [t_lo]
        return [t_hi, t_lo]

    def rstd_rows(sq, n, ready, mean_of, eps, diag):
        nt = n // P
        i, bank, after = att.take()
        for c in range(nt):
            t = pe.put(lambda c=c: T.matmul(bank[:, c:c + 1], sq[:, c * P:(c + 1) * P], ones[:, 0:1],
                                            start=True, stop=True), after, ready, ones_set)
        v, r = small[:, 0:nt], small[:, 8:8 + nt]
        t1 = dve.put(lambda: V.tensor_scalar(v, bank[:, 0:nt], 1.0 / mean_of, eps, ALU.mult, ALU.add), t, state.get("small"))
        att.give(i, t1)
        t2 = dve.put(lambda: V.reciprocal(v, v), t1)
        t3 = act.put(lambda: S.activation(r, v, ACT.Sqrt), t2)
        state["small"] = [t3]
        for c in range(nt):
            t4 = dve.put(lambda c=c: V.tensor_scalar(diag[:, c * P:(c + 1) * P], ident[:, :], r[:, c:c + 1],
                                                     None, ALU.mult), t3, t)
        j, rows, after = att.take()
        t5 = pe.put(lambda: T.matmul(rows[:, 0:n], ones[:, :], diag[:, 0:n], start=True, stop=True), t4, after)
        state["small"] = [t3, t4]
        return j, rows[:, 0:n], t5

    silu_cond = act.put(lambda: S.activation(cond[:, :], vc("cond", 0, 2 * KD), ACT.Silu), consts)
    ada_map = Map(END - 2 * KMAX * P * 4, END)
    ada_raw = ada_map.sb("ada_raw", [P, 2, KMAX * P])
    ada_end = END - 2 * KMAX * P * 4
    ada_sem = [dma_slot(f"loaded_ada{i}") for i in range(2)]
    ada_ring = Ring([0, 1])
    mod_ready = {}

    def ada_chunks(layer, chunks):
        bank_i, bank, after = last.take()
        done = []
        for c in chunks:
            for b in range(8 * c, 8 * c + 8):
                slot, _, free = ada_ring.take()
                loaded = pool.dma(ada_raw[:, slot, :], w[f"ada_{layer}"][b], ada_sem[slot], free)
                for k in range(KD):
                    call = (lambda k=k, b=b, slot=slot: T.matmul(
                        bank[:, 2 * b:2 * b + 2], ada_raw[:, slot, k * P:(k + 1) * P], cond[:, 2 * k:2 * k + 2],
                        start=k == 0, stop=k == KD - 1))
                    t = pe.put(call, loaded, silu_cond, after)
                ada_ring.give(slot, t)
                yield
            cols = slice(8 * c, 8 * c + 8)
            bias = vc("ada_b", 48 * layer + 8 * c, 8).unsqueeze(2).to_broadcast([P, 8, 2])
            src = bank[:, 16 * c:16 * c + 16].rearrange("p (b g) -> p b g", g=2)
            done = dve.put(lambda cols=cols, src=src, bias=bias: V.tensor_tensor(mod[layer][:, cols, :], src, bias, ALU.add), t, consts)
            if c in (1, 4):
                done = dve.put(lambda cols=cols: V.tensor_scalar(mod[layer][:, cols, :], mod[layer][:, cols, :],
                                                                 1.0, None, ALU.add), done)
            mod_ready[layer, c] = done
            after = done
        last.give(bank_i, done)

    def mod_col(layer, c, k, g):
        j = 0 if g == LAT else 1
        return mod[layer][:, 8 * c + k, j:j + 1]

    H = {CTX: h_ctx, LAT: h_lat}
    X = Split({CTX: x_ctx, LAT: x_lat})
    h_ready = {(k, g): [x_loaded] for k in range(KD) for g in BOTH}
    h_used = {(k, g): [] for k in range(KD) for g in BOTH}

    def modulate(layer, c, groups, scale_h=True):
        for g in groups:
            for k in range(KD):
                ti, t_ap, after = tmp_ring.take()
                n = TOKENS[g]
                t = dve.put(lambda t_ap=t_ap, n=n, g=g, k=k: V.tensor_scalar(
                    t_ap[:, 0:n], H[g][:, k, :], mod_col(layer, c + 1, k, g), mod_col(layer, c, k, g),
                    ALU.mult, ALU.add), after, h_ready[k, g], mod_ready[layer, c], mod_ready[layer, c + 1])
                X.ready[k, g] = []
                tmp_ring.give(ti, *put_split(X, k, g, t_ap[:, 0:n], t))
                if scale_h:
                    h_ready[k, g] = [pool.put(lambda g=g, k=k: G.tensor_scalar(
                        H[g][:, k, :], H[g][:, k, :], ALPHA, 1.0, ALU.mult, ALU.mult), t, h_ready[k, g])]

    def add_gated(layer, c, o, groups, outs):
        for (i, bank, t), g in zip(outs, groups):
            t2 = dve.put(lambda bank=bank, g=g: V.scalar_tensor_tensor(
                H[g][:, o, :], bank, mod_col(layer, c, o, g), H[g][:, o, :], ALU.mult, ALU.add),
                t, h_ready[o, g], mod_ready[layer, c])
            h_ready[o, g] = [t2]
            lin.give(i, t2)

    sums = {}

    def layer_norm(which, groups, scr, after_fence):
        total, sq = scr
        for g in groups:
            n = TOKENS[g]
            tot, sqs = total[g], sq[g]
            t = dve.put(lambda g=g, tot=tot: V.tensor_tensor(tot, H[g][:, 0, :], H[g][:, 1, :], ALU.add),
                        h_ready[0, g], h_ready[1, g], after_fence)
            for k in range(2, KD):
                t = dve.put(lambda g=g, tot=tot, k=k: V.tensor_tensor(tot, tot, H[g][:, k, :], ALU.add), t, h_ready[k, g])
            i, bank, free = att.take()
            t = pe.put(lambda bank=bank, n=n, tot=tot: T.matmul(bank[:, 0:n], ones[:, :], tot, start=True, stop=True), t, free, ones_set)
            t_mean = act.put(lambda bank=bank, n=n, tot=tot: S.activation(tot, bank[:, 0:n], ACT.Copy, scale=1.0 / D), t)
            att.give(i, t_mean)
            acc = None
            for k in range(KD):
                t = dve.put(lambda g=g, k=k, tot=tot: V.tensor_tensor(H[g][:, k, :], H[g][:, k, :], tot, ALU.subtract), t_mean, h_ready[k, g])
                h_ready[k, g] = [t]
                if k == 0:
                    acc = act.put(lambda g=g, sqs=sqs: S.activation(sqs, H[g][:, 0, :], ACT.Square), t, after_fence)
                else:
                    ti, t_ap, free = tmp_ring.take()
                    t = act.put(lambda g=g, k=k, t_ap=t_ap, n=n: S.activation(t_ap[:, 0:n], H[g][:, k, :], ACT.Square), t, free)
                    acc = pool.put(lambda sqs=sqs, t_ap=t_ap, n=n: G.tensor_tensor(sqs, sqs, t_ap[:, 0:n], ALU.add), t, acc)
                    tmp_ring.give(ti, acc)
            i, rows, t = rstd_rows(sqs, n, acc, D, LN_EPS, sqs)
            for k in range(KD):
                t1 = dve.put(lambda g=g, k=k, rows=rows: V.tensor_tensor(H[g][:, k, :], H[g][:, k, :], rows, ALU.mult), t, h_ready[k, g])
                t2 = act.put(lambda g=g, k=k: S.activation(H[g][:, k, :], H[g][:, k, :], ACT.Identity,
                                                           bias=vc("ln_b", which * KD + k), scale=vc("ln_g", which * KD + k)), t1)
                h_ready[k, g] = [t2]
            att.give(i, t1)

    def rms_scale(g, rows_of, scr_sq, gain, after_fence, finish):
        sqs = scr_sq
        acc = None
        for k in range(KD):
            if k == 0:
                acc = act.put(lambda: S.activation(sqs, H[g][:, 0, :], ACT.Square), h_ready[0, g], after_fence)
            else:
                ti, t_ap, free = tmp_ring.take()
                t = act.put(lambda k=k, t_ap=t_ap: S.activation(t_ap[:, 0:NLAT], H[g][:, k, :], ACT.Square), h_ready[k, g], free)
                acc = pool.put(lambda t_ap=t_ap: G.tensor_tensor(sqs, sqs, t_ap[:, 0:NLAT], ALU.add), t, acc)
                tmp_ring.give(ti, acc)
        i, rows, t = rstd_rows(sqs, NLAT, acc, D, RMS_EPS, sqs)
        for k in range(KD):
            ti, t_ap, free = tmp_ring.take()
            t1 = dve.put(lambda k=k, t_ap=t_ap: V.scalar_tensor_tensor(
                t_ap[:, 0:NLAT], H[g][:, k, :], vc(gain, k), rows, ALU.mult, ALU.mult), t, free, h_ready[k, g])
            tmp_ring.give(ti, *finish(k, t_ap[:, 0:NLAT], t1))
        att.give(i, t1)

    def ffn(name, groups, prev, start, gated):
        m = Map(start, ada_end)
        hid = Split({g: [m.sb(f"{name}_hid{g}{s}", [P, KMAX, TOKENS[g]], F32R) for s in ("hi", "lo")] for g in groups})
        silu = Ring([m.sb(f"{name}_silu{i}", [P, NTOK]) for i in range(2)])
        hid.read = prev
        silu.free = [prev, prev]
        scr = ({g: m.sb(f"{name}_tot{g}", [P, TOKENS[g]])[:, :] for g in groups},
               {g: m.sb(f"{name}_sq{g}", [P, TOKENS[g]])[:, :] for g in groups})
        for f0, nf in FF_CHUNKS:
            for j in range(nf):
                si, s_ap, free = silu.take()
                t_silu = {}
                for (i, bank, t), g in zip(linear(X, KD, groups), groups):
                    cols = slice(START[g], START[g] + TOKENS[g])
                    t_silu[g] = act.put(lambda bank=bank, cols=cols, s_ap=s_ap: S.activation(s_ap[:, cols], bank, ACT.Silu), t, free)
                    lin.give(i, t_silu[g])
                ended = []
                for (i, bank, t), g in zip(linear(X, KD, groups), groups):
                    cols = slice(START[g], START[g] + TOKENS[g])
                    t2 = dve.put(lambda bank=bank, cols=cols, s_ap=s_ap: V.tensor_tensor(s_ap[:, cols], bank, s_ap[:, cols], ALU.mult), t, t_silu[g])
                    lin.give(i, t2)
                    hid.ready[j, g] = []
                    ended += put_split(hid, j, g, s_ap[:, cols], t2)
                silu.give(si, *ended)
            for o in range(KD):
                gated(o, linear(hid, nf, groups))
        return scr

    trickle.append(ada_chunks(0, (0, 1)))
    drain_trickle()
    modulate(0, 0, BOTH)
    trickle.append(ada_chunks(0, (2, 3, 4, 5)))

    m = Map(PHASE, ada_end)
    ret_q = m.sb("ret_q", [P, 2, NTOK])
    ret_k = m.sb("ret_k", [P, 2, NTOK])
    ret_vt = m.sb("ret_vt", [P, NTOK])
    ret_v = m.sb("ret_v", [P, NTOK // P, RET_DV])
    y_hi = {g: m.sb(f"ret_y_hi{g}", [P, 4, TOKENS[g]], F32R) for g in BOTH}
    y_at = m.at
    y_lo = {g: m.sb(f"ret_y_lo{g}", [P, 4, TOKENS[g]], F32R) for g in BOTH}
    over = Map(y_at, m.at)
    gate = {g: over.sb(f"ret_gate{g}", [P, 4, TOKENS[g]]) for g in BOTH}
    scores = m.sb("ret_scores", [P, NTOK // P, NLAT])
    scores_ctx = m.sb("ret_scores_ctx", [P, NCTX // P, NCTX])
    WIDE = NLAT + 3 * P
    near = m.sb("ret_near", [P, WIDE])
    far = m.sb("ret_far", [P, NLAT + P])
    rope = [m.sb(f"ret_{n}", [P, NLAT]) for n in ("cos", "sin")]
    ret_sq = m.sb("ret_sq", [P, NLAT])
    ret_u = m.sb("ret_u", [P, NLAT])
    rope_sem = dma_slot("loaded_rope")
    for dst, src in zip(rope, (a["cos"], a["sin"])):
        rope_loaded = sp.dma(dst[:, :], src, rope_sem)
    dist_sem = dma_slot("loaded_dist")

    t = act.put(lambda: S.activation(log_gamma[:, :], vc("decay", 0, 8), ACT.Exp), consts)
    lg_ready = dve.put(lambda: V.tensor_scalar(log_gamma[:, :], log_gamma[:, :], -1.0, None, ALU.mult), t)
    neg_lg, far_bias = small[:, 32:40], small[:, 40:48]
    t = dve.put(lambda: V.tensor_scalar(neg_lg, log_gamma[:, :], -1.0, None, ALU.mult), lg_ready)
    t = dve.put(lambda: V.tensor_scalar(far_bias[:, 0:4], log_gamma[:, 0:4], 512.0, None, ALU.mult), lg_ready)
    lg_ready = dve.put(lambda: V.tensor_scalar(far_bias[:, 4:8], log_gamma[:, 4:8], 256.0, None, ALU.mult), lg_ready)

    near_ready, near_used = [None], [None]

    def decay_tables(h):
        i0, a0, free0 = tmp_ring.take()
        done = []
        dist = w["dist"]
        tmp_ring.give(i0, *free0) if free0 else tmp_ring.give(i0)
        half = WIDE // 2
        for c0 in (0, half):
            i0, d_ap, f0 = tmp_ring.take()
            i1, e_ap, f1 = tmp_ring.take()
            d, e1, e2 = d_ap[:, 0:half], e_ap[:, 0:half], near[:, c0:c0 + half]
            t0 = sp.dma(d, dist[:, c0:c0 + half], dist_sem, f0)
            t = dve.put(lambda e1=e1, d=d: V.tensor_scalar(e1, d, 0.0, None, ALU.max), t0, f1)
            t = act.put(lambda e1=e1: S.activation(e1, e1, ACT.Exp, scale=log_gamma[:, h:h + 1]), t, lg_ready)
            t_f = pool.put(lambda e1=e1, c0=c0: G.affine_select(out=e1, in_=e1, compare_op=ALU.is_ge, fill=0.0,
                                                               base=c0 - 3 * P, pattern=[[1, half]], channel_multiplier=-1), t)
            t = dve.put(lambda e2=e2, d=d: V.tensor_scalar(e2, d, 0.0, None, ALU.min), t0, near_used[0])
            t = act.put(lambda e2=e2: S.activation(e2, e2, ACT.Exp, scale=neg_lg[:, 4 + h:5 + h]), t, lg_ready)
            t_b = pool.put(lambda e2=e2, c0=c0: G.affine_select(out=e2, in_=e2, compare_op=ALU.is_ge, fill=0.0,
                                                               base=3 * P - c0, pattern=[[-1, half]], channel_multiplier=1), t)
            t_n = dve.put(lambda e1=e1, e2=e2: V.tensor_tensor(e2, e2, e1, ALU.add), t_f, t_b)
            done.append(t_n)
            n = min(half, NLAT + P - c0)
            if n > 0:
                fo = far[:, c0:c0 + n]
                t = act.put(lambda fo=fo, d=d, n=n: S.activation(fo, d[:, 0:n], ACT.Exp, bias=far_bias[:, h:h + 1],
                                                                scale=log_gamma[:, h:h + 1]), t0, lg_ready, near_used[0])
                t_e = act.put(lambda e1=e1, d=d, n=n: S.activation(e1[:, 0:n], d[:, 0:n], ACT.Exp, bias=far_bias[:, 4 + h:5 + h],
                                                                  scale=neg_lg[:, 4 + h:5 + h]), t_n)
                t_n = dve.put(lambda fo=fo, e1=e1, n=n: V.tensor_tensor(fo, fo, e1[:, 0:n], ALU.add), t, t_e)
                done.append(t_n)
            tmp_ring.give(i0, t_n)
            tmp_ring.give(i1, t_n)
        near_ready[0] = done

    ret = {"q": {}, "k": {}, "v": [], "gate": {}, "s_read": [], "qk_read": [], "v_read": [], "y_read": [],
           "s_ready": {}, "vt_read": [], "sq_read": []}
    Y = Split({g: [y_hi[g], y_lo[g]] for g in BOTH})

    def ret_project_qk(h):
        for name, dst in (("q", ret_q), ("k", ret_k)):
            for half in range(2):
                outs = linear(X, KD, BOTH)
                i, bank, t = outs[0]
                ret[name][half, CTX] = [act.put(lambda bank=bank, half=half, dst=dst: S.activation(
                    dst[:, half, 0:NCTX], bank, ACT.Copy), t, ret["qk_read"])]
                lin.give(i, *ret[name][half, CTX])
                i, bank, t = outs[1]
                lat = slice(NCTX, NTOK)
                if half == 0:
                    t1 = act.put(lambda bank=bank, dst=dst: S.activation(dst[:, 0, lat], bank, ACT.Copy), t, ret["qk_read"])
                    lin.give(i, t1)
                    continue
                i0, t_ap, free = tmp_ring.take()
                i1, u_ap, free1 = tmp_ring.take()
                x1, x2, p1, p2 = dst[:, 0, lat], dst[:, 1, lat], t_ap[:, 0:NLAT], u_ap[:, 0:NLAT]
                ta = dve.put(lambda bank=bank, p1=p1: V.tensor_tensor(p1, bank, rope[1][:, :], ALU.mult), t, free, rope_loaded)
                tb = dve.put(lambda bank=bank, x2=x2: V.tensor_tensor(x2, bank, rope[0][:, :], ALU.mult), t, ret["qk_read"])
                lin.give(i, tb)
                tc = pool.put(lambda x1=x1, p2=p2: G.tensor_tensor(p2, x1, rope[1][:, :], ALU.mult), t1, free1, rope_loaded)
                td = pool.put(lambda x1=x1: G.tensor_tensor(x1, x1, rope[0][:, :], ALU.mult), tc)
                te = dve.put(lambda x2=x2, p2=p2: V.tensor_tensor(x2, x2, p2, ALU.add), tb, tc)
                tf = dve.put(lambda x1=x1, p1=p1: V.tensor_tensor(x1, x1, p1, ALU.subtract), td, ta)
                tmp_ring.give(i0, tf)
                tmp_ring.give(i1, te)
                ret[name][0, LAT], ret[name][1, LAT] = [tf], [te]

    def ret_project_vg(h):
        ret["v"] = []
        for j in range(4):
            outs = linear(X, KD, BOTH)
            ts = []
            for (i, bank, t), g in zip(outs, BOTH):
                cols = slice(START[g], START[g] + TOKENS[g])
                ts.append(act.put(lambda bank=bank, cols=cols: S.activation(ret_vt[:, cols], bank, ACT.Copy), t, ret["vt_read"]))
                lin.give(i, ts[-1])
            ret["vt_read"] = []
            for s0, ns in ((0, 2), (2, 4)):
                i, bank, free = att.take()
                for s in range(ns):
                    cols = slice((s0 + s) * P, (s0 + s + 1) * P)
                    t = pe.put(lambda s=s, bank=bank, cols=cols: T.transpose(bank[:, s * P:(s + 1) * P], ret_vt[:, cols], ident[:, :]), ts, free, consts)
                t2 = dve.put(lambda bank=bank, s0=s0, ns=ns, j=j: V.tensor_copy(
                    ret_v[:, s0:s0 + ns, j * P:(j + 1) * P], bank[:, 0:ns * P].rearrange("p (s c) -> p s c", c=P)), t, ret["v_read"])
                att.give(i, t2)
                ret["vt_read"].append(t)
                ret["v"].append(t2)
        for j in range(4):
            outs = linear(X, KD, BOTH)
            for (i, bank, t), g in zip(outs, BOTH):
                t2 = act.put(lambda bank=bank, g=g, j=j: S.activation(gate[g][:, j, :], bank, ACT.Silu), t, ret["y_read"])
                lin.give(i, t2)
                ret["gate"][j, g] = t2

    def ret_scores():
        reads = []
        for s in range(NTOK // P):
            g_s = CTX if s < 2 else LAT
            for g_t in ((CTX, LAT) if s < 2 else (LAT,)):
                n = TOKENS[g_t]
                i, bank, free = att.take()
                tq = slice(START[g_t], START[g_t] + n)
                for half in range(2):
                    t = pe.put(lambda half=half, bank=bank, n=n, s=s, tq=tq: T.matmul(
                        bank[:, 0:n], ret_k[:, half, s * P:(s + 1) * P], ret_q[:, half, tq], start=half == 0, stop=half == 1),
                        free, ret["k"][half, g_s], ret["q"][half, g_t])
                if g_s == CTX and g_t == CTX:
                    dst, table = scores_ctx[:, s, :], near[:, 3 * P - s * P:3 * P - s * P + n]
                elif g_s == CTX:
                    dst, table = scores[:, s, :], far[:, P - s * P:P - s * P + n]
                else:
                    dst, table = scores[:, s, :], near[:, 3 * P - (s - 2) * P:3 * P - (s - 2) * P + n]
                t2 = dve.put(lambda bank=bank, n=n, dst=dst, table=table: V.scalar_tensor_tensor(
                    dst, bank[:, 0:n], RET_DK ** -0.5, table, ALU.mult, ALU.mult), t, near_ready[0], ret["s_read"])
                att.give(i, t2)
                ret["s_ready"][s, g_t] = t2
                near_used[0] = [t2]
                ret["qk_read"] = [t]
                yield

    def ret_readout():
        for g in BOTH:
            n = TOKENS[g]
            src = scores if g == LAT else scores_ctx
            nsrc = NTOK // P if g == LAT else NCTX // P
            o_ready = []
            sq, u = ret_sq[:, 0:n], ret_u[:, 0:n]
            for j in range(4):
                i, bank, free = att.take()
                for s in range(nsrc):
                    call = (lambda s=s, bank=bank, j=j: T.matmul(bank[:, 0:n], ret_v[:, s, j * P:(j + 1) * P], src[:, s, :],
                                                                 start=s == 0, stop=s == nsrc - 1))
                    t = pe.put(call, free, ret["v"], ret["s_ready"][s, g])
                if j == 0:
                    t_sq = act.put(lambda bank=bank: S.activation(sq, bank[:, 0:n], ACT.Square), t, ret["sq_read"])
                else:
                    tu = act.put(lambda bank=bank: S.activation(u, bank[:, 0:n], ACT.Square), t, t_sq)
                    t_sq = pool.put(lambda: G.tensor_tensor(sq, sq, u, ALU.add), tu)
                t_y = dve.put(lambda bank=bank, j=j: V.tensor_tensor(gate[g][:, j, :], bank[:, 0:n], gate[g][:, j, :], ALU.mult), t_sq if j == 0 else tu, ret["gate"][j, g])
                att.give(i, t_y)
                o_ready.append(t_y)
                ret["s_read"] = [t]
                ret["v_read"] = [t]
                yield
            i, rows, t = rstd_rows(sq, n, t_sq, RET_DV, RMS_EPS, sq)
            ret["sq_read"] = [t]
            for j in range(4):
                t2 = dve.put(lambda j=j, rows=rows: V.tensor_tensor(gate[g][:, j, :], gate[g][:, j, :], rows, ALU.mult), t, o_ready[j])
                Y.ready[j, g] = []
                put_split(Y, j, g, gate[g][:, j, :], t2)
            att.give(i, t2)
            yield

    def ret_out():
        for o in range(KD):
            add_gated(0, 2, o, BOTH, linear(Y, 4, BOTH))
        ret["y_read"] = Y.read

    for h in range(RET_HEADS):
        ret_project_qk(h)
        drain()
        decay_tables(h)
        background.append(ret_scores())
        if h:
            ret_out()
        ret_project_vg(h)
        drain()
        background.append(ret_readout())
    drain()
    ret_out()
    drain_trickle()

    prev = fence()
    m = Map(PHASE, ada_end)
    scr = ({g: m.sb(f"ln0_tot{g}", [P, TOKENS[g]])[:, :] for g in BOTH},
           {g: m.sb(f"ln0_sq{g}", [P, TOKENS[g]])[:, :] for g in BOTH})
    layer_norm(0, BOTH, scr, prev)
    modulate(0, 3, BOTH)
    trickle.append(ada_chunks(1, range(6)))
    scr = ffn("ffn0", BOTH, prev, m.at, lambda o, outs: add_gated(0, 5, o, BOTH, outs))
    drain_trickle()
    layer_norm(1, BOTH, scr, prev)
    modulate(1, 0, BOTH)

    def attend(jobs, p_ring, pt_ring):
        def stage_scores(job):
            n_all = sum(s[0] for s in job["segs"])
            pi, p_full, p_free = p_ring.take()
            p = p_full[:, 0:n_all]
            col, written = 0, []
            for n, mms, bias, view, place in job["segs"]:
                i, bank, free = att.take()
                for x, (lhsT, rhs) in enumerate(mms):
                    t = pe.put(lambda lhsT=lhsT, rhs=rhs, bank=bank, n=n, view=view: T.matmul(
                        view(bank[:, 0:n]), lhsT, rhs, start=True, stop=True), free, job["ready"])
                dst = p[:, col:col + n]
                if bias is None:
                    t2 = act.put(lambda dst=dst, bank=bank, n=n: S.activation(dst, bank[:, 0:n], ACT.Copy), t, p_free)
                else:
                    t2 = dve.put(lambda: V.tensor_tensor(place(dst), view(bank[:, 0:n]), view(bias), ALU.add),
                                 t, p_free, job["bias_ready"])
                att.give(i, t2)
                written.append(t2)
                col += n
            job["scored"] = t
            job["bias_read"](written)
            neg, total, inv = (small[:, 48 + 3 * pi + x:49 + 3 * pi + x] for x in range(3))
            t = dve.put(lambda: V.tensor_reduce(neg, p, AX, ALU.max, negate=True), written)
            t = act.put(lambda: S.activation(p, p, ACT.Exp, bias=neg, accum_out=total), t)
            t = dve.put(lambda: V.reciprocal(inv, total), t)
            job["p"] = (pi, p, dve.put(lambda: V.tensor_scalar(p, p, inv, None, ALU.mult), t))

        def stage_transpose(job):
            pi, p, t_p = job["p"]
            n = p.shape[-1] // P
            qi, pt, pt_free = pt_ring.take()
            ts = []
            for c0 in range(0, n, 4):
                nc_ = min(4, n - c0)
                i, bank, free = att.take()
                for c in range(nc_):
                    t = pe.put(lambda c=c, c0=c0, bank=bank: T.transpose(bank[:, c * P:(c + 1) * P], p[:, (c0 + c) * P:(c0 + c + 1) * P], ident[:, :]),
                               t_p, free)
                dst = pt[:, c0 * P:(c0 + nc_) * P]
                t2 = act.put(lambda dst=dst, bank=bank, nc_=nc_: S.activation(dst, bank[:, 0:nc_ * P], ACT.Copy), t, pt_free)
                att.give(i, t2)
                ts.append(t2)
            p_ring.give(pi, t)
            job["pt"] = (qi, pt, ts)

        held = {}

        def stage_values(job):
            qi, pt, ts = job["pt"]
            rows = slice(64 * job["half"], 64 * job["half"] + 64)
            if job["half"] == 0:
                held["o"] = last.take()
            i, bank, free = held["o"]
            nv = len(job["vals"])
            for c, v in enumerate(job["vals"]):
                t = pe.put(lambda c=c, v=v, bank=bank, rows=rows: T.matmul(bank[rows, 0:P], v, pt[:, c * P:(c + 1) * P],
                                                                        start=c == 0, stop=c == nv - 1), ts, free, job["v_ready"])
            pt_ring.give(qi, t)
            if job["half"] == 1:
                last.give(i, *job["finish"](bank[:, 0:P], t))
                if job.get("done"):
                    job["done"](t)

        for s in range(len(jobs) + 2):
            if s < len(jobs):
                stage_scores(jobs[s])
            if 0 <= s - 1 < len(jobs):
                stage_transpose(jobs[s - 1])
            if 0 <= s - 2 < len(jobs):
                stage_values(jobs[s - 2])
            yield

    prev = fence()
    m = Map(PHASE, END)
    na_y = Split({LAT: [m.sb(f"na_y_{s}", [P, KD, NLAT], F32R) for s in ("hi", "lo")]})
    na_q = Ring([m.sb(f"na_q{i}", [P, NLAT]) for i in range(2)])
    na_k = Ring([m.sb(f"na_k{i}", [P, NTOK]) for i in range(2)])
    na_v = Ring([m.sb(f"na_v{i}", [P, 10, P]) for i in range(2)])
    na_vt = m.sb("na_vt", [P, NTOK])
    na_rel = Ring([m.sb(f"na_rel{i}", [P, ROWS, REL]) for i in range(2)])
    na_bias = Ring([m.sb(f"na_bias{i}", [P, 3, ROWS * BAND]) for i in range(2)])
    na_mask = m.sb("na_mask", [P, 3, BAND])
    na_p = Ring([m.sb(f"na_p{i}", [P, NCTX + ROWS * BAND]) for i in range(2)])
    na_pt = Ring([m.sb(f"na_pt{i}", [P, NCTX + ROWS * BAND]) for i in range(2)])
    for r in (na_q, na_k, na_v, na_rel, na_bias, na_p, na_pt):
        r.free = [list(prev) for _ in r.free]
    na_y.read = prev
    mask_sem = dma_slot("loaded_na_mask")
    mask_loaded = pool.dma(na_mask[:, :, :], a["na_mask"], mask_sem, prev)
    rel_sem = [dma_slot(f"loaded_rel{i}") for i in range(2)]

    pad_sem = dma_slot("stored_rpb")
    rpb_dram = nc.dram_tensor("rpb_padded", [NA_HEADS * RPB_ROWS, RPB_WIDE], F32)
    half_rows = NA_HEADS * RPB_ROWS // 2
    pad = tmp[0:half_rows, 0, 0:2 * RPB_WIDE].rearrange("p (a c) -> p a c", a=2)
    ti, _, free = tmp_ring.take()
    if ti != 0:
        tmp_ring.give(ti, *free)
        ti, _, free = tmp_ring.take()
    t = pool.put(lambda: G.memset(pad, 0.0), free)
    t = pool.dma(pad[:, :, 16:16 + RPB_COLS], a["rpb"], pad_sem, t)
    rpb_stored = pool.dma(rpb_dram.ap().rearrange("(p a) c -> p a c", a=2), pad, pad_sem, t)
    tmp_ring.give(ti, rpb_stored)
    rpb_size = NA_HEADS * RPB_ROWS * RPB_WIDE
    rpb_copies = nc.dram_tensor("rpb_copies", [QB, rpb_size], F32)
    copy_sem = dma_slot("copied_rpb")
    rpb_stored = pool.dma(rpb_copies.ap(), bass.AP(rpb_dram.ap().tensor, 0, [[0, QB], [1, rpb_size]]), copy_sem, rpb_stored)

    BAND_START = [BAND0[n] - QB * n + QB for n in range(4)]
    VARIANT = [0, 1, 1, 2]
    grid = lambda ap: ap.rearrange("p (r c) -> p r c", c=GRID)
    vt_read = [prev]

    def na_head_bias(head):
        ri, rel, rfree = na_rel.take()
        for r in range(ROWS):
            src = bass.AP(rpb_copies.ap().tensor, (head * RPB_ROWS + 7 - r) * RPB_WIDE + 15,
                          [[rpb_size - 1, QB], [RPB_WIDE, ROWS], [1, REL]])
            t = pool.dma(rel[r * QB:(r + 1) * QB, :, :], src, rel_sem[ri], rfree, rpb_stored)
        bi, bias, bfree = na_bias.take()
        ts = []
        for v, n in enumerate((0, 1, 3)):
            b0 = BAND_START[n]
            ts.append(pool.put(lambda v=v, b0=b0: G.tensor_tensor(
                bias[:, v, :].rearrange("p (r c) -> p r c", c=BAND), rel[:, :, b0:b0 + BAND],
                na_mask[:, v:v + 1, :].to_broadcast([P, ROWS, BAND]), ALU.add), t, bfree, mask_loaded))
        na_rel.give(ri, *ts)
        return bi, bias, ts

    plain = lambda ap: ap

    def na_pair(pair):
        qi, q, qfree = na_q.take()
        (i, bank, t), = linear(X, KD, ONLY_LAT, 4)
        tq = act.put(lambda: S.activation(q[:, :].rearrange("p (n r c) -> p r n c", r=ROWS, c=QB),
                                          bank.rearrange("p (r n c) -> p r n c", r=ROWS, c=QB),
                                          ACT.Copy, scale=HEAD ** -0.5), t, qfree)
        lin.give(i, tq)
        ki, kk, kfree = na_k.take()
        tk = []
        for (i, bank, t), g in zip(linear(X, KD, BOTH, 4), BOTH):
            tk.append(act.put(lambda bank=bank, g=g: S.activation(kk[:, START[g]:START[g] + TOKENS[g]], bank, ACT.Copy), t, kfree))
            lin.give(i, tk[-1])
        vi, vv, vfree = na_v.take()
        tv = []
        for (i, bank, t), g in zip(linear(X, KD, BOTH, 4), BOTH):
            dst = na_vt[:, START[g]:START[g] + TOKENS[g]]
            if g == LAT:
                dst, bank = dst.rearrange("p (c r) -> p r c", r=ROWS), grid(bank)
            tv.append(act.put(lambda: S.activation(dst, bank, ACT.Copy), t, vt_read[0]))
            lin.give(i, tv[-1])
        tiles = [na_vt[:, s * P:(s + 1) * P] for s in range(2)]
        for n in range(4):
            for u in range(2):
                c0 = NCTX + ROWS * (BAND0[n] + QB * u)
                tiles.append(na_vt[:, c0:c0 + P])
        v_ready = []
        for c0 in range(0, 10, 4):
            nt = min(4, 10 - c0)
            i, bank, free = att.take()
            for c in range(nt):
                t = pe.put(lambda c=c, c0=c0, bank=bank: T.transpose(bank[:, c * P:(c + 1) * P], tiles[c0 + c], ident[:, :]), tv, free)
            t2 = dve.put(lambda c0=c0, nt=nt, bank=bank: V.tensor_copy(vv[:, c0:c0 + nt, :], bank[:, 0:nt * P].rearrange("p (s c) -> p s c", c=P)), t, vfree)
            att.give(i, t2)
            v_ready.append(t2)
        vt_read[0] = [t]
        jobs = []
        drain()
        biases = [na_head_bias(2 * pair + e) for e in range(2)]
        for n in range(4):
            for e in range(2):
                rows = slice(64 * e, 64 * e + 64)
                bi, bias, b_ready = biases[e]
                lhsT = q[rows, n * P:(n + 1) * P]
                keys = grid(kk[rows, NCTX:NTOK])[:, :, BAND0[n]:BAND0[n] + BAND]

                def bias_read(ts, n=n, bi=bi):
                    if n == 3:
                        na_bias.give(bi, *ts)

                def finish(bank, t, n=n):
                    view = lambda ap: grid(ap)[:, :, QB * n:QB * n + QB]
                    return put_split(na_y, pair, LAT, bank.rearrange("p (r c) -> p r c", c=QB), t, view=view)

                def done(t, n=n):
                    if n == 3:
                        na_q.give(qi, t)
                        na_k.give(ki, t)
                        na_v.give(vi, t)

                jobs.append(dict(segs=[(NCTX, [(lhsT, kk[rows, 0:NCTX])], None, plain, plain),
                                       (ROWS * BAND, [(lhsT, keys)], bias[:, VARIANT[n], :],
                                        lambda ap: ap.rearrange("p (r c) -> p r c", c=BAND),
                                        lambda ap: ap.rearrange("p (c r) -> p r c", c=BAND))],
                                 ready=[tq] + tk, bias_ready=b_ready, bias_read=bias_read, half=e, v_ready=v_ready,
                                 vals=[vv[:, s, 64 * e:64 * e + 64] for s in (0, 1, 2 + 2 * n, 3 + 2 * n)],
                                 finish=finish, done=done))
        return jobs

    for pair in range(NA_HEADS // 2):
        jobs = na_pair(pair)
        background.append(attend(jobs, na_p, na_pt))
    drain()
    for o in range(KD):
        add_gated(1, 2, o, ONLY_LAT, linear(na_y, KD, ONLY_LAT))

    prev = fence()
    m = Map(PHASE, ada_end)
    scr = ({LAT: m.sb("ln2_tot", [P, NLAT])[:, :]}, {LAT: m.sb("ln2_sq", [P, NLAT])[:, :]})
    layer_norm(2, ONLY_LAT, scr, prev)
    modulate(1, 3, ONLY_LAT)
    scr = ffn("ffn1", ONLY_LAT, prev, m.at, lambda o, outs: add_gated(1, 5, o, ONLY_LAT, outs))
    layer_norm(3, ONLY_LAT, scr, prev)

    def to_x(k, ap, t):
        X.ready[k, LAT] = []
        return put_split(X, k, LAT, ap, t)

    rms_scale(LAT, None, scr[1][LAT], "g_mix", prev, to_x)

    prev = fence()
    m = Map(PHASE, END)
    o_a = Split({LAT: [m.sb(f"o_a_{s}", [P, 2, NLAT], F32R) for s in ("hi", "lo")]})
    o_b = Split({LAT: [m.sb(f"o_b_{s}", [P, 4, NLAT], F32R) for s in ("hi", "lo")]})
    o_c = Split({LAT: [m.sb(f"o_c_{s}", [P, 4, NLAT], F32R) for s in ("hi", "lo")]})
    for x in (o_a, o_b, o_c):
        x.read = prev
    merge_start = m.at
    DIL_KEYS = NLAT + 2 * P
    U0W = NLAT + 3
    dil_q = [m.sb(f"dil_q{g}", [P, NLAT]) for g in range(3)]
    moba_start = m.at
    dil_k = [m.sb(f"dil_k{g}", [P, NLAT]) for g in range(3)]
    dil_v = m.sb("dil_v", [P, 12, P])
    vt2 = m.sb("vt2", [P, NLAT])
    dil_bias = Ring([m.sb(f"dil_bias{i}", [P, U0W + 2 * P]) for i in range(2)])
    p_ring = Ring([m.sb(f"p2_{i}", [P, DIL_KEYS]) for i in range(2)])
    pt_ring = Ring([m.sb(f"pt2_{i}", [P, DIL_KEYS]) for i in range(2)])
    c = Map(ctx_start, ctx_end)
    lru = {n: c.sb(f"lru_{n}", [P, NLAT + (3 if n == "x" else 0)]) for n in ("x", "g", "xc", "r", "ig", "a", "s", "u")}
    gate_w = c.sb("lru_gate_w", [P, 2, LRU_TILES, P])
    for r in (dil_bias, p_ring, pt_ring):
        r.free = [list(prev) for _ in r.free]

    PATTERNS = (("w", 0, 4, 1024), ("d4", 4, 4, 256), ("d16", 8, 4, 256), ("c", 12, 8, 640))
    table = c.sb("rel_table", [33, 20])
    table_sem, hot_sem, toep_sem = dma_slot("loaded_table"), dma_slot("loaded_onehot"), dma_slot("stored_toeplitz")
    table_loaded = pool.dma(table[:, :], a["table"], table_sem, prev)
    toep, copied_sem = {}, dma_slot("copied_toeplitz")
    for name, h0, nh, width in PATTERNS:
        toep[name] = nc.dram_tensor(f"toeplitz_{name}", [nh, width], F32)
        for c0 in range(0, width, 512):
            n = min(512, width - c0)
            pi, hot, free = p_ring.take()
            loaded = pool.dma(hot[0:33, 0:n], a[f"hot_{name}"][:, c0:c0 + n], hot_sem, free)
            i, bank, bfree = att.take()
            t = pe.put(lambda bank=bank, hot=hot, n=n, h0=h0, nh=nh: T.matmul(
                bank[0:nh, 0:n], table[:, h0:h0 + nh], hot[0:33, 0:n], start=True, stop=True), loaded, table_loaded, bfree)
            qi, row, rfree = pt_ring.take()
            t2 = act.put(lambda bank=bank, row=row, n=n, nh=nh: S.activation(row[0:nh, 0:n], bank[0:nh, 0:n], ACT.Copy), t, rfree)
            att.give(i, t2)
            t3 = pool.dma(toep[name].ap()[:, c0:c0 + n], row[0:nh, 0:n], toep_sem, t2)
            toep_stored = t3
            p_ring.give(pi, t)
            pool.wait([t3])
            pt_ring.give(qi, t3)
        copies = nc.dram_tensor(f"toeplitz_copies_{name}", [P, nh * width], F32)
        toep_copied = pool.dma(copies.ap(), bass.AP(toep[name].ap().tensor, 0, [[0, P], [1, nh * width]]), copied_sem, toep_stored)
        toep[name] = (copies, nh * width)

    def diagonals(name, head, width, base, step, cols):
        copies, pitch = toep[name]
        return bass.AP(copies.ap().tensor, head * width + base, [[pitch + step, P], [1, cols]])

    bias_sem = [dma_slot(f"loaded_dil_bias{i}") for i in range(2)]

    def dil_head_bias(j):
        bi, bias, free = dil_bias.take()
        pool.dma(bias[:, 0:U0W], diagonals("w", j, 1024, 508, -4, U0W), bias_sem[bi], free, toep_copied)
        pool.dma(bias[:, U0W:U0W + P], diagonals("d4", j, 256, 127, -1, P), bias_sem[bi])
        t = pool.dma(bias[:, U0W + P:U0W + 2 * P], diagonals("d16", j, 256, 127, -1, P), bias_sem[bi])
        return bi, bias, [t]

    dil = {"read": [prev], "vt": [prev]}
    by4 = lambda ap: ap.rearrange("p (i r) -> p r i", r=4)

    def v_tiles(dst, sources, ready, free_v):
        ts = []
        for c0 in range(0, len(sources), 4):
            nt = min(4, len(sources) - c0)
            i, bank, free = att.take()
            for c in range(nt):
                t = pe.put(lambda c=c, c0=c0, bank=bank: T.transpose(bank[:, c * P:(c + 1) * P], sources[c0 + c], ident[:, :]), ready, free)
            t2 = dve.put(lambda c0=c0, nt=nt, bank=bank: V.tensor_copy(dst(c0, nt), bank[:, 0:nt * P].rearrange("p (s c) -> p s c", c=P)), t, free_v)
            att.give(i, t2)
            ts.append(t2)
        return ts, t

    def dilated_pair(jp):
        ready = []
        for name, dst in (("q", dil_q), ("k", dil_k)):
            for g in range(3):
                (i, bank, t), = linear(X, KD, ONLY_LAT)
                ready.append(act.put(lambda bank=bank, d=dst[g], s=(HEAD ** -0.5 if name == "q" else 1.0):
                                     S.activation(d[:, :], bank, ACT.Copy, scale=s), t, dil["read"]))
                lin.give(i, ready[-1])
        v_ready = []
        for g in range(3):
            (i, bank, t), = linear(X, KD, ONLY_LAT)
            tv = act.put(lambda bank=bank: S.activation(vt2[:, :], bank, ACT.Copy), t, dil["vt"])
            lin.give(i, tv)
            src = [vt2[:, s * P:(s + 1) * P] if g == 0 else by4(vt2[:, :])[:, s, :] for s in range(4)]
            ts, t = v_tiles(lambda c0, nt, g=g: dil_v[:, 4 * g + c0:4 * g + c0 + nt, :], src, tv, dil["read"])
            dil["vt"] = [t]
            v_ready += ts
        drain()
        biases = [dil_head_bias(2 * jp + e) for e in range(2)]
        jobs = []
        for r in range(4):
            for e in range(2):
                rows = slice(64 * e, 64 * e + 64)
                bi, bias, b_ready = biases[e]

                def bias_read(ts, r=r, bi=bi):
                    if r == 3:
                        dil_bias.give(bi, *ts)

                def finish(bank, t, r=r):
                    return put_split(o_a, jp, LAT, bank, t, view=lambda ap: by4(ap)[:, r, :])

                def done(t, r=r):
                    if r == 3:
                        dil["read"] = [t]

                q = [by4(dil_q[g][rows, :])[:, r, :] for g in range(3)]
                segs = [(NLAT, [(q[0], dil_k[0][rows, :])], bias[:, 3 - r:3 - r + NLAT], plain, plain)]
                for g in (1, 2):
                    segs.append((P, [(q[g], by4(dil_k[g][rows, :])[:, r, :])], bias[:, U0W + (g - 1) * P:U0W + g * P], plain, plain))
                jobs.append(dict(segs=segs, ready=ready, bias_ready=b_ready, bias_read=bias_read, half=e, v_ready=v_ready,
                                 vals=[dil_v[:, s, 64 * e:64 * e + 64] for s in (0, 1, 2, 3, 4 + r, 8 + r)],
                                 finish=finish, done=done))
        return jobs

    lru_sem = dma_slot("loaded_lru_gates")
    t = pool.put(lambda: G.memset(gate_w[:, :, :, :], 0.0), prev)
    for which, name in enumerate(("lru_wa", "lru_wx")):
        for e in range(2):
            rows = slice(64 * e, 64 * e + 64)
            gates_loaded = pool.dma(gate_w[rows, which, :, rows], a[name][e], lru_sem, t)
    t_pad = pool.put(lambda: G.memset(lru["x"][:, 0:3], 0.0), prev)
    lam = vc("lru_lam", 0, 4)
    y0, z, z2, acc, sp_c = (small[:, 64 + 4 * i:68 + 4 * i] for i in range(5))
    t = act.put(lambda: S.activation(y0, lam, ACT.Abs), consts)
    t = act.put(lambda: S.activation(y0, y0, ACT.Exp, scale=-1.0), t)
    t = dve.put(lambda: V.tensor_scalar(z, y0, 2.0, None, ALU.add), t)
    t = dve.put(lambda: V.reciprocal(z, z), t)
    t = dve.put(lambda: V.tensor_tensor(z, z, y0, ALU.mult), t)
    t = dve.put(lambda: V.tensor_tensor(z2, z, z, ALU.mult), t)
    t = dve.put(lambda: V.tensor_scalar(acc, z2, 1.0 / 17, 1.0 / 15, ALU.mult, ALU.add), t)
    for d in (13, 11, 9, 7, 5, 3, 1):
        t = dve.put(lambda: V.tensor_tensor(acc, acc, z2, ALU.mult), t)
        t = dve.put(lambda d=d: V.tensor_scalar(acc, acc, 1.0 / d, None, ALU.add), t)
    t = dve.put(lambda: V.tensor_tensor(acc, acc, z, ALU.mult), t)
    t = dve.put(lambda: V.tensor_scalar(y0, lam, -1.0, 0.0, ALU.mult, ALU.max), t)
    t = dve.put(lambda: V.scalar_tensor_tensor(sp_c, acc, 2.0, y0, ALU.mult, ALU.add), t)
    sp_ready = dve.put(lambda: V.tensor_scalar(sp_c, sp_c, -8.0, None, ALU.mult), t)
    lru_free = {"x": [prev, t_pad], "g": [prev], "rest": [prev]}

    def lru_tile(k):
        xt, xc, r, ig, la, s, u = (lru[n] for n in ("x", "xc", "r", "ig", "a", "s", "u"))
        (i, bank, t), = linear(X, KD, ONLY_LAT, 4)
        tx = act.put(lambda: S.activation(xt[:, 3:3 + NLAT], bank, ACT.Copy), t, lru_free["x"])
        lin.give(i, tx)
        (i, bank2, t), = linear(X, KD, ONLY_LAT, 4)
        gb = lru["g"][:, :]
        tg = act.put(lambda: S.activation(gb, bank2, ACT.Copy), t, lru_free["g"])
        lin.give(i, tg)
        cw = lambda i: vc("conv_w", 4 * k + i)
        t = dve.put(lambda: V.tensor_scalar(xc[:, :], xt[:, 0:NLAT], cw(0), vc("conv_b", k), ALU.mult, ALU.add), tx, t_pad, lru_free["rest"])
        for i_ in range(1, 4):
            t = dve.put(lambda i_=i_: V.scalar_tensor_tensor(xc[:, :], xt[:, i_:i_ + NLAT], cw(i_), xc[:, :], ALU.mult, ALU.add), t)
        lru_free["x"] = [t]
        t_xc = t
        gates = []
        for which, (dst, b) in enumerate(((r, "lru_ba"), (ig, "lru_bx"))):
            i, bank3, free = att.take()
            t = pe.put(lambda bank3=bank3, which=which: T.matmul(bank3[:, :], gate_w[:, which, k, :], xc[:, :], start=True, stop=True), t_xc, free, gates_loaded)
            t2 = act.put(lambda bank3=bank3, dst=dst, b=b: S.activation(dst[:, :], bank3[:, :], ACT.Sigmoid, bias=vc(b, k)), t, lru_free["rest"])
            att.give(i, t2)
            gates.append(t2)
        t_la = dve.put(lambda: V.tensor_scalar(la[:, :], r[:, :], sp_c[:, k:k + 1], None, ALU.mult), gates, sp_ready, lru_free["rest"])
        t = dve.put(lambda: V.tensor_tensor(u[:, :], gb, gb, ALU.mult), tg, lru_free["rest"])
        t = dve.put(lambda: V.tensor_scalar(u[:, :], u[:, :], 0.044715, 1.0, ALU.mult, ALU.add), t)
        t = dve.put(lambda: V.tensor_tensor(u[:, :], u[:, :], gb, ALU.mult), t)
        t_u = act.put(lambda: S.activation(u[:, :], u[:, :], ACT.Tanh, scale=(2 / np.pi) ** 0.5), t)
        t_s = act.put(lambda: S.activation(s[:, :], la[:, :], ACT.Tanh, scale=-1.0), t_la)
        t_r = act.put(lambda: S.activation(r[:, :], la[:, :], ACT.Exp, scale=2.0), t_la)
        t_a = act.put(lambda: S.activation(la[:, :], la[:, :], ACT.Exp), t_r, t_s)
        t = dve.put(lambda: V.scalar_tensor_tensor(s[:, :], r[:, :], 1.0, s[:, :], ALU.add, ALU.mult), t_s, t_r)
        t_s = act.put(lambda: S.activation(s[:, :], s[:, :], ACT.Sqrt), t)
        t = dve.put(lambda: V.tensor_tensor(ig[:, :], ig[:, :], xc[:, :], ALU.mult), gates, t_xc)
        t = dve.put(lambda: V.tensor_tensor(s[:, :], s[:, :], ig[:, :], ALU.mult), t, t_s)
        t_h = dve.put(lambda: V.tensor_tensor_scan(r[:, :], la[:, :], s[:, :], 0.0, ALU.mult, ALU.add), t, t_a)
        t = dve.put(lambda: V.tensor_scalar(u[:, :], u[:, :], 0.5, 0.5, ALU.mult, ALU.add), t_u)
        t = dve.put(lambda: V.tensor_tensor(u[:, :], u[:, :], gb, ALU.mult), t)
        lru_free["g"] = [t]
        t = dve.put(lambda: V.tensor_tensor(u[:, :], u[:, :], r[:, :], ALU.mult), t, t_h)
        lru_free["rest"] = put_split(o_b, k, LAT, u[:, :], t)

    jobs = dilated_pair(0)
    background.append(attend(jobs, p_ring, pt_ring))
    for k in range(LRU_TILES):
        lru_tile(k)
    jobs = dilated_pair(1)
    background.append(attend(jobs, p_ring, pt_ring))

    c2 = Map(c.at, ctx_end)
    m2 = Map(ada_end, END)
    moba_bias_t = [m.sb(f"moba_bias{i}", [P, NLAT]) for i in range(2)] if m.at + 4096 + 64 <= END else [m2.sb(f"moba_bias{i}", [P, NLAT]) for i in range(2)]
    after_lru = fence()
    c3 = Map(ctx_start, ctx_end)
    mq = Ring([c3.sb(f"moba_q{i}", [P, NLAT]) for i in range(2)])
    mk = Ring([c3.sb(f"moba_k{i}", [P, NLAT]) for i in range(2)])
    mv = Ring([c3.sb(f"moba_v{i}", [P, 4, P]) for i in range(2)])
    mb = Ring(moba_bias_t)
    for r in (mq, mk, mv, mb):
        r.free = [list(after_lru) for _ in r.free]
    mb_sem = [dma_slot(f"loaded_moba_bias{i}") for i in range(2)]

    def moba_pair(pair):
        (i, bank, t), = linear(X, KD, ONLY_LAT, 4)
        qi, q, free = mq.take()
        tq = act.put(lambda: S.activation(q[:, :], bank, ACT.Copy, scale=HEAD ** -0.5), t, free)
        lin.give(i, tq)
        (i, bank1, t), = linear(X, KD, ONLY_LAT, 4)
        ki, kk, free = mk.take()
        tk = act.put(lambda: S.activation(kk[:, :], bank1, ACT.Copy), t, free)
        lin.give(i, tk)
        (i, bank2, t), = linear(X, KD, ONLY_LAT, 4)
        tv = act.put(lambda: S.activation(vt2[:, :], bank2, ACT.Copy), t, dil["vt"])
        lin.give(i, tv)
        vi, vv, free = mv.take()
        v_ready, t = v_tiles(lambda c0, nt: vv[:, c0:c0 + nt, :], [vt2[:, s * P:(s + 1) * P] for s in range(4)], tv, free)
        dil["vt"] = [t]
        drain()
        biases = []
        for e in range(2):
            bi, bias, free = mb.take()
            biases.append((bi, bias, [pool.dma(bias[:, :], diagonals("c", 2 * pair + e, 640, 127, -1, NLAT), mb_sem[bi], free, toep_copied)]))
        jobs = []
        for n in range(4):
            for e in range(2):
                rows = slice(64 * e, 64 * e + 64)
                bi, bias, b_ready = biases[e]

                def bias_read(ts, n=n, bi=bi):
                    if n == 3:
                        mb.give(bi, *ts)

                def finish(bank, t, n=n):
                    return put_split(o_c, pair, LAT, bank, t, view=lambda ap: ap[:, n * P:(n + 1) * P])

                def done(t, n=n):
                    if n == 3:
                        mq.give(qi, t)
                        mk.give(ki, t)
                        mv.give(vi, t)

                keys = (n + 1) * P
                jobs.append(dict(segs=[(keys, [(q[rows, n * P:(n + 1) * P], kk[rows, 0:keys])],
                                        bias[:, NLAT - keys:NLAT], plain, plain)],
                                 ready=[tq, tk], bias_ready=b_ready, bias_read=bias_read, half=e, v_ready=v_ready,
                                 vals=[vv[:, s, 64 * e:64 * e + 64] for s in range(n + 1)], finish=finish, done=done))
        background.append(attend(jobs, p_ring, pt_ring))

    for pair in range(MOBA_HEADS // 2):
        moba_pair(pair)
    drain()

    prev = fence()
    m = Map(merge_start, END)
    merged = Split({LAT: [m.sb(f"merged_{s}", [P, KD, NLAT], F32R) for s in ("hi", "lo")]})
    merged.read = prev
    gates_r = Ring([m.sb(f"gate2_{i}", [P, NLAT]) for i in range(3)])
    sum_r = Ring([m.sb(f"sum2_{i}", [P, NLAT]) for i in range(2)])
    for r in (gates_r, sum_r):
        r.free = [list(prev) for _ in r.free]
    for o in range(KD):
        si, total, sfree = sum_r.take()
        t_sum = None
        for branch, (x, kt) in enumerate(((o_a, 2), (o_b, 4), (o_c, 4))):
            (i, bank, t), = linear(X, KD, ONLY_LAT)
            gi, gt, free = gates_r.take()
            tg = act.put(lambda bank=bank, gt=gt: S.activation(gt[:, :], bank, ACT.Sigmoid), t, free)
            lin.give(i, tg)
            (i, bank, t), = linear(x, kt, ONLY_LAT)
            dst = total if branch == 0 else gt
            t2 = dve.put(lambda bank=bank, gt=gt, dst=dst: V.tensor_tensor(dst[:, :], bank, gt[:, :], ALU.mult), t, tg, sfree)
            lin.give(i, t2)
            if branch:
                t2 = dve.put(lambda gt=gt, total=total: V.tensor_tensor(total[:, :], total[:, :], gt[:, :], ALU.add), t2, t_sum)
            t_sum = t2
            gates_r.give(gi, t2)
        sum_r.give(si, *put_split(merged, o, LAT, total[:, :], t_sum))

    def add_plain(o, outs):
        (i, bank, t), = outs
        t2 = dve.put(lambda: V.tensor_tensor(H[LAT][:, o, :], bank, H[LAT][:, o, :], ALU.add), t, h_ready[o, LAT])
        h_ready[o, LAT] = [t2]
        lin.give(i, t2)

    for o in range(KD):
        add_plain(o, linear(merged, KD, ONLY_LAT))
    prev = fence()
    m = Map(PHASE, ada_end)
    sq3 = m.sb("sq3", [P, NLAT])
    rms_scale(LAT, None, sq3[:, :], "g_ffn", prev, to_x)
    scr = ffn("ffn2", ONLY_LAT, prev, m.at, add_plain)

    out_sem = dma_slot("stored_out")

    def store(k, ap, t):
        end = sp.dma(out[:, k, :], ap, out_sem, t)
        sp.wait([end])
        return [end]

    rms_scale(LAT, None, scr[1][LAT], "g_final", prev, store)
    assert state["taken"] == len(plan)

    stack.close()


def _blocks(m):
    K, N = m.shape
    return np.ascontiguousarray(m.reshape(K // P, P, N // P, P).transpose(2, 1, 0, 3)).reshape(N // P, P, K)


def _cols(v):
    return np.ascontiguousarray(v.reshape(-1, P).T)


def _buckets(dist):
    d = np.maximum(dist, 0)
    df = np.maximum(d, 1).astype(np.float32)
    large = 16 + (np.log(df / np.float32(16)) / np.float32(np.log(2048 / 16)) * np.float32(16)).astype(np.int32)
    return np.where(d < 16, d, np.minimum(large, 31))


def _one_hot(dist, valid, width):
    hot = np.zeros((33, width), np.float32)
    row = np.where(valid, _buckets(dist), 32)
    hot[row, np.arange(len(dist))] = 1.0
    hot[32, len(dist):] = 1.0
    return hot


def _constants():
    t = np.arange(NLAT)
    nf = RET_DK // 4
    inv = np.float32(10000.0) ** (-np.arange(nf, dtype=np.float32) / np.float32(nf))
    ang = np.concatenate([(t // GRID).astype(np.float32)[:, None] * inv, (t % GRID).astype(np.float32)[:, None] * inv], -1)
    c = {"cos": np.ascontiguousarray(np.cos(ang).T), "sin": np.ascontiguousarray(np.sin(ang).T)}
    c["ident"] = np.eye(P, dtype=np.float32)
    c["dist"] = (np.arange(NLAT + 3 * P)[None, :] - np.arange(P)[:, None] - 3 * P).astype(np.float32)
    mask = np.full((P, 3, BAND), NEG, np.float32)
    for v, n in enumerate((0, 1, 3)):
        for q in range(P):
            qc = n * QB + q % QB
            start = min(max(qc - WIN // 2, 0), GRID - WIN)
            for j in range(BAND):
                if start <= BAND0[n] + j < start + WIN:
                    mask[q, v, j] = 0.0
    c["na_mask"] = mask
    i = np.arange(1023)
    c["hot_w"] = _one_hot(511 - i, (511 - i >= 0) & (511 - i <= 128), 1024)
    i = np.arange(255)
    d = 127 - i
    c["hot_d4"] = _one_hot(4 * d, d >= 0, 256)
    c["hot_d16"] = _one_hot(4 * d, (d >= 0) & (d % 4 == 0), 256)
    i = np.arange(639)
    c["hot_c"] = _one_hot(511 - i, 511 - i >= 0, 640)
    return {k: np.ascontiguousarray(v.astype(np.float32)) for k, v in c.items()}


def kernel(**inputs):
    import concourse.bacc as bacc
    from concourse.bass_utils import run_bass_kernel_spmd

    f = {k: np.asarray(v) for k, v in inputs.items()}
    wts = {"ret_in": _blocks(f["ret_w_in"]), "na_qkv": _blocks(f["na_w_qkv"]), "na_out": _blocks(f["na_w_out"]),
           "in_2": _blocks(f["w_in_2"][0]), "out_2": _blocks(f["w_out_2"][0]),
           "p_a": _blocks(f["p_a_2"][0]), "p_b": _blocks(f["p_b_2"][0]), "p_c": _blocks(f["p_c_2"][0]),
           "w13_0": _blocks(f["ffn_w13"][0]), "w13_1": _blocks(f["ffn_w13"][1]), "w13_2": _blocks(f["w_gu_2"][0]),
           "ret_out": np.stack([_blocks(f["ret_w_out"][RET_DV * h:RET_DV * (h + 1)]) for h in range(RET_HEADS)]),
           "ada_0": _blocks(f["ada_w"][0]), "ada_1": _blocks(f["ada_w"][1])}
    for n, w2 in enumerate((f["ffn_w2"][0], f["ffn_w2"][1], f["w_down_2"][0])):
        for c, (f0, k) in enumerate(FF_CHUNKS):
            wts[f"w2_{n}_{c}"] = _blocks(w2[P * f0:P * (f0 + k)])
    cond = np.stack([f["c"][0], f["c_ctx"]], -1).reshape(KD, P, 2).transpose(1, 0, 2).reshape(P, 2 * KD)
    vec = np.concatenate([
        _cols(f["ada_b"]), _cols(f["ln_g"]), _cols(f["ln_b"]), _cols(f["g_mix_2"]), _cols(f["g_ffn_2"]),
        _cols(f["g_final_2"]), f["conv_w_2"][0].reshape(4, LRU_TILES, P).transpose(2, 1, 0).reshape(P, 16),
        _cols(f["conv_b_2"]), _cols(f["lru_ba_2"]), _cols(f["lru_bx_2"]), _cols(f["lru_lam_2"]), cond,
        np.broadcast_to(f["ret_decay"].reshape(1, 8), (P, 8))], 1)
    acts = dict(_constants())
    acts["vec"] = np.ascontiguousarray(vec)
    acts["x"] = np.ascontiguousarray(f["x"][0].T.reshape(KD, P, NLAT).transpose(1, 0, 2))
    acts["ctx"] = np.ascontiguousarray(f["ctx"][0].T.reshape(KD, P, NCTX).transpose(1, 0, 2))
    acts["rpb"] = np.ascontiguousarray(f["na_rpb"].reshape(NA_HEADS * RPB_ROWS // 2, 2, RPB_COLS))
    acts["table"] = np.concatenate([f["rel_bias_2"], np.full((1, 20), NEG, np.float32)], 0)
    for n in ("lru_wa", "lru_wx"):
        acts[n] = np.ascontiguousarray(f[n + "_2"][0].reshape(LRU_TILES, 2, 64, 64).transpose(1, 2, 0, 3))
    wts["dist"] = acts.pop("dist")

    nc = bacc.Bacc("TRN2", target_bir_lowering=False, num_devices=1)
    arrays, aps = {}, ({}, {})
    for which, group in enumerate((acts, wts)):
        for name, array in group.items():
            arrays[f"in_{name}"] = array
            aps[which][name] = nc.dram_tensor(f"in_{name}", list(array.shape), mybir.dt.from_np(array.dtype),
                                              kind="ExternalInput").ap()
    out = nc.dram_tensor("out_t", [P, KD, NLAT], F32, kind="ExternalOutput")
    program(nc, aps[0], aps[1], out.ap())
    result = run_bass_kernel_spmd(nc, [arrays], core_ids=[0]).results[0]["out_t"]
    return np.ascontiguousarray(result.transpose(2, 1, 0).reshape(1, NLAT, D))
```

```python
from collections import deque
from contextlib import ExitStack

import numpy as np
import concourse.bass as bass
from concourse import mybir
from concourse.alu_op_type import AluOpType as ALU

F32 = mybir.dt.float32
F32R = mybir.dt.float32r
ACT = mybir.ActivationFunctionType
AX = mybir.AxisListType.X

P = 128
D = 1024
KD = D // P
NCTX, NLAT = 256, 512
NTOK = NCTX + NLAT
CTX, LAT = 0, 1
TOKENS = {CTX: NCTX, LAT: NLAT}
START = {CTX: 0, LAT: NCTX}
BOTH, ONLY_LAT = (CTX, LAT), (LAT,)
FF = -(-8 * D // (3 * 256)) * 256
KF = FF // P
KMAX = 8
FF_CHUNKS = [(a, min(KMAX, KF - a)) for a in range(0, KF, KMAX)]
ALPHA = 4 ** 0.25
LN_EPS, RMS_EPS = 1e-5, 1e-6
NEG = -1e30
GRID = 64
ROWS = NLAT // GRID
RET_HEADS, RET_DK, RET_DV = 4, 256, 512
NA_HEADS, HEAD = 16, 64
QB, BAND, WIN = 16, 32, 16
BAND0 = [int(v) for v in np.clip(np.arange(GRID // QB) * QB - WIN // 2, 0, GRID - BAND)]
RPB_ROWS, RPB_COLS, RPB_WIDE = 15, 31, 64
REL = QB + BAND
GROUP_HEADS, DIL_GROUPS, MOBA_HEADS = 4, 3, 8
LRU_TILES = 4
ADA_REST, ADA_ALL = (2, 3, 4, 5), (0, 1, 2, 3, 4, 5)

VECS = {}


def _vec(name, n):
    VECS[name] = (sum(k for _, k in VECS.values()), n)


for _name, _n in (("ada_b", 2 * 48), ("ln_g", 4 * KD), ("ln_b", 4 * KD), ("g_mix", KD), ("g_ffn", KD),
                  ("g_final", KD), ("conv_w", 4 * LRU_TILES), ("conv_b", LRU_TILES), ("lru_ba", LRU_TILES),
                  ("lru_bx", LRU_TILES), ("lru_lam", LRU_TILES), ("decay", 8)):
    _vec(_name, _n)
NVEC = sum(k for _, k in VECS.values())


class Queue:

    def __init__(self, engine, sem):
        self.engine, self.sem, self.count, self.met = engine, sem, 0, {}

    def wait(self, tokens):
        for t in tokens:
            if t is None:
                continue
            if isinstance(t, list):
                self.wait(t)
                continue
            sem, value = t
            if self.met.get(id(sem), 0) < value:
                self.met[id(sem)] = value
                self.engine.wait_ge(sem, value)

    def put(self, build, *after):
        self.wait(after)
        self.count += 1
        build().then_inc(self.sem, 1)
        return self.sem, self.count

    def quiet(self, build, *after):
        self.wait(after)
        build()

    def dma(self, out, in_, slot, *after):
        self.wait(after)
        slot[1] += 16
        self.engine.dma_start(out, in_).then_inc(slot[0], 16)
        return slot[0], slot[1]


class Ring:

    def __init__(self, slots):
        self.slots, self.free, self.at = slots, [[] for _ in slots], 0

    def take(self):
        i = self.at % len(self.slots)
        assert self.free[i] is not None, "slot still in use"
        after, self.free[i] = self.free[i], None
        self.at += 1
        return i, self.slots[i], after

    def give(self, i, *tokens):
        self.free[i] = list(tokens)


class Block:

    def __init__(self, dram, key=None):
        self.dram, self.tiles, self.key = dram, dram.shape[-1] // P, key


def weight_plan(w):
    plan, trickle = [], deque()

    def start_trickle(layer, chunks):
        trickle.extend(Block(w[f"ada_{layer}"][b], (layer, b)) for c in chunks for b in range(KD * c, KD * c + KD))

    def end_trickle():
        while trickle:
            plan.append(trickle.popleft())

    def add(name, *index):
        block = w[name]
        for i in index:
            block = block[i]
        plan.append(Block(block))
        if trickle:
            plan.append(trickle.popleft())

    def ffn(name13, name2):
        for c, (f0, n) in enumerate(FF_CHUNKS):
            for f in range(f0, f0 + n):
                add(name13, f)
                add(name13, KF + f)
            for o in range(KD):
                add(f"{name2}_{c}", o)

    def ret_out(h):
        for o in range(KD):
            add("ret_out", h, o)

    for b in range(KD):
        plan.append(Block(w["ada_0"][b], (0, b)))
        plan.append(Block(w["ada_scale_0"][b], ("scale", b)))
    start_trickle(0, ADA_REST)
    for h in range(RET_HEADS):
        for b in (2 * h, 2 * h + 1, 8 + 2 * h, 9 + 2 * h):
            add("ret_in", b)
        if h:
            ret_out(h - 1)
        for b in range(4):
            add("ret_in", 16 + 4 * h + b)
        for b in range(4):
            add("ret_in", 32 + 4 * h + b)
    ret_out(RET_HEADS - 1)
    end_trickle()
    start_trickle(1, ADA_ALL)
    ffn("w13_0", "w2_0")
    end_trickle()
    for pair in range(NA_HEADS // 2):
        for b in (pair, KD + pair, 2 * KD + pair):
            add("na_qkv", b)
    for o in range(KD):
        add("na_out", o)
    ffn("w13_1", "w2_1")
    for jp in range(2):
        for part in range(3):
            for g in range(DIL_GROUPS):
                add("in_2", 6 * part + 2 * g + jp)
        if jp == 0:
            for t in range(LRU_TILES):
                add("in_2", 18 + t)
                add("in_2", 22 + t)
    for pair in range(MOBA_HEADS // 2):
        for part in range(3):
            add("in_2", 26 + 4 * part + pair)
    for o in range(KD):
        for branch, name in enumerate(("p_a", "p_b", "p_c")):
            add("in_2", 38 + KD * branch + o)
            add(name, o)
    for o in range(KD):
        add("out_2", o)
    ffn("w13_2", "w2_2")
    return plan


def program(nc, a, w, out):
    stack = ExitStack()
    sems = []

    def sem(name):
        s = stack.enter_context(nc.semaphore(name))
        sems.append(s)
        return s

    def dma_slot(name):
        return [sem(name), 0]

    pe, act, dve, pool, sp = (Queue(engine, sem(f"done_{name}")) for name, engine in (
        ("pe", nc.tensor), ("act", nc.scalar), ("dve", nc.vector), ("pool", nc.gpsimd), ("sp", nc.sync)))
    V, S, G, T = nc.vector, nc.scalar, nc.gpsimd, nc.tensor

    class Map:
        def __init__(self, start, end):
            self.at, self.end = start, end

        def sb(self, name, shape, dt=F32):
            size = int(np.prod(shape[1:])) * mybir.dt.size(dt)
            at = (self.at + 31) // 32 * 32
            assert at + size <= self.end, f"{name}: {at + size} > {self.end}"
            self.at = at + size
            return nc.alloc_sbuf_tensor_at(name, list(shape), dt, offset=at)

    keep = Map((nc.sbuf_base + 31) // 32 * 32, nc.sbuf_usable_end)
    h_lat = keep.sb("h_lat", [P, KD, NLAT])
    x_lat = [keep.sb(f"x_lat_{s}", [P, KD, NLAT], F32R) for s in ("hi", "lo")]
    ctx_start = keep.at
    h_ctx = keep.sb("h_ctx", [P, KD, NCTX])
    x_ctx = [keep.sb(f"x_ctx_{s}", [P, KD, NCTX], F32R) for s in ("hi", "lo")]
    ctx_end = keep.at
    NRAW, NSPLIT, AHEAD = 3, 3, 2
    w_raw = keep.sb("w_raw", [P, NRAW, KMAX * P])
    w_hi = keep.sb("w_hi", [P, NSPLIT, KMAX * P], F32R)
    w_lo = keep.sb("w_lo", [P, NSPLIT, KMAX * P], F32R)
    TMPS = 2
    tmp = keep.sb("tmp", [P, TMPS, NLAT])
    total = {g: keep.sb(f"total{g}", [P, TOKENS[g]])[:, :] for g in BOTH}
    norm_vec = keep.sb("norm_vec", [P, 6, KD])
    ones_mean = keep.sb("ones_mean", [P, P])
    ident = keep.sb("ident", [P, P])
    vec = keep.sb("vec", [P, NVEC])
    cond = keep.sb("cond", [P, 2 * D])
    cond_cols = keep.sb("cond_cols", [P, KD, 2])
    dot_out = keep.sb("dot_out", [P, D], mybir.dt.bfloat16)
    mod = [keep.sb(f"mod_{l}", [P, 48, 2]) for l in range(2)]
    table = keep.sb("rel_table", [33, 20])
    log_gamma = keep.sb("log_gamma", [P, 8])
    small = keep.sb("small", [P, 96])

    banks = [stack.enter_context(nc.psum_tensor(f"bank{i}", [P, 512], F32)) for i in range(8)]
    lin = Ring(banks[0:4])
    att = Ring(banks[4:7])
    last = Ring(banks[7:8])

    def vc(name, i=0, n=1):
        c = VECS[name][0] + i
        return vec[:, c:c + n]

    def fence():
        return [(q.sem, q.count) for q in (pe, act, dve, pool) if q.count]

    cond_sem, cond_cols_sem, const_sem, *x_sem = (dma_slot(f"loaded_{n}") for n in ("cond", "cond_cols", "constants", "x_ctx", "x_lat"))
    cond_loaded = sp.dma(cond[:, :], a["cond"].partition_broadcast(P), cond_sem)
    cond_cols_loaded = act.dma(cond_cols[:, :, :], a["cond_cols"], cond_cols_sem)
    for dst, src in ((vec[:, :], a["vec"]), (ident[:, :], a["ident"])):
        consts = act.dma(dst, src, const_sem)
    x_loads = {10: (LAT, h_lat, a["x"]), 16: (CTX, h_ctx, a["ctx"])}
    ones_set = pool.put(lambda: G.memset(ones_mean[:, :], 1.0 / D))
    eps_col = {}
    for i, e in enumerate((LN_EPS, RMS_EPS)):
        eps_col[e] = small[:, i:i + 1]
        eps_set = pool.put(lambda: G.memset(eps_col[e], e))

    plan = weight_plan(w)
    h_ready = {}
    raw_sem = [dma_slot(f"loaded_w{i}") for i in range(NRAW)]
    raw_free = [[] for _ in range(NRAW)]
    raw_token, split_token, split_free = {}, {}, [[] for _ in range(NSPLIT)]
    state = {"fetched": 0, "used": 0, "split": 0, "taken": 0}
    tiles_of_split = []

    def fetch_next():
        i = state["fetched"]
        state["fetched"] += 1
        slot, block = i % NRAW, plan[i]
        if i in x_loads:
            g, dst, x = x_loads[i]
            h_ready.update({(k, g): [sp.dma(dst[:, k, :], x[:, k, :], x_sem[g])] for k in range(KD)})
        raw_token[i] = sp.dma(w_raw[:, slot, 0:block.tiles * P], block.dram, raw_sem[slot], raw_free[slot])

    def use_next():
        i = state["used"]
        state["used"] += 1
        while state["fetched"] < min(i + NRAW, len(plan)):
            fetch_next()
        raw, block = i % NRAW, plan[i]
        n = block.tiles * P
        src = w_raw[:, raw, 0:n]
        if block.key is not None and block.key[0] == "scale":
            raw_free[raw] = [first_scale_block(block.key[1], src, raw_token[i])]
            return
        if block.key is not None:
            raw_free[raw] = [modulation_block(*block.key, src, raw_token[i])]
            return
        j = state["split"]
        state["split"] += 1
        to = j % NSPLIT
        hi, lo = w_hi[:, to, 0:n], w_lo[:, to, 0:n]
        t_hi = act.put(lambda: S.activation(hi, src, ACT.Copy), raw_token[i], split_free[to])
        t_lo = dve.put(lambda: V.tensor_tensor(lo, src, hi.bitcast(F32), ALU.subtract), t_hi, split_free[to])
        raw_free[raw] = [t_lo]
        split_token[j] = t_lo
        tiles_of_split.append(block.tiles)

    def take_weights(kt):
        j = state["taken"]
        state["taken"] += 1
        while state["split"] <= j + AHEAD and state["used"] < len(plan):
            use_next()
        assert tiles_of_split[j] == kt, (j, tiles_of_split[j], kt)
        return j

    background = deque()

    def advance(works):
        while works:
            try:
                next(works[0])
                return
            except StopIteration:
                works.popleft()

    def tick(n=1):
        for _ in range(n):
            advance(background)

    def drain():
        while background:
            advance(background)

    class Split:

        def __init__(self, parts):
            self.parts, self.ready, self.read = parts, {}, []

        def ap(self, part, k, g):
            return self.parts[g][part][:, k, :]

    def linear(x, kt, groups, ticks=1):
        i = take_weights(kt)
        slot = i % NSPLIT
        taken = {g: lin.take() for g in groups}
        outs, done, steps = {}, 0, 0
        pe.wait([split_token[i]])
        for g in reversed(groups):
            index, bank, after = taken[g]
            o = bank[:, 0:TOKENS[g]]
            pe.wait([after])
            for k in range(kt):
                hi, lo = (t[:, slot, k * P:(k + 1) * P] for t in (w_hi, w_lo))
                pe.wait([x.ready[k, g]])
                pe.quiet(lambda: T.matmul(o, hi, x.ap(0, k, g), start=k == 0, stop=False))
                pe.quiet(lambda: T.matmul(o, hi, x.ap(1, k, g), start=False, stop=False))
                low = lambda: T.matmul(o, lo, x.ap(0, k, g), start=False, stop=k == kt - 1)
                if k < kt - 1:
                    pe.quiet(low)
                else:
                    token = pe.put(low)
                steps += 1
                while done < ticks * steps // (kt * len(groups)) and steps < kt * len(groups):
                    advance(background)
                    done += 1
            outs[g] = (index, o, token)
        split_free[slot] = [token]
        x.read = [token]
        tick(ticks - done)
        return [outs[g] for g in groups]

    tmp_ring = Ring([tmp[:, i, :] for i in range(TMPS)])

    def put_split(x, k, g, src, ready, cols=slice(None), view=None, src_view=None):
        hi, lo = x.ap(0, k, g), x.ap(1, k, g)
        if view is not None:
            hi, lo = view(hi), view(lo)
        t_hi = act.put(lambda: S.activation(hi, src, ACT.Copy), ready, x.read)
        t_lo = dve.put(lambda: V.tensor_tensor(lo, src, hi.bitcast(F32), ALU.subtract), t_hi, x.read)
        x.ready.setdefault((k, g), [])
        x.ready[k, g] = x.ready[k, g] + [t_lo]
        return [t_hi, t_lo]

    silu_cols = act.put(lambda: S.activation(cond_cols[:, :, :], cond_cols[:, :, :], ACT.Silu), cond_cols_loaded)
    silu_cond = act.put(lambda: S.activation(cond[:, :], cond[:, :], ACT.Silu), cond_loaded)
    mod_ready = {}

    def modulation_block(layer, b, weights, loaded):
        c = b // KD
        for g in range(2):
            t = dve.put(lambda: V.tensor_tensor_reduce(
                out=dot_out[:, :], in0=weights, in1=cond[:, g * D:(g + 1) * D], scale=1.0, scalar=0.0,
                op0=ALU.mult, op1=ALU.add, accum_out=mod[layer][:, b, g:g + 1]), loaded, silu_cond,
                state.get("dot"))
            state["dot"] = [t]
        if b % KD == KD - 1:
            finish_chunk(layer, c, mod[layer][:, KD * c:KD * c + KD, :], t)
        return t

    def finish_chunk(layer, c, src, t):
        dst = mod[layer][:, KD * c:KD * c + KD, :]
        bias = vc("ada_b", 48 * layer + KD * c, KD).unsqueeze(2).to_broadcast([P, KD, 2])
        done = dve.put(lambda: V.tensor_tensor(dst, src, bias, ALU.add), t, consts)
        if c in (1, 4):
            done = dve.put(lambda: V.tensor_scalar(dst, dst, 1.0, None, ALU.add), done)
        mod_ready[layer, c] = done
        return done

    scale_bank = {}

    def first_scale_block(b, weights, loaded):
        if b == 0:
            scale_bank["at"], scale_bank["bank"], scale_bank["free"] = att.take()
        bank = scale_bank["bank"]
        pe.wait([loaded, silu_cols, scale_bank["free"]])
        for k in range(KD):
            call = lambda: T.matmul(bank[:, 2 * b:2 * b + 2], weights[:, k * P:(k + 1) * P], cond_cols[:, k, :],
                                    start=k == 0, stop=k == KD - 1)
            if k < KD - 1:
                pe.quiet(call)
            else:
                t = pe.put(call)
        if b == KD - 1:
            att.give(scale_bank["at"], finish_chunk(0, 1, bank[:, 0:2 * KD].rearrange("p (k g) -> p k g", g=2), t))
        return t

    def need_mod(layer, c):
        while (layer, c) not in mod_ready:
            use_next()
        return mod_ready[layer, c]

    def mod_col(layer, c, k, g):
        j = 0 if g == LAT else 1
        return mod[layer][:, 8 * c + k, j:j + 1]

    PHASE, END = keep.at, keep.end // 32 * 32
    H = {CTX: h_ctx, LAT: h_lat}
    X = Split({CTX: x_ctx, LAT: x_lat})

    def to_x(k, g, src, t):
        X.ready[k, g] = []
        return put_split(X, k, g, src, t)

    def one_apart(n, begin, end):
        begun = begin(0)
        for k in range(n):
            after = begin(k + 1) if k + 1 < n else None
            end(k, begun)
            begun = after

    def modulate(layer, c, groups):
        shift, scale = need_mod(layer, c), need_mod(layer, c + 1)
        for g in groups:
            def begin(k):
                ti, t_ap, after = tmp_ring.take()
                x, h = t_ap[:, 0:TOKENS[g]], H[g][:, k, :]
                t = dve.put(lambda: V.tensor_scalar(x, h, mod_col(layer, c + 1, k, g), mod_col(layer, c, k, g),
                                                    ALU.mult, ALU.add), after, h_ready[k, g], shift, scale)
                h_ready[k, g] = [pool.put(lambda: G.tensor_scalar(h, h, ALPHA, 1.0, ALU.mult, ALU.mult), t)]
                return ti, x, t

            def end(k, begun):
                ti, x, t = begun
                tmp_ring.give(ti, *to_x(k, g, x, t))

            one_apart(KD, begin, end)

    def add_gated(layer, c, o, groups, outs, sum_up=False):
        gate_ready = need_mod(layer, c)
        for (i, bank, t), g in zip(outs, groups):
            h = H[g][:, o, :]
            t2 = dve.put(lambda: V.scalar_tensor_tensor(h, bank, mod_col(layer, c, o, g), h, ALU.mult, ALU.add),
                         t, h_ready[o, g], gate_ready)
            h_ready[o, g] = [t2]
            lin.give(i, t2)
            if sum_up and o:
                before = H[g][:, 0, :] if o == 1 else total[g]
                total_ready[g] = [pool.put(lambda: G.tensor_tensor(total[g], before, h, ALU.add), t2, total_ready[g])]

    total_ready = {g: [] for g in BOTH}

    def open_sums(g):
        i, bank, free = att.take()
        return dict(i=i, bank=bank[:, 0:TOKENS[g]], free=free, g=g)

    def add_squares(sums, k, src, ready, last_k, later=False):
        close_sums(sums)
        ti, t_ap, after = tmp_ring.take()
        sq = t_ap[:, 0:TOKENS[sums["g"]]]
        t = act.put(lambda: S.activation(sq, src, ACT.Square), ready, after)

        def product():
            sums["token"] = pe.put(lambda: T.matmul(sums["bank"], ones_mean[:, :], sq, start=k == 0, stop=k == last_k),
                                   t, sums["free"], ones_set)
            tmp_ring.give(ti, sums["token"])

        sums["pending"] = product
        if not later:
            close_sums(sums)

    def close_sums(sums):
        if sums.get("pending"):
            sums.pop("pending")()

    def rstd_rows(sums, scale, eps, rows, rows_free):
        close_sums(sums)
        t = act.put(lambda: S.activation(rows, sums["bank"], ACT.Sqrt, bias=eps, scale=scale), sums["token"], rows_free, eps_set)
        att.give(sums["i"], t)
        return dve.put(lambda: V.reciprocal(rows, rows), t)

    norm_vec_used = [[]]

    def layer_norm(which, groups, layer=None, c=None):
        gain, shift_ln = vc("ln_g", which * KD, KD), vc("ln_b", which * KD, KD)
        vec_ready = consts
        if layer is not None:
            shift, scale = need_mod(layer, c), need_mod(layer, c + 1)
            for x, src in ((4, gain), (5, shift_ln)):
                vec_ready = dve.put(lambda: V.tensor_scalar(norm_vec[:, x, :], src, ALPHA, None, ALU.mult), norm_vec_used[0])
            for g in groups:
                col = 0 if g == LAT else 1
                a_, b_ = (mod[layer][:, KD * (c + x):KD * (c + x + 1), col] for x in (1, 0))
                G_, B_ = norm_vec[:, 2 * g, :], norm_vec[:, 2 * g + 1, :]
                dve.put(lambda: V.tensor_tensor(G_, gain, a_, ALU.mult), scale, norm_vec_used[0])
                t = dve.put(lambda: V.tensor_tensor(B_, shift_ln, a_, ALU.mult), scale, norm_vec_used[0])
                vec_ready = dve.put(lambda: V.tensor_tensor(B_, B_, b_, ALU.add), t, shift)
        stats = {}
        for g in reversed(groups):
            n = TOKENS[g]
            i, bank, free = att.take()
            t = pe.put(lambda: T.matmul(bank[:, 0:n], ones_mean[:, :], total[g], start=True, stop=True),
                       free, ones_set, total_ready[g])
            stats[g] = sums = open_sums(g)
            for k in range(KD):
                h = H[g][:, k, :]
                t_c = dve.put(lambda: V.tensor_tensor(h, h, bank[:, 0:n], ALU.subtract), t, h_ready[k, g])
                add_squares(sums, k, h, t_c, KD - 1)
            att.give(i, t_c)
            sums["mean_read"] = t
        for g in reversed(groups):
            n, sums, rows = TOKENS[g], stats[g], total[g]
            t_rows = rstd_rows(sums, 1.0, eps_col[LN_EPS], rows, sums["mean_read"])

            def begin(k):
                h = H[g][:, k, :]
                t_n = dve.put(lambda: V.tensor_tensor(h, h, rows, ALU.mult), t_rows)
                total_ready[g] = [t_n]
                if layer is None:
                    h_ready[k, g] = [pool.put(lambda: G.tensor_scalar(h, h, gain[:, k:k + 1], shift_ln[:, k:k + 1],
                                                                      ALU.mult, ALU.add), t_n)]
                    return
                ti, t_ap, after = tmp_ring.take()
                x = t_ap[:, 0:n]
                t_x = act.put(lambda: S.activation(x, h, ACT.Identity, bias=norm_vec[:, 2 * g + 1, k:k + 1],
                                                   scale=norm_vec[:, 2 * g, k:k + 1]), t_n, after, vec_ready)
                h_ready[k, g] = [pool.put(lambda: G.tensor_scalar(h, h, norm_vec[:, 4, k:k + 1], norm_vec[:, 5, k:k + 1],
                                                                  ALU.mult, ALU.add), t_x, vec_ready)]
                norm_vec_used[0] = [t_x, h_ready[k, g]]
                return ti, x, t_x

            def end(k, begun):
                if begun:
                    ti, x, t_x = begun
                    tmp_ring.give(ti, *to_x(k, g, x, t_x))

            one_apart(KD, begin, end)

    def rms_norm(sums, gain, finish):
        rows = total[LAT]
        t_rows = rstd_rows(sums, 1.0, eps_col[RMS_EPS], rows, total_ready[LAT])

        def begin(k):
            ti, t_ap, free = tmp_ring.take()
            x = t_ap[:, 0:NLAT]
            t = dve.put(lambda: V.scalar_tensor_tensor(x, H[LAT][:, k, :], vc(gain, k), rows, ALU.mult, ALU.mult),
                        t_rows, free, h_ready[k, LAT])
            total_ready[LAT] = [t]
            return ti, x, t

        def end(k, begun):
            ti, x, t = begun
            tmp_ring.give(ti, *finish(k, x, t))

        one_apart(KD, begin, end)

    def ffn(name, groups, prev, add):
        m = Map(PHASE, END)
        hid = Split({g: [m.sb(f"{name}_hid{g}{s}", [P, KMAX, TOKENS[g]], F32R) for s in ("hi", "lo")] for g in groups})
        silu = Ring([m.sb(f"{name}_silu{i}", [P, NTOK]) for i in range(2)])
        hid.read = prev
        silu.free = [prev, prev]
        for f0, nf in FF_CHUNKS:
            for j in range(nf):
                si, s_ap, free = silu.take()
                t_silu = {}
                for (i, bank, t), g in zip(linear(X, KD, groups), groups):
                    cols = slice(START[g], START[g] + TOKENS[g])
                    t_silu[g] = act.put(lambda bank=bank, cols=cols, s_ap=s_ap: S.activation(s_ap[:, cols], bank, ACT.Silu), t, free)
                    lin.give(i, t_silu[g])
                ended = []
                for (i, bank, t), g in zip(linear(X, KD, groups), groups):
                    cols = slice(START[g], START[g] + TOKENS[g])
                    t2 = dve.put(lambda bank=bank, cols=cols, s_ap=s_ap: V.tensor_tensor(s_ap[:, cols], bank, s_ap[:, cols], ALU.mult), t, t_silu[g])
                    lin.give(i, t2)
                    hid.ready[j, g] = []
                    ended += put_split(hid, j, g, s_ap[:, cols], t2)
                silu.give(si, *ended)
            for o in range(KD):
                add(o, linear(hid, nf, groups), f0 + nf == KF)

    m = Map(PHASE, END)
    ret_q = m.sb("ret_q", [P, 2, NTOK])
    ret_k = m.sb("ret_k", [P, 2, NTOK])
    ret_vt = m.sb("ret_vt", [P, NTOK])
    ret_v = m.sb("ret_v", [P, NTOK // P, RET_DV])
    y_hi = {g: m.sb(f"ret_y_hi{g}", [P, 4, TOKENS[g]], F32R) for g in BOTH}
    y_at = m.at
    y_lo = {g: m.sb(f"ret_y_lo{g}", [P, 4, TOKENS[g]], F32R) for g in BOTH}
    over = Map(y_at, m.at)
    gate = {g: over.sb(f"ret_gate{g}", [P, 4, TOKENS[g]]) for g in BOTH}
    scores = m.sb("ret_scores", [P, NTOK // P, NLAT])
    scores_ctx = m.sb("ret_scores_ctx", [P, NCTX // P, NCTX])
    WIDE = NLAT + 3 * P
    near = m.sb("ret_near", [P, WIDE])
    far = m.sb("ret_far", [P, NLAT + P])
    rope = [m.sb(f"ret_{n}", [P, NLAT]) for n in ("cos", "sin")]
    ret_sq = m.sb("ret_sq", [P, NLAT])
    ret_u = m.sb("ret_u", [P, NLAT])
    rope_sem = dma_slot("loaded_rope")
    for dst, src in zip(rope, (a["cos"], a["sin"])):
        rope_loaded = pool.dma(dst[:, :], src, rope_sem)
    dist_sem = dma_slot("loaded_dist")

    t = act.put(lambda: S.activation(log_gamma[:, :], vc("decay", 0, 8), ACT.Exp), consts)
    lg_ready = dve.put(lambda: V.tensor_scalar(log_gamma[:, :], log_gamma[:, :], -1.0, None, ALU.mult), t)
    neg_lg, far_bias = small[:, 32:40], small[:, 40:48]
    t = dve.put(lambda: V.tensor_scalar(neg_lg, log_gamma[:, :], -1.0, None, ALU.mult), lg_ready)
    t = dve.put(lambda: V.tensor_scalar(far_bias[:, 0:4], log_gamma[:, 0:4], 512.0, None, ALU.mult), lg_ready)
    lg_ready = dve.put(lambda: V.tensor_scalar(far_bias[:, 4:8], log_gamma[:, 4:8], 256.0, None, ALU.mult), lg_ready)

    near_ready, near_used = [None], [None]

    def decay_tables(h):
        near_ready[0] = []
        half = WIDE // 2
        for c0 in (0, half):
            i0, d_ap, f0 = tmp_ring.take()
            i1, e_ap, f1 = tmp_ring.take()
            d, e1, e2 = d_ap[:, 0:half], e_ap[:, 0:half], near[:, c0:c0 + half]
            t0 = pool.dma(d, w["dist"][:, c0:c0 + half], dist_sem, f0)
            yield
            t = dve.put(lambda: V.tensor_scalar(e1, d, 0.0, None, ALU.max), t0, f1)
            t = act.put(lambda: S.activation(e1, e1, ACT.Exp, scale=log_gamma[:, h:h + 1]), t, lg_ready)
            t_f = pool.put(lambda: G.affine_select(out=e1, in_=e1, compare_op=ALU.is_ge, fill=0.0,
                                                   base=c0 - 3 * P, pattern=[[1, half]], channel_multiplier=-1), t)
            t = dve.put(lambda: V.tensor_scalar(e2, d, 0.0, None, ALU.min), t0, near_used[0])
            t = act.put(lambda: S.activation(e2, e2, ACT.Exp, scale=neg_lg[:, 4 + h:5 + h]), t, lg_ready)
            t_b = pool.put(lambda: G.affine_select(out=e2, in_=e2, compare_op=ALU.is_ge, fill=0.0,
                                                   base=3 * P - c0, pattern=[[-1, half]], channel_multiplier=1), t)
            n = min(half, NLAT + P - c0)
            fo = far[:, c0:c0 + n]
            t_fo = act.put(lambda: S.activation(fo, d[:, 0:n], ACT.Exp, bias=far_bias[:, h:h + 1],
                                                scale=log_gamma[:, h:h + 1]), t0, lg_ready, near_used[0])
            yield
            t_n = dve.put(lambda: V.tensor_tensor(e2, e2, e1, ALU.add), t_f, t_b)
            t_e = act.put(lambda: S.activation(e1[:, 0:n], d[:, 0:n], ACT.Exp, bias=far_bias[:, 4 + h:5 + h],
                                               scale=neg_lg[:, 4 + h:5 + h]), t_n)
            yield
            t_far = dve.put(lambda: V.tensor_tensor(fo, fo, e1[:, 0:n], ALU.add), t_fo, t_e)
            near_ready[0] += [t_n, t_far]
            tmp_ring.give(i0, t_e)
            tmp_ring.give(i1, t_far)

    for _ in decay_tables(0):
        pass
    need_mod(0, 0), need_mod(0, 1)
    for g in (LAT, CTX):
        use_next()
        modulate(0, 0, (g,))

    ret = {"q": {}, "k": {}, "v": [], "gate": {}, "s_read": [], "qk_read": [], "v_read": [], "y_read": [],
           "s_ready": {}, "vt_read": [], "sq_read": []}
    Y = Split({g: [y_hi[g], y_lo[g]] for g in BOTH})

    def ret_project_qk(h):
        for name, dst in (("q", ret_q), ("k", ret_k)):
            for half in range(2):
                outs = linear(X, KD, BOTH, 5)
                i, bank, t = outs[0]
                ret[name][half, CTX] = [act.put(lambda bank=bank, half=half, dst=dst: S.activation(
                    dst[:, half, 0:NCTX], bank, ACT.Copy), t, ret["qk_read"])]
                lin.give(i, *ret[name][half, CTX])
                i, bank, t = outs[1]
                lat = slice(NCTX, NTOK)
                if half == 0:
                    t1 = act.put(lambda bank=bank, dst=dst: S.activation(dst[:, 0, lat], bank, ACT.Copy), t, ret["qk_read"])
                    lin.give(i, t1)
                    continue
                i0, t_ap, free = tmp_ring.take()
                i1, u_ap, free1 = tmp_ring.take()
                x1, x2, p1, p2 = dst[:, 0, lat], dst[:, 1, lat], t_ap[:, 0:NLAT], u_ap[:, 0:NLAT]
                ta = dve.put(lambda bank=bank, p1=p1: V.tensor_tensor(p1, bank, rope[1][:, :], ALU.mult), t, free, rope_loaded)
                tb = dve.put(lambda bank=bank, x2=x2: V.tensor_tensor(x2, bank, rope[0][:, :], ALU.mult), t, ret["qk_read"])
                lin.give(i, tb)
                tc = pool.put(lambda x1=x1, p2=p2: G.tensor_tensor(p2, x1, rope[1][:, :], ALU.mult), t1, free1, rope_loaded)
                td = pool.put(lambda x1=x1: G.tensor_tensor(x1, x1, rope[0][:, :], ALU.mult), tc)
                te = dve.put(lambda x2=x2, p2=p2: V.tensor_tensor(x2, x2, p2, ALU.add), tb, tc)
                tf = dve.put(lambda x1=x1, p1=p1: V.tensor_tensor(x1, x1, p1, ALU.subtract), td, ta)
                tmp_ring.give(i0, tf)
                tmp_ring.give(i1, te)
                ret[name][0, LAT], ret[name][1, LAT] = [tf], [te]

    def ret_v_tiles(j, ts):
        ret["vt_read"] = []
        for s0, ns in ((2, 4), (0, 2)):
            i, bank, free = att.take()
            for s in range(ns):
                cols = slice((s0 + s) * P, (s0 + s + 1) * P)
                t = pe.put(lambda: T.transpose(bank[:, s * P:(s + 1) * P], ret_vt[:, cols], ident[:, :]), ts, free, consts)
            t2 = dve.put(lambda: V.tensor_copy(
                ret_v[:, s0:s0 + ns, j * P:(j + 1) * P], bank[:, 0:ns * P].rearrange("p (s c) -> p s c", c=P)), t, ret["v_read"])
            att.give(i, t2)
            ret["vt_read"].append(t)
            ret["v"].append(t2)
            if s0:
                yield

    def ret_project_vg(h):
        ret["v"] = []
        for j in range(4):
            outs = linear(X, KD, BOTH, 3)
            ts = []
            for (i, bank, t), g in zip(outs, BOTH):
                cols = slice(START[g], START[g] + TOKENS[g])
                ts.append(act.put(lambda bank=bank, cols=cols: S.activation(ret_vt[:, cols], bank, ACT.Copy), t, ret["vt_read"]))
                lin.give(i, ts[-1])
            background.appendleft(ret_v_tiles(j, ts))
        for j in range(4):
            outs = linear(X, KD, BOTH, 3)
            for (i, bank, t), g in zip(outs, BOTH):
                t2 = act.put(lambda bank=bank, g=g, j=j: S.activation(gate[g][:, j, :], bank, ACT.Silu), t, ret["y_read"])
                lin.give(i, t2)
                ret["gate"][j, g] = t2

    def ret_scores():
        reads = []
        for s in range(NTOK // P):
            g_s = CTX if s < 2 else LAT
            for g_t in ((CTX, LAT) if s < 2 else (LAT,)):
                n = TOKENS[g_t]
                i, bank, free = att.take()
                tq = slice(START[g_t], START[g_t] + n)
                for half in range(2):
                    t = pe.put(lambda half=half, bank=bank, n=n, s=s, tq=tq: T.matmul(
                        bank[:, 0:n], ret_k[:, half, s * P:(s + 1) * P], ret_q[:, half, tq], start=half == 0, stop=half == 1),
                        free, ret["k"][half, g_s], ret["q"][half, g_t])
                if g_s == CTX and g_t == CTX:
                    dst, table = scores_ctx[:, s, :], near[:, 3 * P - s * P:3 * P - s * P + n]
                elif g_s == CTX:
                    dst, table = scores[:, s, :], far[:, P - s * P:P - s * P + n]
                else:
                    dst, table = scores[:, s, :], near[:, 3 * P - (s - 2) * P:3 * P - (s - 2) * P + n]
                t2 = dve.put(lambda bank=bank, n=n, dst=dst, table=table: V.scalar_tensor_tensor(
                    dst, bank[:, 0:n], RET_DK ** -0.5, table, ALU.mult, ALU.mult), t, near_ready[0], ret["s_read"])
                att.give(i, t2)
                ret["s_ready"][s, g_t] = t2
                near_used[0] = [t2]
                ret["qk_read"] = [t]
                yield

    def ret_readout():
        for g in (LAT, CTX):
            n = TOKENS[g]
            src = scores if g == LAT else scores_ctx
            nsrc = NTOK // P if g == LAT else NCTX // P
            o_ready = []
            sq, u = ret_sq[:, 0:n], ret_u[:, 0:n]
            for j in range(4):
                i, bank, free = att.take()
                for s in range(nsrc):
                    call = (lambda s=s, bank=bank, j=j: T.matmul(bank[:, 0:n], ret_v[:, s, j * P:(j + 1) * P], src[:, s, :],
                                                                 start=s == 0, stop=s == nsrc - 1))
                    t = pe.put(call, free, ret["v"], ret["s_ready"][s, g])
                if j == 0:
                    t_sq = act.put(lambda bank=bank: S.activation(sq, bank[:, 0:n], ACT.Square), t, ret["sq_read"])
                else:
                    tu = act.put(lambda bank=bank: S.activation(u, bank[:, 0:n], ACT.Square), t, t_sq)
                    t_sq = pool.put(lambda: G.tensor_tensor(sq, sq, u, ALU.add), tu)
                t_y = dve.put(lambda bank=bank, j=j: V.tensor_tensor(gate[g][:, j, :], bank[:, 0:n], gate[g][:, j, :], ALU.mult), t_sq if j == 0 else tu, ret["gate"][j, g])
                att.give(i, t_y)
                o_ready.append(t_y)
                ret["s_read"] = [t]
                ret["v_read"] = [t]
                yield
            sums = open_sums(g)
            sums["token"] = pe.put(lambda: T.matmul(sums["bank"], ones_mean[:, :], sq, start=True, stop=True),
                                   t_sq, sums["free"], ones_set)
            t = rstd_rows(sums, D / RET_DV, eps_col[RMS_EPS], sq, sums["token"])
            yield
            for j in range(4):
                t2 = dve.put(lambda: V.tensor_tensor(gate[g][:, j, :], gate[g][:, j, :], sq, ALU.mult), t, o_ready[j])
                Y.ready[j, g] = []
                put_split(Y, j, g, gate[g][:, j, :], t2)
            ret["sq_read"] = [t2]
            yield

    def ret_out(sum_up=False):
        for o in range(KD):
            add_gated(0, 2, o, BOTH, linear(Y, 4, BOTH), sum_up)
        ret["y_read"] = Y.read

    for h in range(RET_HEADS):
        ret_project_qk(h)
        drain()
        background.append(ret_scores())
        if h:
            ret_out()
        if h + 1 < RET_HEADS:
            background.append(decay_tables(h + 1))
        ret_project_vg(h)
        drain()
        background.append(ret_readout())
    drain()
    ret_out(True)

    prev = fence()
    layer_norm(0, BOTH, 0, 3)
    ffn("ffn0", BOTH, prev, lambda o, outs, end: add_gated(0, 5, o, BOTH, outs, end))
    layer_norm(1, BOTH, 1, 0)

    def attend(jobs, p_ring, pt_ring):
        def stage_scores(job):
            n_all = sum(s[0] for s in job["segs"])
            pi, p_full, p_free = p_ring.take()
            p = p_full[:, 0:n_all]
            col, written = 0, []
            for n, mms, bias, view, place in job["segs"]:
                i, bank, free = att.take()
                for x, (lhsT, rhs) in enumerate(mms):
                    t = pe.put(lambda lhsT=lhsT, rhs=rhs, bank=bank, n=n, view=view: T.matmul(
                        view(bank[:, 0:n]), lhsT, rhs, start=True, stop=True), free, job["ready"])
                dst = p[:, col:col + n]
                if bias is None:
                    t2 = act.put(lambda dst=dst, bank=bank, n=n: S.activation(dst, bank[:, 0:n], ACT.Copy), t, p_free)
                else:
                    t2 = dve.put(lambda: V.tensor_tensor(place(dst), view(bank[:, 0:n]), view(bias), ALU.add),
                                 t, p_free, job["bias_ready"])
                att.give(i, t2)
                written.append(t2)
                col += n
            job["scored"] = t
            job["bias_read"](written)
            neg, total, inv = (small[:, 48 + 3 * pi + x:49 + 3 * pi + x] for x in range(3))
            t = dve.put(lambda: V.tensor_reduce(neg, p, AX, ALU.max, negate=True), written)
            t = act.put(lambda: S.activation(p, p, ACT.Exp, bias=neg, accum_out=total), t)
            t = dve.put(lambda: V.reciprocal(inv, total), t)
            job["p"] = (pi, p, dve.put(lambda: V.tensor_scalar(p, p, inv, None, ALU.mult), t))

        def stage_transpose(job):
            pi, p, t_p = job["p"]
            n = p.shape[-1] // P
            qi, pt, pt_free = pt_ring.take()
            ts = []
            for c0 in range(0, n, 4):
                nc_ = min(4, n - c0)
                i, bank, free = att.take()
                for c in range(nc_):
                    t = pe.put(lambda c=c, c0=c0, bank=bank: T.transpose(bank[:, c * P:(c + 1) * P], p[:, (c0 + c) * P:(c0 + c + 1) * P], ident[:, :]),
                               t_p, free)
                dst = pt[:, c0 * P:(c0 + nc_) * P]
                t2 = act.put(lambda dst=dst, bank=bank, nc_=nc_: S.activation(dst, bank[:, 0:nc_ * P], ACT.Copy), t, pt_free)
                att.give(i, t2)
                ts.append(t2)
            p_ring.give(pi, t)
            job["pt"] = (qi, pt, ts)

        held = {}

        def stage_values(job):
            qi, pt, ts = job["pt"]
            rows = slice(64 * job["half"], 64 * job["half"] + 64)
            if job["half"] == 0:
                held["o"] = last.take()
            i, bank, free = held["o"]
            nv = len(job["vals"])
            for c, v in enumerate(job["vals"]):
                t = pe.put(lambda c=c, v=v, bank=bank, rows=rows: T.matmul(bank[rows, 0:P], v, pt[:, c * P:(c + 1) * P],
                                                                        start=c == 0, stop=c == nv - 1), ts, free, job["v_ready"])
            pt_ring.give(qi, t)
            if job["half"] == 1:
                last.give(i, *job["finish"](bank[:, 0:P], t))
                if job.get("done"):
                    job["done"](t)

        for s in range(len(jobs) + 2):
            if s < len(jobs):
                stage_scores(jobs[s])
            if 0 <= s - 1 < len(jobs):
                stage_transpose(jobs[s - 1])
            if 0 <= s - 2 < len(jobs):
                stage_values(jobs[s - 2])
            yield

    prev = fence()
    m = Map(PHASE, END)
    na_y = Split({LAT: [m.sb(f"na_y_{s}", [P, KD, NLAT], F32R) for s in ("hi", "lo")]})
    na_q = Ring([m.sb(f"na_q{i}", [P, NLAT]) for i in range(2)])
    na_k = Ring([m.sb(f"na_k{i}", [P, NTOK]) for i in range(2)])
    na_v = Ring([m.sb(f"na_v{i}", [P, 10, P]) for i in range(2)])
    na_vt = m.sb("na_vt", [P, NTOK])
    na_rel = Ring([m.sb(f"na_rel{i}", [P, ROWS, REL]) for i in range(2)])
    na_bias = Ring([m.sb(f"na_bias{i}", [P, 3, ROWS * BAND]) for i in range(2)])
    na_mask = m.sb("na_mask", [P, 3, BAND])
    na_p = Ring([m.sb(f"na_p{i}", [P, NCTX + ROWS * BAND]) for i in range(2)])
    na_pt = Ring([m.sb(f"na_pt{i}", [P, NCTX + ROWS * BAND]) for i in range(2)])
    for r in (na_q, na_k, na_v, na_rel, na_bias, na_p, na_pt):
        r.free = [list(prev) for _ in r.free]
    na_y.read = prev
    mask_sem = dma_slot("loaded_na_mask")
    mask_loaded = pool.dma(na_mask[:, :, :], a["na_mask"], mask_sem, prev)
    rel_sem = [dma_slot(f"loaded_rel{i}") for i in range(2)]

    pad_sem = dma_slot("stored_rpb")
    rpb_dram = nc.dram_tensor("rpb_padded", [NA_HEADS * RPB_ROWS, RPB_WIDE], F32)
    half_rows = NA_HEADS * RPB_ROWS // 2
    pad = tmp[0:half_rows, 0, 0:2 * RPB_WIDE].rearrange("p (a c) -> p a c", a=2)
    ti, _, free = tmp_ring.take()
    if ti != 0:
        tmp_ring.give(ti, *free)
        ti, _, free = tmp_ring.take()
    t = pool.put(lambda: G.memset(pad, 0.0), free)
    t = pool.dma(pad[:, :, 16:16 + RPB_COLS], a["rpb"], pad_sem, t)
    rpb_stored = pool.dma(rpb_dram.ap().rearrange("(p a) c -> p a c", a=2), pad, pad_sem, t)
    tmp_ring.give(ti, rpb_stored)
    rpb_size = NA_HEADS * RPB_ROWS * RPB_WIDE
    rpb_copies = nc.dram_tensor("rpb_copies", [QB, rpb_size], F32)
    copy_sem = dma_slot("copied_rpb")
    rpb_stored = pool.dma(rpb_copies.ap(), bass.AP(rpb_dram.ap().tensor, 0, [[0, QB], [1, rpb_size]]), copy_sem, rpb_stored)

    BAND_START = [BAND0[n] - QB * n + QB for n in range(4)]
    VARIANT = [0, 1, 1, 2]
    grid = lambda ap: ap.rearrange("p (r c) -> p r c", c=GRID)
    vt_read = [prev]

    def na_head_bias(head):
        ri, rel, rfree = na_rel.take()
        for r in range(ROWS):
            src = bass.AP(rpb_copies.ap().tensor, (head * RPB_ROWS + 7 - r) * RPB_WIDE + 15,
                          [[rpb_size - 1, QB], [RPB_WIDE, ROWS], [1, REL]])
            t = pool.dma(rel[r * QB:(r + 1) * QB, :, :], src, rel_sem[ri], rfree, rpb_stored)
        bi, bias, bfree = na_bias.take()
        ts = []
        for v, n in enumerate((0, 1, 3)):
            b0 = BAND_START[n]
            ts.append(pool.put(lambda v=v, b0=b0: G.tensor_tensor(
                bias[:, v, :].rearrange("p (r c) -> p r c", c=BAND), rel[:, :, b0:b0 + BAND],
                na_mask[:, v:v + 1, :].to_broadcast([P, ROWS, BAND]), ALU.add), t, bfree, mask_loaded))
        na_rel.give(ri, *ts)
        return bi, bias, ts

    plain = lambda ap: ap

    def na_pair(pair):
        qi, q, qfree = na_q.take()
        (i, bank, t), = linear(X, KD, ONLY_LAT, 4)
        tq = act.put(lambda: S.activation(q[:, :].rearrange("p (n r c) -> p r n c", r=ROWS, c=QB),
                                          bank.rearrange("p (r n c) -> p r n c", r=ROWS, c=QB),
                                          ACT.Copy, scale=HEAD ** -0.5), t, qfree)
        lin.give(i, tq)
        ki, kk, kfree = na_k.take()
        tk = []
        for (i, bank, t), g in zip(linear(X, KD, BOTH, 4), BOTH):
            tk.append(act.put(lambda bank=bank, g=g: S.activation(kk[:, START[g]:START[g] + TOKENS[g]], bank, ACT.Copy), t, kfree))
            lin.give(i, tk[-1])
        vi, vv, vfree = na_v.take()
        tv = []
        for (i, bank, t), g in zip(linear(X, KD, BOTH, 4), BOTH):
            dst = na_vt[:, START[g]:START[g] + TOKENS[g]]
            if g == LAT:
                dst, bank = dst.rearrange("p (c r) -> p r c", r=ROWS), grid(bank)
            tv.append(act.put(lambda: S.activation(dst, bank, ACT.Copy), t, vt_read[0]))
            lin.give(i, tv[-1])
        tiles = [na_vt[:, s * P:(s + 1) * P] for s in range(2)]
        for n in range(4):
            for u in range(2):
                c0 = NCTX + ROWS * (BAND0[n] + QB * u)
                tiles.append(na_vt[:, c0:c0 + P])
        v_ready = []
        for c0 in range(0, 10, 4):
            nt = min(4, 10 - c0)
            i, bank, free = att.take()
            for c in range(nt):
                t = pe.put(lambda c=c, c0=c0, bank=bank: T.transpose(bank[:, c * P:(c + 1) * P], tiles[c0 + c], ident[:, :]), tv, free)
            t2 = dve.put(lambda c0=c0, nt=nt, bank=bank: V.tensor_copy(vv[:, c0:c0 + nt, :], bank[:, 0:nt * P].rearrange("p (s c) -> p s c", c=P)), t, vfree)
            att.give(i, t2)
            v_ready.append(t2)
        vt_read[0] = [t]
        jobs = []
        drain()
        biases = [na_head_bias(2 * pair + e) for e in range(2)]
        for n in range(4):
            for e in range(2):
                rows = slice(64 * e, 64 * e + 64)
                bi, bias, b_ready = biases[e]
                lhsT = q[rows, n * P:(n + 1) * P]
                keys = grid(kk[rows, NCTX:NTOK])[:, :, BAND0[n]:BAND0[n] + BAND]

                def bias_read(ts, n=n, bi=bi):
                    if n == 3:
                        na_bias.give(bi, *ts)

                def finish(bank, t, n=n):
                    view = lambda ap: grid(ap)[:, :, QB * n:QB * n + QB]
                    return put_split(na_y, pair, LAT, bank.rearrange("p (r c) -> p r c", c=QB), t, view=view)

                def done(t, n=n):
                    if n == 3:
                        na_q.give(qi, t)
                        na_k.give(ki, t)
                        na_v.give(vi, t)

                jobs.append(dict(segs=[(NCTX, [(lhsT, kk[rows, 0:NCTX])], None, plain, plain),
                                       (ROWS * BAND, [(lhsT, keys)], bias[:, VARIANT[n], :],
                                        lambda ap: ap.rearrange("p (r c) -> p r c", c=BAND),
                                        lambda ap: ap.rearrange("p (c r) -> p r c", c=BAND))],
                                 ready=[tq] + tk, bias_ready=b_ready, bias_read=bias_read, half=e, v_ready=v_ready,
                                 vals=[vv[:, s, 64 * e:64 * e + 64] for s in (0, 1, 2 + 2 * n, 3 + 2 * n)],
                                 finish=finish, done=done))
        return jobs

    for pair in range(NA_HEADS // 2):
        jobs = na_pair(pair)
        background.append(attend(jobs, na_p, na_pt))
    drain()
    for o in range(KD):
        add_gated(1, 2, o, ONLY_LAT, linear(na_y, KD, ONLY_LAT), True)

    prev = fence()
    layer_norm(2, ONLY_LAT, 1, 3)
    PATTERNS = (("w", 0, 4, 1024), ("d4", 4, 4, 256), ("d16", 8, 4, 256), ("c", 12, 8, 640))
    table_sem, hot_sem, toep_sem, copied_sem = (dma_slot(n) for n in (
        "loaded_table", "loaded_onehot", "stored_toeplitz", "copied_toeplitz"))
    toep = {}

    def relative_bias():
        table_loaded = pool.dma(table[:, :], a["table"], table_sem)
        for name, h0, nh, width in PATTERNS:
            by_distance = nc.dram_tensor(f"toeplitz_{name}", [nh, width], F32)
            for c0 in range(0, width, NLAT):
                n = min(NLAT, width - c0)
                pi, hot, free = tmp_ring.take()
                loaded = pool.dma(hot[0:33, 0:n], a[f"hot_{name}"][:, c0:c0 + n], hot_sem, free)
                yield
                i, bank, bfree = att.take()
                t = pe.put(lambda: T.matmul(bank[0:nh, 0:n], table[:, h0:h0 + nh], hot[0:33, 0:n], start=True, stop=True),
                           loaded, table_loaded, bfree)
                yield
                qi, row, rfree = tmp_ring.take()
                t2 = act.put(lambda: S.activation(row[0:nh, 0:n], bank[0:nh, 0:n], ACT.Copy), t, rfree)
                att.give(i, t2)
                stored = pool.dma(by_distance.ap()[:, c0:c0 + n], row[0:nh, 0:n], toep_sem, t2)
                tmp_ring.give(pi, t)
                pool.wait([stored])
                tmp_ring.give(qi, stored)
                yield
            copies = nc.dram_tensor(f"toeplitz_copies_{name}", [P, nh * width], F32)
            toep["copied"] = pool.dma(copies.ap(), bass.AP(by_distance.ap().tensor, 0, [[0, P], [1, nh * width]]),
                                      copied_sem, stored)
            toep[name] = (copies, nh * width)
            yield

    background.append(relative_bias())
    ffn("ffn1", ONLY_LAT, prev, lambda o, outs, end: add_gated(1, 5, o, ONLY_LAT, outs, end))
    drain()
    layer_norm(3, ONLY_LAT)

    sums = open_sums(LAT)
    for k in range(KD):
        add_squares(sums, k, H[LAT][:, k, :], h_ready[k, LAT], KD - 1)
    rms_norm(sums, "g_mix", lambda k, x, t: to_x(k, LAT, x, t))

    prev = fence()
    m = Map(PHASE, END)
    o_a = Split({LAT: [m.sb(f"o_a_{s}", [P, 2, NLAT], F32R) for s in ("hi", "lo")]})
    o_b = Split({LAT: [m.sb(f"o_b_{s}", [P, 4, NLAT], F32R) for s in ("hi", "lo")]})
    o_c = Split({LAT: [m.sb(f"o_c_{s}", [P, 4, NLAT], F32R) for s in ("hi", "lo")]})
    for x in (o_a, o_b, o_c):
        x.read = prev
    merge_start = m.at
    DIL_KEYS = NLAT + 2 * P
    U0W = NLAT + 3
    dil_q = [m.sb(f"dil_q{g}", [P, NLAT]) for g in range(3)]
    moba_start = m.at
    dil_k = [m.sb(f"dil_k{g}", [P, NLAT]) for g in range(3)]
    dil_v = m.sb("dil_v", [P, 12, P])
    vt2 = m.sb("vt2", [P, NLAT])
    dil_bias = Ring([m.sb(f"dil_bias{i}", [P, U0W + 2 * P]) for i in range(2)])
    p_ring = Ring([m.sb(f"p2_{i}", [P, DIL_KEYS]) for i in range(2)])
    pt_ring = Ring([m.sb(f"pt2_{i}", [P, DIL_KEYS]) for i in range(2)])
    c = Map(ctx_start, ctx_end)
    lru = {n: c.sb(f"lru_{n}", [P, NLAT + (3 if n == "x" else 0)]) for n in ("x", "g", "xc", "r", "ig", "a", "s", "u")}
    gate_w = c.sb("lru_gate_w", [P, 2, LRU_TILES, P])
    for r in (dil_bias, p_ring, pt_ring):
        r.free = [list(prev) for _ in r.free]

    def diagonals(name, head, width, base, step, cols):
        copies, pitch = toep[name]
        return bass.AP(copies.ap().tensor, head * width + base, [[pitch + step, P], [1, cols]])

    bias_sem = [dma_slot(f"loaded_dil_bias{i}") for i in range(2)]

    def dil_head_bias(j):
        bi, bias, free = dil_bias.take()
        pool.dma(bias[:, 0:U0W], diagonals("w", j, 1024, 508, -4, U0W), bias_sem[bi], free, toep["copied"])
        pool.dma(bias[:, U0W:U0W + P], diagonals("d4", j, 256, 127, -1, P), bias_sem[bi])
        t = pool.dma(bias[:, U0W + P:U0W + 2 * P], diagonals("d16", j, 256, 127, -1, P), bias_sem[bi])
        return bi, bias, [t]

    dil = {"read": [prev], "vt": [prev]}
    by4 = lambda ap: ap.rearrange("p (i r) -> p r i", r=4)

    def v_tiles(dst, sources, ready, free_v):
        ts = []
        for c0 in range(0, len(sources), 4):
            nt = min(4, len(sources) - c0)
            i, bank, free = att.take()
            for c in range(nt):
                t = pe.put(lambda c=c, c0=c0, bank=bank: T.transpose(bank[:, c * P:(c + 1) * P], sources[c0 + c], ident[:, :]), ready, free)
            t2 = dve.put(lambda c0=c0, nt=nt, bank=bank: V.tensor_copy(dst(c0, nt), bank[:, 0:nt * P].rearrange("p (s c) -> p s c", c=P)), t, free_v)
            att.give(i, t2)
            ts.append(t2)
        return ts, t

    def dilated_pair(jp):
        ready = []
        for name, dst in (("q", dil_q), ("k", dil_k)):
            for g in range(3):
                (i, bank, t), = linear(X, KD, ONLY_LAT)
                ready.append(act.put(lambda bank=bank, d=dst[g], s=(HEAD ** -0.5 if name == "q" else 1.0):
                                     S.activation(d[:, :], bank, ACT.Copy, scale=s), t, dil["read"]))
                lin.give(i, ready[-1])
        v_ready = []
        for g in range(3):
            (i, bank, t), = linear(X, KD, ONLY_LAT)
            tv = act.put(lambda bank=bank: S.activation(vt2[:, :], bank, ACT.Copy), t, dil["vt"])
            lin.give(i, tv)
            src = [vt2[:, s * P:(s + 1) * P] if g == 0 else by4(vt2[:, :])[:, s, :] for s in range(4)]
            ts, t = v_tiles(lambda c0, nt, g=g: dil_v[:, 4 * g + c0:4 * g + c0 + nt, :], src, tv, dil["read"])
            dil["vt"] = [t]
            v_ready += ts
        drain()
        biases = [dil_head_bias(2 * jp + e) for e in range(2)]
        jobs = []
        for r in range(4):
            for e in range(2):
                rows = slice(64 * e, 64 * e + 64)
                bi, bias, b_ready = biases[e]

                def bias_read(ts, r=r, bi=bi):
                    if r == 3:
                        dil_bias.give(bi, *ts)

                def finish(bank, t, r=r):
                    return put_split(o_a, jp, LAT, bank, t, view=lambda ap: by4(ap)[:, r, :])

                def done(t, r=r):
                    if r == 3:
                        dil["read"] = [t]

                q = [by4(dil_q[g][rows, :])[:, r, :] for g in range(3)]
                segs = [(NLAT, [(q[0], dil_k[0][rows, :])], bias[:, 3 - r:3 - r + NLAT], plain, plain)]
                for g in (1, 2):
                    segs.append((P, [(q[g], by4(dil_k[g][rows, :])[:, r, :])], bias[:, U0W + (g - 1) * P:U0W + g * P], plain, plain))
                jobs.append(dict(segs=segs, ready=ready, bias_ready=b_ready, bias_read=bias_read, half=e, v_ready=v_ready,
                                 vals=[dil_v[:, s, 64 * e:64 * e + 64] for s in (0, 1, 2, 3, 4 + r, 8 + r)],
                                 finish=finish, done=done))
        return jobs

    lru_sem = dma_slot("loaded_lru_gates")
    t = pool.put(lambda: G.memset(gate_w[:, :, :, :], 0.0), prev)
    for which, name in enumerate(("lru_wa", "lru_wx")):
        for e in range(2):
            rows = slice(64 * e, 64 * e + 64)
            gates_loaded = pool.dma(gate_w[rows, which, :, rows], a[name][e], lru_sem, t)
    t_pad = pool.put(lambda: G.memset(lru["x"][:, 0:3], 0.0), prev)
    lam = vc("lru_lam", 0, 4)
    y0, z, z2, acc, sp_c = (small[:, 64 + 4 * i:68 + 4 * i] for i in range(5))
    t = act.put(lambda: S.activation(y0, lam, ACT.Abs), consts)
    t = act.put(lambda: S.activation(y0, y0, ACT.Exp, scale=-1.0), t)
    t = dve.put(lambda: V.tensor_scalar(z, y0, 2.0, None, ALU.add), t)
    t = dve.put(lambda: V.reciprocal(z, z), t)
    t = dve.put(lambda: V.tensor_tensor(z, z, y0, ALU.mult), t)
    t = dve.put(lambda: V.tensor_tensor(z2, z, z, ALU.mult), t)
    t = dve.put(lambda: V.tensor_scalar(acc, z2, 1.0 / 17, 1.0 / 15, ALU.mult, ALU.add), t)
    for d in (13, 11, 9, 7, 5, 3, 1):
        t = dve.put(lambda: V.tensor_tensor(acc, acc, z2, ALU.mult), t)
        t = dve.put(lambda d=d: V.tensor_scalar(acc, acc, 1.0 / d, None, ALU.add), t)
    t = dve.put(lambda: V.tensor_tensor(acc, acc, z, ALU.mult), t)
    t = dve.put(lambda: V.tensor_scalar(y0, lam, -1.0, 0.0, ALU.mult, ALU.max), t)
    t = dve.put(lambda: V.scalar_tensor_tensor(sp_c, acc, 2.0, y0, ALU.mult, ALU.add), t)
    sp_ready = dve.put(lambda: V.tensor_scalar(sp_c, sp_c, -8.0, None, ALU.mult), t)
    lru_free = {"x": [prev, t_pad], "g": [prev], "rest": [prev]}

    def lru_tile(k):
        xt, xc, r, ig, la, s, u = (lru[n] for n in ("x", "xc", "r", "ig", "a", "s", "u"))
        (i, bank, t), = linear(X, KD, ONLY_LAT, 4)
        tx = act.put(lambda: S.activation(xt[:, 3:3 + NLAT], bank, ACT.Copy), t, lru_free["x"])
        lin.give(i, tx)
        (i, bank2, t), = linear(X, KD, ONLY_LAT, 4)
        gb = lru["g"][:, :]
        tg = act.put(lambda: S.activation(gb, bank2, ACT.Copy), t, lru_free["g"])
        lin.give(i, tg)
        cw = lambda i: vc("conv_w", 4 * k + i)
        t = dve.put(lambda: V.tensor_scalar(xc[:, :], xt[:, 0:NLAT], cw(0), vc("conv_b", k), ALU.mult, ALU.add), tx, t_pad, lru_free["rest"])
        for i_ in range(1, 4):
            t = dve.put(lambda i_=i_: V.scalar_tensor_tensor(xc[:, :], xt[:, i_:i_ + NLAT], cw(i_), xc[:, :], ALU.mult, ALU.add), t)
        lru_free["x"] = [t]
        t_xc = t
        gates = []
        for which, (dst, b) in enumerate(((r, "lru_ba"), (ig, "lru_bx"))):
            i, bank3, free = att.take()
            t = pe.put(lambda bank3=bank3, which=which: T.matmul(bank3[:, :], gate_w[:, which, k, :], xc[:, :], start=True, stop=True), t_xc, free, gates_loaded)
            t2 = act.put(lambda bank3=bank3, dst=dst, b=b: S.activation(dst[:, :], bank3[:, :], ACT.Sigmoid, bias=vc(b, k)), t, lru_free["rest"])
            att.give(i, t2)
            gates.append(t2)
        t_la = dve.put(lambda: V.tensor_scalar(la[:, :], r[:, :], sp_c[:, k:k + 1], None, ALU.mult), gates, sp_ready, lru_free["rest"])
        t = dve.put(lambda: V.tensor_tensor(u[:, :], gb, gb, ALU.mult), tg, lru_free["rest"])
        t = dve.put(lambda: V.tensor_scalar(u[:, :], u[:, :], 0.044715, 1.0, ALU.mult, ALU.add), t)
        t = dve.put(lambda: V.tensor_tensor(u[:, :], u[:, :], gb, ALU.mult), t)
        t_u = act.put(lambda: S.activation(u[:, :], u[:, :], ACT.Tanh, scale=(2 / np.pi) ** 0.5), t)
        t_s = act.put(lambda: S.activation(s[:, :], la[:, :], ACT.Tanh, scale=-1.0), t_la)
        t_r = act.put(lambda: S.activation(r[:, :], la[:, :], ACT.Exp, scale=2.0), t_la)
        t_a = act.put(lambda: S.activation(la[:, :], la[:, :], ACT.Exp), t_r, t_s)
        t = dve.put(lambda: V.scalar_tensor_tensor(s[:, :], r[:, :], 1.0, s[:, :], ALU.add, ALU.mult), t_s, t_r)
        t_s = act.put(lambda: S.activation(s[:, :], s[:, :], ACT.Sqrt), t)
        t = dve.put(lambda: V.tensor_tensor(ig[:, :], ig[:, :], xc[:, :], ALU.mult), gates, t_xc)
        t = dve.put(lambda: V.tensor_tensor(s[:, :], s[:, :], ig[:, :], ALU.mult), t, t_s)
        t_h = dve.put(lambda: V.tensor_tensor_scan(r[:, :], la[:, :], s[:, :], 0.0, ALU.mult, ALU.add), t, t_a)
        t = dve.put(lambda: V.tensor_scalar(u[:, :], u[:, :], 0.5, 0.5, ALU.mult, ALU.add), t_u)
        t = dve.put(lambda: V.tensor_tensor(u[:, :], u[:, :], gb, ALU.mult), t)
        lru_free["g"] = [t]
        t = dve.put(lambda: V.tensor_tensor(u[:, :], u[:, :], r[:, :], ALU.mult), t, t_h)
        lru_free["rest"] = put_split(o_b, k, LAT, u[:, :], t)

    jobs = dilated_pair(0)
    background.append(attend(jobs, p_ring, pt_ring))
    for k in range(LRU_TILES):
        lru_tile(k)
    jobs = dilated_pair(1)
    background.append(attend(jobs, p_ring, pt_ring))

    after_lru = fence()
    c3 = Map(ctx_start, ctx_end)
    mq = Ring([c3.sb(f"moba_q{i}", [P, NLAT]) for i in range(2)])
    mk = Ring([c3.sb(f"moba_k{i}", [P, NLAT]) for i in range(2)])
    mv = Ring([c3.sb(f"moba_v{i}", [P, 4, P]) for i in range(2)])
    mb = Ring([cond[:, i * NLAT:(i + 1) * NLAT] for i in range(2)])
    for r in (mq, mk, mv, mb):
        r.free = [list(after_lru) for _ in r.free]
    mb_sem = [dma_slot(f"loaded_moba_bias{i}") for i in range(2)]

    def moba_pair(pair):
        (i, bank, t), = linear(X, KD, ONLY_LAT, 4)
        qi, q, free = mq.take()
        tq = act.put(lambda: S.activation(q[:, :], bank, ACT.Copy, scale=HEAD ** -0.5), t, free)
        lin.give(i, tq)
        (i, bank1, t), = linear(X, KD, ONLY_LAT, 4)
        ki, kk, free = mk.take()
        tk = act.put(lambda: S.activation(kk[:, :], bank1, ACT.Copy), t, free)
        lin.give(i, tk)
        (i, bank2, t), = linear(X, KD, ONLY_LAT, 4)
        tv = act.put(lambda: S.activation(vt2[:, :], bank2, ACT.Copy), t, dil["vt"])
        lin.give(i, tv)
        vi, vv, free = mv.take()
        v_ready, t = v_tiles(lambda c0, nt: vv[:, c0:c0 + nt, :], [vt2[:, s * P:(s + 1) * P] for s in range(4)], tv, free)
        dil["vt"] = [t]
        drain()
        biases = []
        for e in range(2):
            bi, bias, free = mb.take()
            biases.append((bi, bias, [pool.dma(bias[:, :], diagonals("c", 2 * pair + e, 640, 127, -1, NLAT), mb_sem[bi], free, toep["copied"])]))
        jobs = []
        for n in range(4):
            for e in range(2):
                rows = slice(64 * e, 64 * e + 64)
                bi, bias, b_ready = biases[e]

                def bias_read(ts, n=n, bi=bi):
                    if n == 3:
                        mb.give(bi, *ts)

                def finish(bank, t, n=n):
                    return put_split(o_c, pair, LAT, bank, t, view=lambda ap: ap[:, n * P:(n + 1) * P])

                def done(t, n=n):
                    if n == 3:
                        mq.give(qi, t)
                        mk.give(ki, t)
                        mv.give(vi, t)

                keys = (n + 1) * P
                jobs.append(dict(segs=[(keys, [(q[rows, n * P:(n + 1) * P], kk[rows, 0:keys])],
                                        bias[:, NLAT - keys:NLAT], plain, plain)],
                                 ready=[tq, tk], bias_ready=b_ready, bias_read=bias_read, half=e, v_ready=v_ready,
                                 vals=[vv[:, s, 64 * e:64 * e + 64] for s in range(n + 1)], finish=finish, done=done))
        background.append(attend(jobs, p_ring, pt_ring))

    for pair in range(MOBA_HEADS // 2):
        moba_pair(pair)
    drain()

    prev = fence()
    m = Map(merge_start, END)
    merged = Split({LAT: [m.sb(f"merged_{s}", [P, KD, NLAT], F32R) for s in ("hi", "lo")]})
    merged.read = prev
    c = Map(ctx_start, ctx_end)
    gates_r = Ring([c.sb(f"gate2_{i}", [P, NLAT]) for i in range(3)])
    sum_r = Ring([c.sb(f"sum2_{i}", [P, NLAT]) for i in range(2)])
    for r in (gates_r, sum_r):
        r.free = [list(prev) for _ in r.free]
    for o in range(KD):
        si, mixed, sfree = sum_r.take()
        t_sum = None
        for branch, (x, kt) in enumerate(((o_a, 2), (o_b, 4), (o_c, 4))):
            (i, bank, t), = linear(X, KD, ONLY_LAT)
            gi, gt, free = gates_r.take()
            tg = act.put(lambda bank=bank, gt=gt: S.activation(gt[:, :], bank, ACT.Sigmoid), t, free)
            lin.give(i, tg)
            (i, bank, t), = linear(x, kt, ONLY_LAT)
            dst = mixed if branch == 0 else gt
            t2 = dve.put(lambda bank=bank, gt=gt, dst=dst: V.tensor_tensor(dst[:, :], bank, gt[:, :], ALU.mult), t, tg, sfree)
            lin.give(i, t2)
            if branch:
                t2 = dve.put(lambda gt=gt, mixed=mixed: V.tensor_tensor(mixed[:, :], mixed[:, :], gt[:, :], ALU.add), t2, t_sum)
            t_sum = t2
            gates_r.give(gi, t2)
        sum_r.give(si, *put_split(merged, o, LAT, mixed[:, :], t_sum))

    def add_plain(o, outs, sums):
        (i, bank, t), = outs
        h = H[LAT][:, o, :]
        t2 = dve.put(lambda: V.tensor_tensor(h, bank, h, ALU.add), t, h_ready[o, LAT])
        h_ready[o, LAT] = [t2]
        lin.give(i, t2)
        if sums:
            add_squares(sums, o, h, t2, KD - 1, later=True)

    sums = open_sums(LAT)
    for o in range(KD):
        add_plain(o, linear(merged, KD, ONLY_LAT), sums)
    prev = fence()
    rms_norm(sums, "g_ffn", lambda k, x, t: to_x(k, LAT, x, t))
    sums = open_sums(LAT)
    ffn("ffn2", ONLY_LAT, prev, lambda o, outs, end: add_plain(o, outs, sums if end else None))

    out_sem = dma_slot("stored_out")

    def store(k, ap, t):
        end = sp.dma(out[:, k, :], ap, out_sem, t)
        sp.wait([end])
        return [end]

    rms_norm(sums, "g_final", store)
    assert state["used"] == len(plan) and state["taken"] == state["split"]

    stack.close()


def _blocks(m):
    K, N = m.shape
    return np.ascontiguousarray(m.reshape(K // P, P, N // P, P).transpose(2, 1, 0, 3)).reshape(N // P, P, K)


def _cols(v):
    return np.ascontiguousarray(v.reshape(-1, P).T)


def _buckets(dist):
    d = np.maximum(dist, 0)
    df = np.maximum(d, 1).astype(np.float32)
    large = 16 + (np.log(df / np.float32(16)) / np.float32(np.log(2048 / 16)) * np.float32(16)).astype(np.int32)
    return np.where(d < 16, d, np.minimum(large, 31))


def _one_hot(dist, valid, width):
    hot = np.zeros((33, width), np.float32)
    row = np.where(valid, _buckets(dist), 32)
    hot[row, np.arange(len(dist))] = 1.0
    hot[32, len(dist):] = 1.0
    return hot


def _constants():
    t = np.arange(NLAT)
    nf = RET_DK // 4
    inv = np.float32(10000.0) ** (-np.arange(nf, dtype=np.float32) / np.float32(nf))
    ang = np.concatenate([(t // GRID).astype(np.float32)[:, None] * inv, (t % GRID).astype(np.float32)[:, None] * inv], -1)
    c = {"cos": np.ascontiguousarray(np.cos(ang).T), "sin": np.ascontiguousarray(np.sin(ang).T)}
    c["ident"] = np.eye(P, dtype=np.float32)
    c["dist"] = (np.arange(NLAT + 3 * P)[None, :] - np.arange(P)[:, None] - 3 * P).astype(np.float32)
    mask = np.full((P, 3, BAND), NEG, np.float32)
    for v, n in enumerate((0, 1, 3)):
        for q in range(P):
            qc = n * QB + q % QB
            start = min(max(qc - WIN // 2, 0), GRID - WIN)
            for j in range(BAND):
                if start <= BAND0[n] + j < start + WIN:
                    mask[q, v, j] = 0.0
    c["na_mask"] = mask
    i = np.arange(1023)
    c["hot_w"] = _one_hot(511 - i, (511 - i >= 0) & (511 - i <= 128), 1024)
    i = np.arange(255)
    d = 127 - i
    c["hot_d4"] = _one_hot(4 * d, d >= 0, 256)
    c["hot_d16"] = _one_hot(4 * d, (d >= 0) & (d % 4 == 0), 256)
    i = np.arange(639)
    c["hot_c"] = _one_hot(511 - i, 511 - i >= 0, 640)
    return {k: np.ascontiguousarray(v.astype(np.float32)) for k, v in c.items()}


def kernel(**inputs):
    import concourse.bacc as bacc
    from concourse.bass_utils import run_bass_kernel_spmd

    f = {k: np.asarray(v) for k, v in inputs.items()}
    wts = {"ret_in": _blocks(f["ret_w_in"]), "na_qkv": _blocks(f["na_w_qkv"]), "na_out": _blocks(f["na_w_out"]),
           "in_2": _blocks(f["w_in_2"][0]), "out_2": _blocks(f["w_out_2"][0]),
           "p_a": _blocks(f["p_a_2"][0]), "p_b": _blocks(f["p_b_2"][0]), "p_c": _blocks(f["p_c_2"][0]),
           "w13_0": _blocks(f["ffn_w13"][0]), "w13_1": _blocks(f["ffn_w13"][1]), "w13_2": _blocks(f["w_gu_2"][0]),
           "ret_out": np.stack([_blocks(f["ret_w_out"][RET_DV * h:RET_DV * (h + 1)]) for h in range(RET_HEADS)]),
           **{f"ada_{l}": np.ascontiguousarray(f["ada_w"][l].T).reshape(6 * KD, P, D) for l in range(2)},
           "ada_scale_0": _blocks(f["ada_w"][0][:, D:2 * D])}
    for n, w2 in enumerate((f["ffn_w2"][0], f["ffn_w2"][1], f["w_down_2"][0])):
        for c, (f0, k) in enumerate(FF_CHUNKS):
            wts[f"w2_{n}_{c}"] = _blocks(w2[P * f0:P * (f0 + k)])
    vec = np.concatenate([
        _cols(f["ada_b"]), _cols(f["ln_g"]), _cols(f["ln_b"]), _cols(f["g_mix_2"]), _cols(f["g_ffn_2"]),
        _cols(f["g_final_2"]), f["conv_w_2"][0].reshape(4, LRU_TILES, P).transpose(2, 1, 0).reshape(P, 16),
        _cols(f["conv_b_2"]), _cols(f["lru_ba_2"]), _cols(f["lru_bx_2"]), _cols(f["lru_lam_2"]),
        np.broadcast_to(f["ret_decay"].reshape(1, 8), (P, 8))], 1)
    acts = dict(_constants())
    acts["cond_cols"] = np.ascontiguousarray(np.stack([f["c"][0], f["c_ctx"]]).reshape(2, KD, P).transpose(2, 1, 0))
    acts["cond"] = np.concatenate([f["c"][0], f["c_ctx"]])
    acts["vec"] = np.ascontiguousarray(vec)
    acts["x"] = np.ascontiguousarray(f["x"][0].T.reshape(KD, P, NLAT).transpose(1, 0, 2))
    acts["ctx"] = np.ascontiguousarray(f["ctx"][0].T.reshape(KD, P, NCTX).transpose(1, 0, 2))
    acts["rpb"] = np.ascontiguousarray(f["na_rpb"].reshape(NA_HEADS * RPB_ROWS // 2, 2, RPB_COLS))
    acts["table"] = np.concatenate([f["rel_bias_2"], np.full((1, 20), NEG, np.float32)], 0)
    for n in ("lru_wa", "lru_wx"):
        acts[n] = np.ascontiguousarray(f[n + "_2"][0].reshape(LRU_TILES, 2, 64, 64).transpose(1, 2, 0, 3))
    wts["dist"] = acts.pop("dist")

    nc = bacc.Bacc("TRN2", target_bir_lowering=False, num_devices=1)
    arrays, aps = {}, ({}, {})
    for which, group in enumerate((acts, wts)):
        for name, array in group.items():
            arrays[f"in_{name}"] = array
            aps[which][name] = nc.dram_tensor(f"in_{name}", list(array.shape), mybir.dt.from_np(array.dtype),
                                              kind="ExternalInput").ap()
    out = nc.dram_tensor("out_t", [P, KD, NLAT], F32, kind="ExternalOutput")
    program(nc, aps[0], aps[1], out.ap())
    result = run_bass_kernel_spmd(nc, [arrays], core_ids=[0]).results[0]["out_t"]
    return np.ascontiguousarray(result.transpose(2, 1, 0).reshape(1, NLAT, D))
```

```python
from collections import deque
from contextlib import ExitStack

import numpy as np
import concourse.bass as bass
from concourse import mybir
from concourse.alu_op_type import AluOpType as ALU

F32 = mybir.dt.float32
F32R = mybir.dt.float32r
ACT = mybir.ActivationFunctionType
AX = mybir.AxisListType.X

P = 128
D = 1024
KD = D // P
NCTX, NLAT = 256, 512
NTOK = NCTX + NLAT
CTX, LAT = 0, 1
TOKENS = {CTX: NCTX, LAT: NLAT}
START = {CTX: 0, LAT: NCTX}
BOTH, ONLY_LAT = (CTX, LAT), (LAT,)
FF = -(-8 * D // (3 * 256)) * 256
KF = FF // P
KMAX = 8
FF_CHUNKS = [(a, min(KMAX, KF - a)) for a in range(0, KF, KMAX)]
ALPHA = 4 ** 0.25
LN_EPS, RMS_EPS = 1e-5, 1e-6
NEG = -1e30
GRID = 64
ROWS = NLAT // GRID
RET_HEADS, RET_DK, RET_DV = 4, 256, 512
NA_HEADS, HEAD = 16, 64
QB, BAND, WIN = 16, 32, 16
BAND0 = [int(v) for v in np.clip(np.arange(GRID // QB) * QB - WIN // 2, 0, GRID - BAND)]
RPB_ROWS, RPB_COLS, RPB_WIDE = 15, 31, 64
REL = QB + BAND
GROUP_HEADS, DIL_GROUPS, MOBA_HEADS = 4, 3, 8
LRU_TILES = 4
ADA_REST, ADA_ALL = (2, 3, 4, 5), (0, 1, 2, 3, 4, 5)

VECS = {}


def _vec(name, n):
    VECS[name] = (sum(k for _, k in VECS.values()), n)


for _name, _n in (("ada_b", 2 * 48), ("ln_g", 4 * KD), ("ln_b", 4 * KD), ("g_mix", KD), ("g_ffn", KD),
                  ("g_final", KD), ("conv_w", 4 * LRU_TILES), ("conv_b", LRU_TILES), ("lru_ba", LRU_TILES),
                  ("lru_bx", LRU_TILES), ("lru_lam", LRU_TILES), ("decay", 8)):
    _vec(_name, _n)
NVEC = sum(k for _, k in VECS.values())


class Queue:

    def __init__(self, engine, sem):
        self.engine, self.sem, self.count, self.met = engine, sem, 0, {}

    def wait(self, tokens):
        for t in tokens:
            if t is None:
                continue
            if isinstance(t, list):
                self.wait(t)
                continue
            sem, value = t
            if self.met.get(id(sem), 0) < value:
                self.met[id(sem)] = value
                self.engine.wait_ge(sem, value)

    def put(self, build, *after):
        self.wait(after)
        self.count += 1
        build().then_inc(self.sem, 1)
        return self.sem, self.count

    def quiet(self, build, *after):
        self.wait(after)
        build()

    def dma(self, out, in_, slot, *after):
        self.wait(after)
        slot[1] += 16
        self.engine.dma_start(out, in_).then_inc(slot[0], 16)
        return slot[0], slot[1]


class Ring:

    def __init__(self, slots):
        self.slots, self.free, self.at = slots, [[] for _ in slots], 0

    def take(self):
        i = self.at % len(self.slots)
        assert self.free[i] is not None, "slot still in use"
        after, self.free[i] = self.free[i], None
        self.at += 1
        return i, self.slots[i], after

    def give(self, i, *tokens):
        self.free[i] = list(tokens)


class Block:

    def __init__(self, dram, key=None):
        self.dram, self.tiles, self.key = dram, dram.shape[-1] // P, key


def weight_plan(w):
    plan, trickle = [], deque()

    def start_trickle(layer, chunks):
        trickle.extend(Block(w[f"ada_{layer}"][b], (layer, b)) for c in chunks for b in range(KD * c, KD * c + KD))

    def end_trickle():
        while trickle:
            plan.append(trickle.popleft())

    def add(name, *index):
        block = w[name]
        for i in index:
            block = block[i]
        plan.append(Block(block))
        if trickle:
            plan.append(trickle.popleft())

    def ffn(name13, name2):
        for c, (f0, n) in enumerate(FF_CHUNKS):
            for f in range(f0, f0 + n):
                add(name13, f)
                add(name13, KF + f)
            for o in range(KD):
                add(f"{name2}_{c}", o)

    def ret_out(h):
        for o in range(KD):
            add("ret_out", h, o)

    for b in range(KD):
        plan.append(Block(w["ada_0"][b], (0, b)))
    start_trickle(0, ADA_REST)
    for h in range(RET_HEADS):
        for b in (2 * h, 2 * h + 1, 8 + 2 * h, 9 + 2 * h):
            add("ret_in", b)
        if h:
            ret_out(h - 1)
        for b in range(4):
            add("ret_in", 16 + 4 * h + b)
        for b in range(4):
            add("ret_in", 32 + 4 * h + b)
    ret_out(RET_HEADS - 1)
    end_trickle()
    start_trickle(1, ADA_ALL)
    ffn("w13_0", "w2_0")
    end_trickle()
    for pair in range(NA_HEADS // 2):
        for b in (pair, KD + pair, 2 * KD + pair):
            add("na_qkv", b)
    for o in range(KD):
        add("na_out", o)
    ffn("w13_1", "w2_1")
    for jp in range(2):
        for part in range(3):
            for g in range(DIL_GROUPS):
                add("in_2", 6 * part + 2 * g + jp)
        if jp == 0:
            for t in range(LRU_TILES):
                add("in_2", 18 + t)
                add("in_2", 22 + t)
    for pair in range(MOBA_HEADS // 2):
        for part in range(3):
            add("in_2", 26 + 4 * part + pair)
    for o in range(KD):
        for branch, name in enumerate(("p_a", "p_b", "p_c")):
            add("in_2", 38 + KD * branch + o)
            add(name, o)
    for o in range(KD):
        add("out_2", o)
    ffn("w13_2", "w2_2")
    return plan


def program(nc, a, w, out):
    stack = ExitStack()
    sems = []

    def sem(name):
        s = stack.enter_context(nc.semaphore(name))
        sems.append(s)
        return s

    def dma_slot(name):
        return [sem(name), 0]

    pe, act, dve, pool, sp = (Queue(engine, sem(f"done_{name}")) for name, engine in (
        ("pe", nc.tensor), ("act", nc.scalar), ("dve", nc.vector), ("pool", nc.gpsimd), ("sp", nc.sync)))
    V, S, G, T = nc.vector, nc.scalar, nc.gpsimd, nc.tensor

    class Map:

        def __init__(self, start, end):
            self.at, self.end = start, end

        def sb(self, name, shape, dt=F32):
            size = int(np.prod(shape[1:])) * mybir.dt.size(dt)
            at = (self.at + 31) // 32 * 32
            assert at + size <= self.end, f"{name}: {at + size} > {self.end}"
            self.at = at + size
            return nc.alloc_sbuf_tensor_at(name, list(shape), dt, offset=at)

    keep = Map((nc.sbuf_base + 31) // 32 * 32, nc.sbuf_usable_end)
    h_lat = keep.sb("h_lat", [P, KD, NLAT])
    x_lat = [keep.sb(f"x_lat_{s}", [P, KD, NLAT], F32R) for s in ("hi", "lo")]
    ctx_start = keep.at
    h_ctx = keep.sb("h_ctx", [P, KD, NCTX])
    x_ctx = [keep.sb(f"x_ctx_{s}", [P, KD, NCTX], F32R) for s in ("hi", "lo")]
    ctx_end = keep.at
    NRAW, NSPLIT, AHEAD = 3, 3, 2
    w_raw = keep.sb("w_raw", [P, NRAW, KMAX * P])
    w_hi = keep.sb("w_hi", [P, NSPLIT, KMAX * P], F32R)
    w_lo = keep.sb("w_lo", [P, NSPLIT, KMAX * P], F32R)
    TMPS = 2
    tmp = keep.sb("tmp", [P, TMPS, NLAT])
    total = {g: keep.sb(f"total{g}", [P, TOKENS[g]])[:, :] for g in BOTH}
    norm_vec = keep.sb("norm_vec", [P, 6, KD])
    ones_mean = keep.sb("ones_mean", [P, P])
    ident = keep.sb("ident", [P, P])
    vec = keep.sb("vec", [P, NVEC])
    cond = keep.sb("cond", [P, 2 * D])
    cond_cols = keep.sb("cond_cols", [P, KD, 2])
    dot_out = keep.sb("dot_out", [P, D], mybir.dt.bfloat16)
    mod = [keep.sb(f"mod_{l}", [P, 48, 2]) for l in range(2)]
    table = keep.sb("rel_table", [33, 20])
    log_gamma = keep.sb("log_gamma", [P, 8])
    small = keep.sb("small", [P, 96])

    banks = [stack.enter_context(nc.psum_tensor(f"bank{i}", [P, 512], F32)) for i in range(8)]
    lin = Ring(banks[0:4])
    att = Ring(banks[4:7])
    last = Ring(banks[7:8])

    def vc(name, i=0, n=1):
        c = VECS[name][0] + i
        return vec[:, c:c + n]

    def fence():
        return [(q.sem, q.count) for q in (pe, act, dve, pool) if q.count]

    cond_sem, cond_cols_sem, const_sem, *x_sem = (dma_slot(f"loaded_{n}") for n in ("cond", "cond_cols", "constants", "x_ctx", "x_lat"))
    cond_loaded = sp.dma(cond[:, :], a["cond"].partition_broadcast(P), cond_sem)
    cond_cols_loaded = act.dma(cond_cols[:, :, :], a["cond_cols"], cond_cols_sem)
    for dst, src in ((vec[:, :], a["vec"]), (ident[:, :], a["ident"])):
        consts = act.dma(dst, src, const_sem)
    x_loads = {5: (LAT, h_lat, a["x"]), 9: (CTX, h_ctx, a["ctx"])}
    ones_set = pool.put(lambda: G.memset(ones_mean[:, :], 1.0 / D))
    eps_col = {}
    for i, e in enumerate((LN_EPS, RMS_EPS)):
        eps_col[e] = small[:, i:i + 1]
        eps_set = pool.put(lambda: G.memset(eps_col[e], e))

    PHASE, END = keep.at, keep.end // 32 * 32
    scale_w = Map(PHASE, END).sb("scale_w", [P, KD, D])
    scale_sem = [dma_slot(f"loaded_scale_w{i}") for i in range(2)]
    scale_loaded = [act.dma(scale_w[:, i * KD // 2:(i + 1) * KD // 2, :],
                            w["ada_scale_0"][i * KD // 2:(i + 1) * KD // 2].rearrange("b p k -> p b k"), scale_sem[i])
                    for i in range(2)]

    plan = weight_plan(w)
    h_ready = {}
    raw_sem = [dma_slot(f"loaded_w{i}") for i in range(NRAW)]
    raw_free = [[] for _ in range(NRAW)]
    raw_token, split_token, split_free = {}, {}, [[] for _ in range(NSPLIT)]
    state = {"fetched": 0, "used": 0, "split": 0, "taken": 0}
    tiles_of_split = []

    def fetch_next():
        i = state["fetched"]
        state["fetched"] += 1
        slot, block = i % NRAW, plan[i]
        if i in x_loads:
            g, dst, x = x_loads[i]
            loaded = sp.dma(dst[:, :, :], x, x_sem[g])
            h_ready.update({(k, g): [loaded] for k in range(KD)})
        raw_token[i] = sp.dma(w_raw[:, slot, 0:block.tiles * P], block.dram, raw_sem[slot], raw_free[slot])

    def use_next():
        i = state["used"]
        state["used"] += 1
        while state["fetched"] < min(i + NRAW, len(plan)):
            fetch_next()
        raw, block = i % NRAW, plan[i]
        n = block.tiles * P
        src = w_raw[:, raw, 0:n]
        if block.key is not None:
            raw_free[raw] = [modulation_block(*block.key, src, raw_token[i])]
            return
        j = state["split"]
        state["split"] += 1
        to = j % NSPLIT
        hi, lo = w_hi[:, to, 0:n], w_lo[:, to, 0:n]
        t_hi = act.put(lambda: S.activation(hi, src, ACT.Copy), raw_token[i], split_free[to])
        t_lo = dve.put(lambda: V.tensor_tensor(lo, src, hi.bitcast(F32), ALU.subtract), t_hi, split_free[to])
        raw_free[raw] = [t_lo]
        split_token[j] = t_lo
        tiles_of_split.append(block.tiles)

    def take_weights(kt, ahead=AHEAD):
        j = state["taken"]
        state["taken"] += 1
        while state["split"] <= j + ahead and state["used"] < len(plan):
            use_next()
        assert tiles_of_split[j] == kt, (j, tiles_of_split[j], kt)
        return j

    background = deque()

    def advance(works):
        while works:
            try:
                next(works[0])
                return
            except StopIteration:
                works.popleft()

    def tick(n=1):
        for _ in range(n):
            advance(background)

    def drain():
        while background:
            advance(background)

    class Split:

        def __init__(self, parts):
            self.parts, self.ready, self.read = parts, {}, []

        def ap(self, part, k, g):
            return self.parts[g][part][:, k, :]

    def multiply(x, kt, i, g, ticks):
        slot = i % NSPLIT
        index, bank, after = lin.take()
        o = bank[:, 0:TOKENS[g]]
        pe.wait([split_token[i], after])
        done = 0
        for k in range(kt):
            hi, lo = (t[:, slot, k * P:(k + 1) * P] for t in (w_hi, w_lo))
            pe.wait([x.ready[k, g]])
            pe.quiet(lambda: T.matmul(o, hi, x.ap(0, k, g), start=k == 0, stop=False))
            pe.quiet(lambda: T.matmul(o, hi, x.ap(1, k, g), start=False, stop=False))
            low = lambda: T.matmul(o, lo, x.ap(0, k, g), start=False, stop=k == kt - 1)
            if k < kt - 1:
                pe.quiet(low)
            else:
                token = pe.put(low)
            while done < ticks * (k + 1) // kt:
                advance(background)
                done += 1
        split_free[slot] = [token]
        x.read = [token]
        return index, o, token

    def linear(x, kt, groups, ticks=1):
        i = take_weights(kt)
        outs, left = {}, ticks
        for n, g in enumerate(reversed(groups)):
            share = left if n == len(groups) - 1 else ticks * 2 // 3
            left -= share
            outs[g] = multiply(x, kt, i, g, share)
        return [outs[g] for g in groups]

    def linear_pair(x, kt, context_late, ticks=1):
        if not context_late:
            return linear(x, kt, BOTH, ticks), linear(x, kt, BOTH, ticks)
        blocks = [take_weights(kt), take_weights(kt, AHEAD - 1)]
        lat = [multiply(x, kt, i, LAT, ticks) for i, ticks in zip(blocks, (0, 2 * KD))]
        drain()
        return [[multiply(x, kt, i, CTX, 0), o] for i, o in zip(blocks, lat)]

    tmp_ring = Ring([tmp[:, i, :] for i in range(TMPS)])

    def put_split(x, k, g, src, ready, view=None):
        hi, lo = x.ap(0, k, g), x.ap(1, k, g)
        if view is not None:
            hi, lo = view(hi), view(lo)
        t_hi = act.put(lambda: S.activation(hi, src, ACT.Copy), ready, x.read)
        t_lo = dve.put(lambda: V.tensor_tensor(lo, src, hi.bitcast(F32), ALU.subtract), t_hi, x.read)
        x.ready.setdefault((k, g), [])
        x.ready[k, g] = x.ready[k, g] + [t_lo]
        return [t_hi, t_lo]

    silu_cols = act.put(lambda: S.activation(cond_cols[:, :, :], cond_cols[:, :, :], ACT.Silu), cond_cols_loaded)
    silu_cond = act.put(lambda: S.activation(cond[:, :], cond[:, :], ACT.Silu), cond_loaded)
    mod_ready = {}

    def modulation_block(layer, b, weights, loaded):
        c = b // KD
        for g in range(2):
            t = dve.put(lambda: V.tensor_tensor_reduce(
                out=dot_out[:, :], in0=weights, in1=cond[:, g * D:(g + 1) * D], scale=1.0, scalar=0.0,
                op0=ALU.mult, op1=ALU.add, accum_out=mod[layer][:, b, g:g + 1]), loaded, silu_cond,
                state.get("dot"))
            state["dot"] = [t]
        if b % KD == KD - 1:
            finish_chunk(layer, c, mod[layer][:, KD * c:KD * c + KD, :], t)
        return t

    def finish_chunk(layer, c, src, t):
        dst = mod[layer][:, KD * c:KD * c + KD, :]
        bias = vc("ada_b", 48 * layer + KD * c, KD).unsqueeze(2).to_broadcast([P, KD, 2])
        done = dve.put(lambda: V.tensor_tensor(dst, src, bias, ALU.add), t, consts)
        if c in (1, 4):
            done = dve.put(lambda: V.tensor_scalar(dst, dst, 1.0, None, ALU.add), done)
        mod_ready[layer, c] = done
        return done

    def first_scales():
        at, bank, free = att.take()
        for b in range(KD):
            pe.wait([scale_loaded[b * 2 // KD], silu_cols, free])
            for k in range(KD):
                t = pe.put(lambda: T.matmul(bank[:, 2 * b:2 * b + 2], scale_w[:, b, k * P:(k + 1) * P], cond_cols[:, k, :],
                                            start=k == 0, stop=k == KD - 1))

        def done():
            att.give(at, finish_chunk(0, 1, bank[:, 0:2 * KD].rearrange("p (k g) -> p k g", g=2), t))
            return t

        return done

    def need_mod(layer, c):
        while (layer, c) not in mod_ready:
            use_next()
        return mod_ready[layer, c]

    def mod_col(layer, c, k, g):
        j = 0 if g == LAT else 1
        return mod[layer][:, 8 * c + k, j:j + 1]

    H = {CTX: h_ctx, LAT: h_lat}
    X = Split({CTX: x_ctx, LAT: x_lat})

    def hi_part(x, k, g, src, t):
        return act.put(lambda: S.activation(x.ap(0, k, g), src, ACT.Copy), t, x.read)

    def lo_part(x, k, g, src, t_hi):
        x.ready[k, g] = dve.put(lambda: V.tensor_tensor(x.ap(1, k, g), src, x.ap(0, k, g).bitcast(F32), ALU.subtract),
                                t_hi, x.read)
        return x.ready[k, g]

    def one_apart(n, begin, end):
        begun = begin(0)
        for k in range(n):
            after = begin(k + 1) if k + 1 < n else None
            end(k, begun)
            begun = after
            if k % 2:
                yield

    def at_once(pieces):
        for _ in pieces:
            pass

    def modulate(layer, c, g):
        shift, scale = need_mod(layer, c), need_mod(layer, c + 1)

        def begin(k):
            ti, t_ap, after = tmp_ring.take()
            x, h = t_ap[:, 0:TOKENS[g]], H[g][:, k, :]
            t = dve.put(lambda: V.tensor_scalar(x, h, mod_col(layer, c + 1, k, g), mod_col(layer, c, k, g),
                                                ALU.mult, ALU.add), after, h_ready[k, g], shift, scale)
            h_ready[k, g] = [pool.put(lambda: G.tensor_scalar(h, h, ALPHA, 1.0, ALU.mult, ALU.mult), t)]
            return ti, x, hi_part(X, k, g, x, t)

        def end(k, begun):
            ti, x, t = begun
            tmp_ring.give(ti, lo_part(X, k, g, x, t))

        yield from one_apart(KD, begin, end)

    def add_gated(layer, c, o, groups, outs, sum_up=False):
        gate_ready = need_mod(layer, c)
        for (i, bank, t), g in zip(outs, groups):
            h = H[g][:, o, :]
            t2 = dve.put(lambda: V.scalar_tensor_tensor(h, bank, mod_col(layer, c, o, g), h, ALU.mult, ALU.add),
                         t, h_ready[o, g], gate_ready)
            h_ready[o, g] = [t2]
            lin.give(i, t2)
            if sum_up and o:
                before = H[g][:, 0, :] if o == 1 else total[g]
                total_ready[g] = [pool.put(lambda: G.tensor_tensor(total[g], before, h, ALU.add), t2, total_ready[g])]

    total_ready = {g: [] for g in BOTH}

    def open_sums(g):
        i, bank, free = att.take()
        return dict(i=i, bank=bank[:, 0:TOKENS[g]], free=free, g=g)

    def add_squares(sums, k, src, ready, last_k, later=False):
        close_sums(sums)
        ti, t_ap, after = tmp_ring.take()
        sq = t_ap[:, 0:TOKENS[sums["g"]]]
        t = act.put(lambda: S.activation(sq, src, ACT.Square), ready, after)

        def product():
            sums["token"] = pe.put(lambda: T.matmul(sums["bank"], ones_mean[:, :], sq, start=k == 0, stop=k == last_k),
                                   t, sums["free"], ones_set)
            tmp_ring.give(ti, sums["token"])

        sums["pending"] = product
        if not later:
            close_sums(sums)

    def close_sums(sums):
        if sums.get("pending"):
            sums.pop("pending")()

    def rstd_rows(sums, scale, eps, rows, rows_free):
        close_sums(sums)
        t = act.put(lambda: S.activation(rows, sums["bank"], ACT.Sqrt, bias=eps, scale=scale), sums["token"], rows_free, eps_set)
        att.give(sums["i"], t)
        return dve.put(lambda: V.reciprocal(rows, rows), t)

    norm_vec_used = [[]]

    def layer_norm(which, groups, layer=None, c=None):
        gain, shift_ln = vc("ln_g", which * KD, KD), vc("ln_b", which * KD, KD)
        vec_ready = consts
        if layer is not None:
            shift, scale = need_mod(layer, c), need_mod(layer, c + 1)
            for x, src in ((4, gain), (5, shift_ln)):
                vec_ready = dve.put(lambda: V.tensor_scalar(norm_vec[:, x, :], src, ALPHA, None, ALU.mult), norm_vec_used[0])
            for g in groups:
                col = 0 if g == LAT else 1
                a_, b_ = (mod[layer][:, KD * (c + x):KD * (c + x + 1), col] for x in (1, 0))
                G_, B_ = norm_vec[:, 2 * g, :], norm_vec[:, 2 * g + 1, :]
                dve.put(lambda: V.tensor_tensor(G_, gain, a_, ALU.mult), scale, norm_vec_used[0])
                t = dve.put(lambda: V.tensor_tensor(B_, shift_ln, a_, ALU.mult), scale, norm_vec_used[0])
                vec_ready = dve.put(lambda: V.tensor_tensor(B_, B_, b_, ALU.add), t, shift)

        def normalise(g):
            n, rows = TOKENS[g], total[g]
            i, bank, free = att.take()
            t = pe.put(lambda: T.matmul(bank[:, 0:n], ones_mean[:, :], total[g], start=True, stop=True),
                       free, ones_set, total_ready[g])
            sums = open_sums(g)
            for k in range(KD):
                h = H[g][:, k, :]
                t_c = dve.put(lambda: V.tensor_tensor(h, h, bank[:, 0:n], ALU.subtract), t, h_ready[k, g])
                add_squares(sums, k, h, t_c, KD - 1)
                if k % 2:
                    yield
            att.give(i, t_c)
            t_rows = rstd_rows(sums, 1.0, eps_col[LN_EPS], rows, t)
            yield

            def begin(k):
                h = H[g][:, k, :]
                t_n = dve.put(lambda: V.tensor_tensor(h, h, rows, ALU.mult), t_rows)
                total_ready[g] = [t_n]
                if layer is None:
                    h_ready[k, g] = [pool.put(lambda: G.tensor_scalar(h, h, gain[:, k:k + 1], shift_ln[:, k:k + 1],
                                                                      ALU.mult, ALU.add), t_n)]
                    return
                ti, t_ap, after = tmp_ring.take()
                x = t_ap[:, 0:n]
                t_x = act.put(lambda: S.activation(x, h, ACT.Identity, bias=norm_vec[:, 2 * g + 1, k:k + 1],
                                                   scale=norm_vec[:, 2 * g, k:k + 1]), t_n, after, vec_ready)
                t_hi = hi_part(X, k, g, x, t_x)
                h_ready[k, g] = [pool.put(lambda: G.tensor_scalar(h, h, norm_vec[:, 4, k:k + 1], norm_vec[:, 5, k:k + 1],
                                                                  ALU.mult, ALU.add), t_x, vec_ready)]
                norm_vec_used[0] = [t_x, h_ready[k, g]]
                return ti, x, t_hi

            def end(k, begun):
                if begun:
                    ti, x, t_hi = begun
                    tmp_ring.give(ti, lo_part(X, k, g, x, t_hi))

            yield from one_apart(KD, begin, end)

        at_once(normalise(LAT))
        if CTX in groups:
            background.append(normalise(CTX))

    def rms_norm(sums, gain, first=lambda k, x, t: hi_part(X, k, LAT, x, t), then=lambda k, x, t: lo_part(X, k, LAT, x, t)):
        rows = total[LAT]
        t_rows = rstd_rows(sums, 1.0, eps_col[RMS_EPS], rows, total_ready[LAT])

        def begin(k):
            ti, t_ap, free = tmp_ring.take()
            x = t_ap[:, 0:NLAT]
            t = dve.put(lambda: V.scalar_tensor_tensor(x, H[LAT][:, k, :], vc(gain, k), rows, ALU.mult, ALU.mult),
                        t_rows, free, h_ready[k, LAT])
            total_ready[LAT] = [t]
            return ti, x, first(k, x, t)

        def end(k, begun):
            ti, x, t = begun
            tmp_ring.give(ti, then(k, x, t))

        at_once(one_apart(KD, begin, end))

    def ffn(name, groups, prev, add):
        m = Map(PHASE, END)
        hid = Split({g: [m.sb(f"{name}_hid{g}{s}", [P, KMAX, TOKENS[g]], F32R) for s in ("hi", "lo")] for g in groups})
        silu = Ring([m.sb(f"{name}_silu{i}", [P, NTOK]) for i in range(2)])
        hid.read = prev
        silu.free = [prev, prev]
        for f0, nf in FF_CHUNKS:
            for j in range(nf):
                si, s_ap, free = silu.take()
                t_silu = {}
                late = f0 + j == 0 and CTX in groups
                products = linear_pair(X, KD, True) if late else (linear(X, KD, groups), None)
                for (i, bank, t), g in zip(products[0], groups):
                    cols = slice(START[g], START[g] + TOKENS[g])
                    t_silu[g] = act.put(lambda: S.activation(s_ap[:, cols], bank, ACT.Silu), t, free)
                    lin.give(i, t_silu[g])
                ended = []
                for (i, bank, t), g in zip(products[1] or linear(X, KD, groups), groups):
                    cols = slice(START[g], START[g] + TOKENS[g])
                    t2 = dve.put(lambda: V.tensor_tensor(s_ap[:, cols], bank, s_ap[:, cols], ALU.mult), t, t_silu[g])
                    lin.give(i, t2)
                    hid.ready[j, g] = []
                    ended += put_split(hid, j, g, s_ap[:, cols], t2)
                silu.give(si, *ended)
            for o in range(KD):
                add(o, linear(hid, nf, groups), f0 + nf == KF)

    m = Map(PHASE, END)
    ret_q = m.sb("ret_q", [P, 2, NTOK])
    ret_k = m.sb("ret_k", [P, 2, NTOK])
    ret_vt = m.sb("ret_vt", [P, NTOK])
    ret_v = m.sb("ret_v", [P, NTOK // P, RET_DV])
    y_hi = {g: m.sb(f"ret_y_hi{g}", [P, 4, TOKENS[g]], F32R) for g in BOTH}
    y_at = m.at
    y_lo = {g: m.sb(f"ret_y_lo{g}", [P, 4, TOKENS[g]], F32R) for g in BOTH}
    over = Map(y_at, m.at)
    gate = {g: over.sb(f"ret_gate{g}", [P, 4, TOKENS[g]]) for g in BOTH}
    scores = m.sb("ret_scores", [P, NTOK // P, NLAT])
    scores_ctx = m.sb("ret_scores_ctx", [P, NCTX // P, NCTX])
    WIDE = NLAT + 3 * P
    near = m.sb("ret_near", [P, WIDE])
    far = m.sb("ret_far", [P, NLAT + P])
    rope = [m.sb(f"ret_{n}", [P, NLAT]) for n in ("cos", "sin")]
    ret_sq = m.sb("ret_sq", [P, NLAT])
    ret_u = m.sb("ret_u", [P, NLAT])
    rope_sem = dma_slot("loaded_rope")
    for dst, src in zip(rope, (a["cos"], a["sin"])):
        rope_loaded = pool.dma(dst[:, :], src, rope_sem)
    dist_sem = dma_slot("loaded_dist")

    t = act.put(lambda: S.activation(log_gamma[:, :], vc("decay", 0, 8), ACT.Exp), consts)
    lg_ready = dve.put(lambda: V.tensor_scalar(log_gamma[:, :], log_gamma[:, :], -1.0, None, ALU.mult), t)
    neg_lg, far_bias = small[:, 32:40], small[:, 40:48]
    t = dve.put(lambda: V.tensor_scalar(neg_lg, log_gamma[:, :], -1.0, None, ALU.mult), lg_ready)
    t = dve.put(lambda: V.tensor_scalar(far_bias[:, 0:4], log_gamma[:, 0:4], 512.0, None, ALU.mult), lg_ready)
    lg_ready = dve.put(lambda: V.tensor_scalar(far_bias[:, 4:8], log_gamma[:, 4:8], 256.0, None, ALU.mult), lg_ready)

    near_ready, near_used = [None], [None]

    def decay_tables(h):
        near_ready[0] = []
        half = WIDE // 2
        for c0 in (0, half):
            i0, d_ap, f0 = tmp_ring.take()
            i1, e_ap, f1 = tmp_ring.take()
            d, e1, e2 = d_ap[:, 0:half], e_ap[:, 0:half], near[:, c0:c0 + half]
            t0 = pool.dma(d, w["dist"][:, c0:c0 + half], dist_sem, f0)
            yield
            t = dve.put(lambda: V.tensor_scalar(e1, d, 0.0, None, ALU.max), t0, f1)
            t = act.put(lambda: S.activation(e1, e1, ACT.Exp, scale=log_gamma[:, h:h + 1]), t, lg_ready)
            t_f = pool.put(lambda: G.affine_select(out=e1, in_=e1, compare_op=ALU.is_ge, fill=0.0,
                                                   base=c0 - 3 * P, pattern=[[1, half]], channel_multiplier=-1), t)
            t = dve.put(lambda: V.tensor_scalar(e2, d, 0.0, None, ALU.min), t0, near_used[0])
            t = act.put(lambda: S.activation(e2, e2, ACT.Exp, scale=neg_lg[:, 4 + h:5 + h]), t, lg_ready)
            t_b = pool.put(lambda: G.affine_select(out=e2, in_=e2, compare_op=ALU.is_ge, fill=0.0,
                                                   base=3 * P - c0, pattern=[[-1, half]], channel_multiplier=1), t)
            n = min(half, NLAT + P - c0)
            fo = far[:, c0:c0 + n]
            t_fo = act.put(lambda: S.activation(fo, d[:, 0:n], ACT.Exp, bias=far_bias[:, h:h + 1],
                                                scale=log_gamma[:, h:h + 1]), t0, lg_ready, near_used[0])
            yield
            t_n = dve.put(lambda: V.tensor_tensor(e2, e2, e1, ALU.add), t_f, t_b)
            t_e = act.put(lambda: S.activation(e1[:, 0:n], d[:, 0:n], ACT.Exp, bias=far_bias[:, 4 + h:5 + h],
                                               scale=neg_lg[:, 4 + h:5 + h]), t_n)
            yield
            t_far = dve.put(lambda: V.tensor_tensor(fo, fo, e1[:, 0:n], ALU.add), t_fo, t_e)
            near_ready[0] += [t_n, t_far]
            tmp_ring.give(i0, t_e)
            tmp_ring.give(i1, t_far)

    scales_done = first_scales()
    need_mod(0, 0)
    at_once(decay_tables(0))
    scales_read = scales_done()
    use_next()
    at_once(modulate(0, 0, LAT))
    background.append(modulate(0, 0, CTX))

    ret = {"q": {}, "k": {}, "v": [], "gate": {}, "s_ready": {}, "s_read": [], "sq_read": [],
           **{n: [scales_read] for n in ("qk_read", "v_read", "vt_read", "y_read")}}
    Y = Split({g: [y_hi[g], y_lo[g]] for g in BOTH})
    Y.read = [scales_read]

    def ret_project_qk(h):
        for name, dst in (("q", ret_q), ("k", ret_k)):
            pair = linear_pair(X, KD, h == 0 and name == "q", 5)
            for half in range(2):
                outs = pair[half]
                i, bank, t = outs[0]
                ret[name][half, CTX] = [act.put(lambda: S.activation(
                    dst[:, half, 0:NCTX], bank, ACT.Copy), t, ret["qk_read"])]
                lin.give(i, *ret[name][half, CTX])
                i, bank, t = outs[1]
                lat = slice(NCTX, NTOK)
                if half == 0:
                    t1 = act.put(lambda: S.activation(dst[:, 0, lat], bank, ACT.Copy), t, ret["qk_read"])
                    lin.give(i, t1)
                    continue
                i0, t_ap, free = tmp_ring.take()
                i1, u_ap, free1 = tmp_ring.take()
                x1, x2, p1, p2 = dst[:, 0, lat], dst[:, 1, lat], t_ap[:, 0:NLAT], u_ap[:, 0:NLAT]
                ta = dve.put(lambda: V.tensor_tensor(p1, bank, rope[1][:, :], ALU.mult), t, free, rope_loaded)
                tb = dve.put(lambda: V.tensor_tensor(x2, bank, rope[0][:, :], ALU.mult), t, ret["qk_read"])
                lin.give(i, tb)
                tc = pool.put(lambda: G.tensor_tensor(p2, x1, rope[1][:, :], ALU.mult), t1, free1, rope_loaded)
                td = pool.put(lambda: G.tensor_tensor(x1, x1, rope[0][:, :], ALU.mult), tc)
                te = dve.put(lambda: V.tensor_tensor(x2, x2, p2, ALU.add), tb, tc)
                tf = dve.put(lambda: V.tensor_tensor(x1, x1, p1, ALU.subtract), td, ta)
                tmp_ring.give(i0, tf)
                tmp_ring.give(i1, te)
                ret[name][0, LAT], ret[name][1, LAT] = [tf], [te]

    def ret_v_tiles(j, ts):
        ret["vt_read"] = []
        for s0, ns in ((2, 4), (0, 2)):
            i, bank, free = att.take()
            for s in range(ns):
                cols = slice((s0 + s) * P, (s0 + s + 1) * P)
                t = pe.put(lambda: T.transpose(bank[:, s * P:(s + 1) * P], ret_vt[:, cols], ident[:, :]), ts, free, consts)
            t2 = dve.put(lambda: V.tensor_copy(
                ret_v[:, s0:s0 + ns, j * P:(j + 1) * P], bank[:, 0:ns * P].rearrange("p (s c) -> p s c", c=P)), t, ret["v_read"])
            att.give(i, t2)
            ret["vt_read"].append(t)
            ret["v"].append(t2)
            if s0:
                yield

    def ret_project_vg(h):
        ret["v"] = []
        for j in range(4):
            outs = linear(X, KD, BOTH, 3)
            ts = []
            for (i, bank, t), g in zip(outs, BOTH):
                cols = slice(START[g], START[g] + TOKENS[g])
                ts.append(act.put(lambda: S.activation(ret_vt[:, cols], bank, ACT.Copy), t, ret["vt_read"]))
                lin.give(i, ts[-1])
            background.appendleft(ret_v_tiles(j, ts))
        for j in range(4):
            outs = linear(X, KD, BOTH, 3)
            for (i, bank, t), g in zip(outs, BOTH):
                t2 = act.put(lambda: S.activation(gate[g][:, j, :], bank, ACT.Silu), t, ret["y_read"])
                lin.give(i, t2)
                ret["gate"][j, g] = t2

    def ret_scores():
        reads = []
        for s in range(NTOK // P):
            g_s = CTX if s < 2 else LAT
            for g_t in ((CTX, LAT) if s < 2 else (LAT,)):
                n = TOKENS[g_t]
                i, bank, free = att.take()
                tq = slice(START[g_t], START[g_t] + n)
                for half in range(2):
                    t = pe.put(lambda: T.matmul(
                        bank[:, 0:n], ret_k[:, half, s * P:(s + 1) * P], ret_q[:, half, tq], start=half == 0, stop=half == 1),
                        free, ret["k"][half, g_s], ret["q"][half, g_t])
                if g_s == CTX and g_t == CTX:
                    dst, table = scores_ctx[:, s, :], near[:, 3 * P - s * P:3 * P - s * P + n]
                elif g_s == CTX:
                    dst, table = scores[:, s, :], far[:, P - s * P:P - s * P + n]
                else:
                    dst, table = scores[:, s, :], near[:, 3 * P - (s - 2) * P:3 * P - (s - 2) * P + n]
                t2 = dve.put(lambda: V.scalar_tensor_tensor(
                    dst, bank[:, 0:n], RET_DK ** -0.5, table, ALU.mult, ALU.mult), t, near_ready[0], ret["s_read"])
                att.give(i, t2)
                ret["s_ready"][s, g_t] = t2
                near_used[0] = [t2]
                ret["qk_read"] = [t]
                yield

    def ret_readout():
        for g in (LAT, CTX):
            n = TOKENS[g]
            src = scores if g == LAT else scores_ctx
            nsrc = NTOK // P if g == LAT else NCTX // P
            o_ready = []
            sq, u = ret_sq[:, 0:n], ret_u[:, 0:n]
            for j in range(4):
                i, bank, free = att.take()
                for s in range(nsrc):
                    call = (lambda: T.matmul(bank[:, 0:n], ret_v[:, s, j * P:(j + 1) * P], src[:, s, :],
                                                                 start=s == 0, stop=s == nsrc - 1))
                    t = pe.put(call, free, ret["v"], ret["s_ready"][s, g])
                if j == 0:
                    t_sq = act.put(lambda: S.activation(sq, bank[:, 0:n], ACT.Square), t, ret["sq_read"])
                else:
                    tu = act.put(lambda: S.activation(u, bank[:, 0:n], ACT.Square), t, t_sq)
                    t_sq = pool.put(lambda: G.tensor_tensor(sq, sq, u, ALU.add), tu)
                t_y = dve.put(lambda: V.tensor_tensor(gate[g][:, j, :], bank[:, 0:n], gate[g][:, j, :], ALU.mult), t_sq if j == 0 else tu, ret["gate"][j, g])
                att.give(i, t_y)
                o_ready.append(t_y)
                ret["s_read"] = [t]
                ret["v_read"] = [t]
                yield
            sums = open_sums(g)
            sums["token"] = pe.put(lambda: T.matmul(sums["bank"], ones_mean[:, :], sq, start=True, stop=True),
                                   t_sq, sums["free"], ones_set)
            t = rstd_rows(sums, D / RET_DV, eps_col[RMS_EPS], sq, sums["token"])
            yield
            def begin(j):
                scaled = dve.put(lambda: V.tensor_tensor(gate[g][:, j, :], gate[g][:, j, :], sq, ALU.mult), t, o_ready[j])
                ret["sq_read"] = [scaled]
                return hi_part(Y, j, g, gate[g][:, j, :], scaled)

            at_once(one_apart(4, begin, lambda j, t_hi: lo_part(Y, j, g, gate[g][:, j, :], t_hi)))
            yield

    def ret_out(sum_up=False):
        for o in range(KD):
            add_gated(0, 2, o, BOTH, linear(Y, 4, BOTH), sum_up)
        ret["y_read"] = Y.read

    for h in range(RET_HEADS):
        ret_project_qk(h)
        drain()
        background.append(ret_scores())
        if h:
            ret_out()
        if h + 1 < RET_HEADS:
            background.append(decay_tables(h + 1))
        ret_project_vg(h)
        drain()
        background.append(ret_readout())
    drain()
    ret_out(True)

    prev = fence()
    m = Map(PHASE, END)
    na_y = Split({LAT: [m.sb(f"na_y_{s}", [P, KD, NLAT], F32R) for s in ("hi", "lo")]})
    na_q = Ring([m.sb(f"na_q{i}", [P, NLAT]) for i in range(2)])
    na_k = Ring([m.sb(f"na_k{i}", [P, NTOK]) for i in range(2)])
    na_v = Ring([m.sb(f"na_v{i}", [P, 10, P]) for i in range(2)])
    na_vt = m.sb("na_vt", [P, NTOK])
    FFN_BYTES = 4 * NTOK * (2 * KMAX + 2)
    assert m.at - PHASE >= FFN_BYTES
    na_rel = Ring([m.sb(f"na_rel{i}", [P, ROWS, REL]) for i in range(2)])
    NB = ROWS * BAND
    na_bias = Ring([m.sb(f"na_bias{i}", [P, 3, NB])[:, :, :] for i in range(2)] +
                   [cond[:, (2 + 3 * i) * NB:(5 + 3 * i) * NB].rearrange("p (v c) -> p v c", v=3) for i in range(2)])
    na_mask = m.sb("na_mask", [P, 3, BAND])
    na_p = Ring([m.sb(f"na_p{i}", [P, NCTX + ROWS * BAND]) for i in range(2)])
    na_pt = Ring([m.sb(f"na_pt{i}", [P, NCTX + ROWS * BAND]) for i in range(2)] + [cond[:, 0:NCTX + ROWS * BAND]])
    for r in (na_rel, na_bias):
        r.free = [list(prev) for _ in r.free]
    mask_sem = dma_slot("loaded_na_mask")
    mask_loaded = pool.dma(na_mask[:, :, :], a["na_mask"], mask_sem, prev)
    rel_sem = [dma_slot(f"loaded_rel{i}") for i in range(2)]

    pad_sem = dma_slot("stored_rpb")
    rpb_dram = nc.dram_tensor("rpb_padded", [NA_HEADS * RPB_ROWS, RPB_WIDE], F32)
    half_rows = NA_HEADS * RPB_ROWS // 2
    pad = m.sb("na_pad", [P, 2 * RPB_WIDE])[0:half_rows, :].rearrange("p (a c) -> p a c", a=2)
    t = pool.put(lambda: G.memset(pad, 0.0), prev)
    t = pool.dma(pad[:, :, 16:16 + RPB_COLS], a["rpb"], pad_sem, t)
    rpb_stored = pool.dma(rpb_dram.ap().rearrange("(p a) c -> p a c", a=2), pad, pad_sem, t)
    rpb_size = NA_HEADS * RPB_ROWS * RPB_WIDE
    rpb_copies = nc.dram_tensor("rpb_copies", [QB, rpb_size], F32)
    copy_sem = dma_slot("copied_rpb")
    rpb_stored = pool.dma(rpb_copies.ap(), bass.AP(rpb_dram.ap().tensor, 0, [[0, QB], [1, rpb_size]]), copy_sem, rpb_stored)

    BAND_START = [BAND0[n] - QB * n + QB for n in range(4)]
    VARIANT = [0, 1, 1, 2]
    grid = lambda ap: ap.rearrange("p (r c) -> p r c", c=GRID)

    def na_head_bias(head):
        ri, rel, rfree = na_rel.take()
        for r in range(ROWS):
            src = bass.AP(rpb_copies.ap().tensor, (head * RPB_ROWS + 7 - r) * RPB_WIDE + 15,
                          [[rpb_size - 1, QB], [RPB_WIDE, ROWS], [1, REL]])
            t = pool.dma(rel[r * QB:(r + 1) * QB, :, :], src, rel_sem[ri], rfree, rpb_stored)
        bi, bias, bfree = na_bias.take()
        ts = []
        for v, n in enumerate((0, 1, 3)):
            b0 = BAND_START[n]
            ts.append(pool.put(lambda: G.tensor_tensor(
                bias[:, v, :].rearrange("p (r c) -> p r c", c=BAND), rel[:, :, b0:b0 + BAND],
                na_mask[:, v:v + 1, :].to_broadcast([P, ROWS, BAND]), ALU.add), t, bfree, mask_loaded))
        na_rel.give(ri, *ts)
        return bi, bias, ts


    na_biases = []

    def first_biases():
        for e in range(2):
            yield
            na_biases.append(na_head_bias(e))

    layer_norm(0, BOTH, 0, 3)
    background.append(first_biases())
    ffn("ffn0", BOTH, prev, lambda o, outs, end: add_gated(0, 5, o, BOTH, outs, end))
    layer_norm(1, BOTH, 1, 0)

    def attend(jobs, p_ring, pt_ring):
        def stage_scores(job):
            n_all = sum(s[0] for s in job["segs"])
            """Scores with their bias, and the softmax over all keys, one query a partition."""
            pi, p_full, p_free = p_ring.take()
            p = p_full[:, 0:n_all]
            col, written = 0, []
            for n, mms, bias, view, place in job["segs"]:
                i, bank, free = att.take()
                for x, (lhsT, rhs) in enumerate(mms):
                    t = pe.put(lambda: T.matmul(
                        view(bank[:, 0:n]), lhsT, rhs, start=True, stop=True), free, job["ready"])
                dst = p[:, col:col + n]
                if bias is None:
                    t2 = act.put(lambda: S.activation(dst, bank[:, 0:n], ACT.Copy), t, p_free)
                else:
                    t2 = dve.put(lambda: V.tensor_tensor(place(dst), view(bank[:, 0:n]), view(bias), ALU.add),
                                 t, p_free, job["bias_ready"])
                att.give(i, t2)
                written.append(t2)
                col += n
            job["scored"] = t
            job["bias_read"](written)
            neg, total, inv = (small[:, 48 + 3 * pi + x:49 + 3 * pi + x] for x in range(3))
            t = dve.put(lambda: V.tensor_reduce(neg, p, AX, ALU.max, negate=True), written)
            t = act.put(lambda: S.activation(p, p, ACT.Exp, bias=neg, accum_out=total), t)
            t = dve.put(lambda: V.reciprocal(inv, total), t)
            job["p"] = (pi, p, dve.put(lambda: V.tensor_scalar(p, p, inv, None, ALU.mult), t))

        def stage_transpose(job):
            pi, p, t_p = job["p"]
            n = p.shape[-1] // P
            qi, pt, pt_free = pt_ring.take()
            ts = []
            for c0 in range(0, n, 4):
                nc_ = min(4, n - c0)
                i, bank, free = att.take()
                for c in range(nc_):
                    t = pe.put(lambda: T.transpose(bank[:, c * P:(c + 1) * P], p[:, (c0 + c) * P:(c0 + c + 1) * P], ident[:, :]),
                               t_p, free)
                dst = pt[:, c0 * P:(c0 + nc_) * P]
                t2 = act.put(lambda: S.activation(dst, bank[:, 0:nc_ * P], ACT.Copy), t, pt_free)
                att.give(i, t2)
                ts.append(t2)
            p_ring.give(pi, t)
            job["pt"] = (qi, pt, ts)

        def stage_values(pair):
            i, bank, free = last.take()
            nv = len(pair[0]["vals"])
            pe.wait([free] + [x for job in pair for x in (job["pt"][2], job["v_ready"])])
            for c in range(nv):
                for job in pair:
                    rows = slice(64 * job["half"], 64 * job["half"] + 64)
                    t = pe.put(lambda: T.matmul(bank[rows, 0:P], job["vals"][c], job["pt"][1][:, c * P:(c + 1) * P],
                                                start=c == 0, stop=c == nv - 1))
            for job in pair:
                pt_ring.give(job["pt"][0], t)
            last.give(i, *pair[1]["finish"](bank[:, 0:P], t))
            if pair[1].get("done"):
                pair[1]["done"](t)

        for s in range(len(jobs) + 2):
            if s < len(jobs):
                stage_scores(jobs[s])
            if s % 2 == 1 and s > 1:
                stage_values(jobs[s - 3:s - 1])
            if 0 <= s - 1 < len(jobs):
                stage_transpose(jobs[s - 1])
            yield

    plain = lambda ap: ap

    prev = fence()
    for r in (na_q, na_k, na_v, na_p, na_pt):
        r.free = [list(prev) for _ in r.free]
    for i in range(2):
        na_bias.free[2 + i] = list(prev)
    na_y.read = prev
    vt_read = [prev]

    def na_pair(pair):
        qi, q, qfree = na_q.take()
        (i, bank, t), = linear(X, KD, ONLY_LAT, 3)
        tq = act.put(lambda: S.activation(q[:, :].rearrange("p (n r c) -> p r n c", r=ROWS, c=QB),
                                          bank.rearrange("p (r n c) -> p r n c", r=ROWS, c=QB),
                                          ACT.Copy, scale=HEAD ** -0.5), t, qfree)
        lin.give(i, tq)
        ki, kk, kfree = na_k.take()
        tk = []
        k_outs, v_outs = linear_pair(X, KD, pair == 0, 4)
        for (i, bank, t), g in zip(k_outs, BOTH):
            tk.append(act.put(lambda: S.activation(kk[:, START[g]:START[g] + TOKENS[g]], bank, ACT.Copy), t, kfree))
            lin.give(i, tk[-1])
        vi, vv, vfree = na_v.take()
        tv = []
        for (i, bank, t), g in zip(v_outs, BOTH):
            dst = na_vt[:, START[g]:START[g] + TOKENS[g]]
            if g == LAT:
                dst, bank = dst.rearrange("p (c r) -> p r c", r=ROWS), grid(bank)
            tv.append(act.put(lambda: S.activation(dst, bank, ACT.Copy), t, vt_read[0]))
            lin.give(i, tv[-1])
        tiles = [na_vt[:, s * P:(s + 1) * P] for s in range(2)]
        for n in range(4):
            for u in range(2):
                c0 = NCTX + ROWS * (BAND0[n] + QB * u)
                tiles.append(na_vt[:, c0:c0 + P])
        v_ready = []
        for c0 in range(0, 10, 4):
            nt = min(4, 10 - c0)
            i, bank, free = att.take()
            for c in range(nt):
                t = pe.put(lambda: T.transpose(bank[:, c * P:(c + 1) * P], tiles[c0 + c], ident[:, :]), tv, free)
            t2 = dve.put(lambda: V.tensor_copy(vv[:, c0:c0 + nt, :], bank[:, 0:nt * P].rearrange("p (s c) -> p s c", c=P)), t, vfree)
            att.give(i, t2)
            v_ready.append(t2)
        vt_read[0] = [t]
        jobs = []
        drain()
        biases = na_biases[2 * pair:]
        if pair + 1 < NA_HEADS // 2:
            na_biases.extend(na_head_bias(2 * pair + 2 + e) for e in range(2))
        for n in range(4):
            for e in range(2):
                rows = slice(64 * e, 64 * e + 64)
                bi, bias, b_ready = biases[e]
                lhsT = q[rows, n * P:(n + 1) * P]
                keys = grid(kk[rows, NCTX:NTOK])[:, :, BAND0[n]:BAND0[n] + BAND]

                def bias_read(ts, n=n, bi=bi):
                    if n == 3:
                        na_bias.give(bi, *ts)

                def finish(bank, t, n=n):
                    view = lambda ap: grid(ap)[:, :, QB * n:QB * n + QB]
                    return put_split(na_y, pair, LAT, bank.rearrange("p (r c) -> p r c", c=QB), t, view=view)

                def done(t, n=n):
                    if n == 3:
                        na_q.give(qi, t)
                        na_k.give(ki, t)
                        na_v.give(vi, t)

                jobs.append(dict(segs=[(NCTX, [(lhsT, kk[rows, 0:NCTX])], None, plain, plain),
                                       (ROWS * BAND, [(lhsT, keys)], bias[:, VARIANT[n], :],
                                        lambda ap: ap.rearrange("p (r c) -> p r c", c=BAND),
                                        lambda ap: ap.rearrange("p (c r) -> p r c", c=BAND))],
                                 ready=[tq] + tk, bias_ready=b_ready, bias_read=bias_read, half=e, v_ready=v_ready,
                                 vals=[vv[:, s, 64 * e:64 * e + 64] for s in (0, 1, 2 + 2 * n, 3 + 2 * n)],
                                 finish=finish, done=done))
        return jobs

    for pair in range(NA_HEADS // 2):
        jobs = na_pair(pair)
        background.append(attend(jobs, na_p, na_pt))
    drain()
    for o in range(KD):
        add_gated(1, 2, o, ONLY_LAT, linear(na_y, KD, ONLY_LAT), True)

    prev = fence()
    layer_norm(2, ONLY_LAT, 1, 3)
    PATTERNS = (("w", 0, 4, 1024), ("d4", 4, 4, 256), ("d16", 8, 4, 256), ("c", 12, 8, 640))
    table_sem, hot_sem, toep_sem, copied_sem = (dma_slot(n) for n in (
        "loaded_table", "loaded_onehot", "stored_toeplitz", "copied_toeplitz"))
    toep = {}

    def relative_bias():
        table_loaded = pool.dma(table[:, :], a["table"], table_sem)
        for name, h0, nh, width in PATTERNS:
            by_distance = nc.dram_tensor(f"toeplitz_{name}", [nh, width], F32)
            for c0 in range(0, width, NLAT):
                n = min(NLAT, width - c0)
                pi, hot, free = tmp_ring.take()
                loaded = pool.dma(hot[0:33, 0:n], a[f"hot_{name}"][:, c0:c0 + n], hot_sem, free)
                yield
                i, bank, bfree = att.take()
                t = pe.put(lambda: T.matmul(bank[0:nh, 0:n], table[:, h0:h0 + nh], hot[0:33, 0:n], start=True, stop=True),
                           loaded, table_loaded, bfree)
                yield
                qi, row, rfree = tmp_ring.take()
                t2 = act.put(lambda: S.activation(row[0:nh, 0:n], bank[0:nh, 0:n], ACT.Copy), t, rfree)
                att.give(i, t2)
                stored = pool.dma(by_distance.ap()[:, c0:c0 + n], row[0:nh, 0:n], toep_sem, t2)
                tmp_ring.give(pi, t)
                pool.wait([stored])
                tmp_ring.give(qi, stored)
                yield
            copies = nc.dram_tensor(f"toeplitz_copies_{name}", [P, nh * width], F32)
            toep["copied"] = pool.dma(copies.ap(), bass.AP(by_distance.ap().tensor, 0, [[0, P], [1, nh * width]]),
                                      copied_sem, stored)
            toep[name] = (copies, nh * width)
            yield

    background.append(relative_bias())
    ffn("ffn1", ONLY_LAT, prev, lambda o, outs, end: add_gated(1, 5, o, ONLY_LAT, outs, end))
    drain()
    layer_norm(3, ONLY_LAT)

    sums = open_sums(LAT)
    for k in range(KD):
        add_squares(sums, k, H[LAT][:, k, :], h_ready[k, LAT], KD - 1)
    rms_norm(sums, "g_mix")

    prev = fence()
    m = Map(PHASE, END)
    o_a = Split({LAT: [m.sb(f"o_a_{s}", [P, 2, NLAT], F32R) for s in ("hi", "lo")]})
    o_b = Split({LAT: [m.sb(f"o_b_{s}", [P, 4, NLAT], F32R) for s in ("hi", "lo")]})
    o_c = Split({LAT: [m.sb(f"o_c_{s}", [P, 4, NLAT], F32R) for s in ("hi", "lo")]})
    for x in (o_a, o_b, o_c):
        x.read = prev
    merge_start = m.at
    DIL_KEYS = NLAT + 2 * P
    U0W = NLAT + 3
    dil_q = [m.sb(f"dil_q{g}", [P, NLAT]) for g in range(3)]
    moba_start = m.at
    dil_k = [m.sb(f"dil_k{g}", [P, NLAT]) for g in range(3)]
    dil_v = m.sb("dil_v", [P, 12, P])
    vt2 = m.sb("vt2", [P, NLAT])
    dil_bias = Ring([m.sb(f"dil_bias{i}", [P, U0W + 2 * P]) for i in range(2)])
    p_ring = Ring([m.sb(f"p2_{i}", [P, DIL_KEYS]) for i in range(2)])
    pt_ring = Ring([m.sb(f"pt2_{i}", [P, DIL_KEYS]) for i in range(2)])
    c = Map(ctx_start, ctx_end)
    lru = {n: c.sb(f"lru_{n}", [P, NLAT + (3 if n == "x" else 0)]) for n in ("x", "g", "xc", "r", "ig", "a", "s", "u")}
    gate_w = c.sb("lru_gate_w", [P, 2, LRU_TILES, P])
    pt_ring.slots.append(c.sb("pt2_2", [P, DIL_KEYS]))
    pt_ring.free.append([])
    for r in (dil_bias, p_ring, pt_ring):
        r.free = [list(prev) for _ in r.free]

    def diagonals(name, head, width, base, step, cols):
        copies, pitch = toep[name]
        return bass.AP(copies.ap().tensor, head * width + base, [[pitch + step, P], [1, cols]])

    bias_sem = [dma_slot(f"loaded_dil_bias{i}") for i in range(2)]

    def dil_head_bias(j):
        bi, bias, free = dil_bias.take()
        pool.dma(bias[:, 0:U0W], diagonals("w", j, 1024, 508, -4, U0W), bias_sem[bi], free, toep["copied"])
        pool.dma(bias[:, U0W:U0W + P], diagonals("d4", j, 256, 127, -1, P), bias_sem[bi])
        t = pool.dma(bias[:, U0W + P:U0W + 2 * P], diagonals("d16", j, 256, 127, -1, P), bias_sem[bi])
        return bi, bias, [t]

    dil = {"read": [prev], "vt": [prev]}
    by4 = lambda ap: ap.rearrange("p (i r) -> p r i", r=4)

    def v_tiles(dst, sources, ready, free_v):
        ts = []
        for c0 in range(0, len(sources), 4):
            nt = min(4, len(sources) - c0)
            i, bank, free = att.take()
            for c in range(nt):
                t = pe.put(lambda: T.transpose(bank[:, c * P:(c + 1) * P], sources[c0 + c], ident[:, :]), ready, free)
            t2 = dve.put(lambda: V.tensor_copy(dst(c0, nt), bank[:, 0:nt * P].rearrange("p (s c) -> p s c", c=P)), t, free_v)
            att.give(i, t2)
            ts.append(t2)
        return ts, t

    def dilated_pair(jp):
        biases = [dil_head_bias(2 * jp + e) for e in range(2)]
        ready = []
        for name, dst in (("q", dil_q), ("k", dil_k)):
            for g in range(3):
                (i, bank, t), = linear(X, KD, ONLY_LAT, 2)
                ready.append(act.put(lambda bank=bank, d=dst[g], s=(HEAD ** -0.5 if name == "q" else 1.0):
                                     S.activation(d[:, :], bank, ACT.Copy, scale=s), t, dil["read"]))
                lin.give(i, ready[-1])
        v_ready = []
        for g in range(3):
            (i, bank, t), = linear(X, KD, ONLY_LAT, 2)
            tv = act.put(lambda: S.activation(vt2[:, :], bank, ACT.Copy), t, dil["vt"])
            lin.give(i, tv)
            src = [vt2[:, s * P:(s + 1) * P] if g == 0 else by4(vt2[:, :])[:, s, :] for s in range(4)]
            ts, t = v_tiles(lambda c0, nt, g=g: dil_v[:, 4 * g + c0:4 * g + c0 + nt, :], src, tv, dil["read"])
            dil["vt"] = [t]
            v_ready += ts
        jobs = []
        for r in range(4):
            for e in range(2):
                rows = slice(64 * e, 64 * e + 64)
                bi, bias, b_ready = biases[e]

                def bias_read(ts, r=r, bi=bi):
                    if r == 3:
                        dil_bias.give(bi, *ts)

                def finish(bank, t, r=r):
                    return put_split(o_a, jp, LAT, bank, t, view=lambda ap: by4(ap)[:, r, :])

                def done(t, r=r):
                    if r == 3:
                        dil["read"] = [t]

                q = [by4(dil_q[g][rows, :])[:, r, :] for g in range(3)]
                segs = [(NLAT, [(q[0], dil_k[0][rows, :])], bias[:, 3 - r:3 - r + NLAT], plain, plain)]
                for g in (1, 2):
                    segs.append((P, [(q[g], by4(dil_k[g][rows, :])[:, r, :])], bias[:, U0W + (g - 1) * P:U0W + g * P], plain, plain))
                jobs.append(dict(segs=segs, ready=ready, bias_ready=b_ready, bias_read=bias_read, half=e, v_ready=v_ready,
                                 vals=[dil_v[:, s, 64 * e:64 * e + 64] for s in (0, 1, 2, 3, 4 + r, 8 + r)],
                                 finish=finish, done=done))
        return jobs

    lru_sem = dma_slot("loaded_lru_gates")
    t = pool.put(lambda: G.memset(gate_w[:, :, :, :], 0.0), prev)
    for which, name in enumerate(("lru_wa", "lru_wx")):
        for e in range(2):
            rows = slice(64 * e, 64 * e + 64)
            gates_loaded = pool.dma(gate_w[rows, which, :, rows], a[name][e], lru_sem, t)
    t_pad = pool.put(lambda: G.memset(lru["x"][:, 0:3], 0.0), prev)
    lam = vc("lru_lam", 0, 4)
    y0, z, z2, acc, sp_c = (small[:, 64 + 4 * i:68 + 4 * i] for i in range(5))
    t = act.put(lambda: S.activation(y0, lam, ACT.Abs), consts)
    t = act.put(lambda: S.activation(y0, y0, ACT.Exp, scale=-1.0), t)
    t = dve.put(lambda: V.tensor_scalar(z, y0, 2.0, None, ALU.add), t)
    t = dve.put(lambda: V.reciprocal(z, z), t)
    t = dve.put(lambda: V.tensor_tensor(z, z, y0, ALU.mult), t)
    t = dve.put(lambda: V.tensor_tensor(z2, z, z, ALU.mult), t)
    t = dve.put(lambda: V.tensor_scalar(acc, z2, 1.0 / 17, 1.0 / 15, ALU.mult, ALU.add), t)
    for d in (13, 11, 9, 7, 5, 3, 1):
        t = dve.put(lambda: V.tensor_tensor(acc, acc, z2, ALU.mult), t)
        t = dve.put(lambda: V.tensor_scalar(acc, acc, 1.0 / d, None, ALU.add), t)
    t = dve.put(lambda: V.tensor_tensor(acc, acc, z, ALU.mult), t)
    t = dve.put(lambda: V.tensor_scalar(y0, lam, -1.0, 0.0, ALU.mult, ALU.max), t)
    t = dve.put(lambda: V.scalar_tensor_tensor(sp_c, acc, 2.0, y0, ALU.mult, ALU.add), t)
    sp_ready = dve.put(lambda: V.tensor_scalar(sp_c, sp_c, -8.0, None, ALU.mult), t)
    lru_free = {"x": [prev, t_pad], "g": [prev], "rest": [prev]}

    def lru_tile(k):
        xt, xc = lru["x"], lru["xc"]
        (i, bank, t), = linear(X, KD, ONLY_LAT, 8)
        tx = act.put(lambda: S.activation(xt[:, 3:3 + NLAT], bank, ACT.Copy), t, lru_free["x"])
        lin.give(i, tx)
        (i, bank2, t), = linear(X, KD, ONLY_LAT, 8)
        gb = lru["g"][:, :]
        tg = act.put(lambda: S.activation(gb, bank2, ACT.Copy), t, lru_free["g"])
        lin.give(i, tg)
        cw = lambda i: vc("conv_w", 4 * k + i)
        t = dve.put(lambda: V.tensor_scalar(xc[:, :], xt[:, 0:NLAT], cw(0), vc("conv_b", k), ALU.mult, ALU.add), tx, t_pad, lru_free["rest"])
        for i_ in range(1, 4):
            t = dve.put(lambda: V.scalar_tensor_tensor(xc[:, :], xt[:, i_:i_ + NLAT], cw(i_), xc[:, :], ALU.mult, ALU.add), t)
        lru_free["x"] = [t]
        t_xc = t
        if k == LRU_TILES - 1:
            drain()
        background.appendleft(lru_tail(k, tg, t_xc))

    def lru_tail(k, tg, t_xc):
        xc, r, ig, la, s, u = (lru[n] for n in ("xc", "r", "ig", "a", "s", "u"))
        gb = lru["g"][:, :]
        t = dve.put(lambda: V.tensor_tensor(u[:, :], gb, gb, ALU.mult), tg, lru_free["rest"])
        t = dve.put(lambda: V.tensor_scalar(u[:, :], u[:, :], 0.044715, 1.0, ALU.mult, ALU.add), t)
        t = dve.put(lambda: V.tensor_tensor(u[:, :], u[:, :], gb, ALU.mult), t)
        yield
        t_u = act.put(lambda: S.activation(u[:, :], u[:, :], ACT.Tanh, scale=(2 / np.pi) ** 0.5), t)
        yield
        gates = []
        for which, (dst, b) in enumerate(((r, "lru_ba"), (ig, "lru_bx"))):
            i, bank3, free = att.take()
            t = pe.put(lambda: T.matmul(bank3[:, :], gate_w[:, which, k, :], xc[:, :], start=True, stop=True), t_xc, free, gates_loaded)
            t2 = act.put(lambda: S.activation(dst[:, :], bank3[:, :], ACT.Sigmoid, bias=vc(b, k)), t, lru_free["rest"])
            att.give(i, t2)
            gates.append(t2)
        yield
        t_la = dve.put(lambda: V.tensor_scalar(la[:, :], r[:, :], sp_c[:, k:k + 1], None, ALU.mult), gates, sp_ready, lru_free["rest"])
        yield
        t_s = act.put(lambda: S.activation(s[:, :], la[:, :], ACT.Tanh, scale=-1.0), t_la)
        t_r = act.put(lambda: S.activation(r[:, :], la[:, :], ACT.Exp, scale=2.0), t_la)
        t_a = act.put(lambda: S.activation(la[:, :], la[:, :], ACT.Exp), t_r, t_s)
        t = dve.put(lambda: V.scalar_tensor_tensor(s[:, :], r[:, :], 1.0, s[:, :], ALU.add, ALU.mult), t_s, t_r)
        yield
        t_s = act.put(lambda: S.activation(s[:, :], s[:, :], ACT.Sqrt), t)
        yield
        t = dve.put(lambda: V.tensor_tensor(ig[:, :], ig[:, :], xc[:, :], ALU.mult), gates, t_xc)
        t = dve.put(lambda: V.tensor_tensor(s[:, :], s[:, :], ig[:, :], ALU.mult), t, t_s)
        t_h = dve.put(lambda: V.tensor_tensor_scan(r[:, :], la[:, :], s[:, :], 0.0, ALU.mult, ALU.add), t, t_a)
        t = dve.put(lambda: V.tensor_scalar(u[:, :], u[:, :], 0.5, 0.5, ALU.mult, ALU.add), t_u)
        t = dve.put(lambda: V.tensor_tensor(u[:, :], u[:, :], gb, ALU.mult), t)
        lru_free["g"] = [t]
        t = dve.put(lambda: V.tensor_tensor(u[:, :], u[:, :], r[:, :], ALU.mult), t, t_h)
        lru_free["rest"] = put_split(o_b, k, LAT, u[:, :], t)

    jobs = dilated_pair(0)
    background.append(attend(jobs, p_ring, pt_ring))
    for k in range(LRU_TILES):
        lru_tile(k)
    jobs = dilated_pair(1)
    drain()
    background.append(attend(jobs, p_ring, pt_ring))

    after_lru = fence()
    c3 = Map(ctx_start, ctx_end)
    mq = Ring([c3.sb(f"moba_q{i}", [P, NLAT]) for i in range(2)])
    mk = Ring([c3.sb(f"moba_k{i}", [P, NLAT]) for i in range(2)])
    mv = Ring([c3.sb(f"moba_v{i}", [P, 4, P]) for i in range(2)])
    mb = Ring([cond[:, i * NLAT:(i + 1) * NLAT] for i in range(4)])
    for r in (mq, mk, mv, mb):
        r.free = [list(after_lru) for _ in r.free]
    mb_sem = [dma_slot(f"loaded_moba_bias{i}") for i in range(4)]

    def moba_pair(pair):
        biases = []
        for e in range(2):
            bi, bias, free = mb.take()
            biases.append((bi, bias, [pool.dma(bias[:, :], diagonals("c", 2 * pair + e, 640, 127, -1, NLAT), mb_sem[bi], free, toep["copied"])]))
        (i, bank, t), = linear(X, KD, ONLY_LAT, 3)
        qi, q, free = mq.take()
        tq = act.put(lambda: S.activation(q[:, :], bank, ACT.Copy, scale=HEAD ** -0.5), t, free)
        lin.give(i, tq)
        (i, bank1, t), = linear(X, KD, ONLY_LAT, 3)
        ki, kk, free = mk.take()
        tk = act.put(lambda: S.activation(kk[:, :], bank1, ACT.Copy), t, free)
        lin.give(i, tk)
        (i, bank2, t), = linear(X, KD, ONLY_LAT, 3)
        tv = act.put(lambda: S.activation(vt2[:, :], bank2, ACT.Copy), t, dil["vt"])
        lin.give(i, tv)
        vi, vv, free = mv.take()
        v_ready, t = v_tiles(lambda c0, nt: vv[:, c0:c0 + nt, :], [vt2[:, s * P:(s + 1) * P] for s in range(4)], tv, free)
        dil["vt"] = [t]
        drain()
        jobs = []
        for n in range(4):
            for e in range(2):
                rows = slice(64 * e, 64 * e + 64)
                bi, bias, b_ready = biases[e]

                def bias_read(ts, n=n, bi=bi):
                    if n == 3:
                        mb.give(bi, *ts)

                def finish(bank, t, n=n):
                    return put_split(o_c, pair, LAT, bank, t, view=lambda ap: ap[:, n * P:(n + 1) * P])

                def done(t, n=n):
                    if n == 3:
                        mq.give(qi, t)
                        mk.give(ki, t)
                        mv.give(vi, t)

                keys = (n + 1) * P
                jobs.append(dict(segs=[(keys, [(q[rows, n * P:(n + 1) * P], kk[rows, 0:keys])],
                                        bias[:, NLAT - keys:NLAT], plain, plain)],
                                 ready=[tq, tk], bias_ready=b_ready, bias_read=bias_read, half=e, v_ready=v_ready,
                                 vals=[vv[:, s, 64 * e:64 * e + 64] for s in range(n + 1)], finish=finish, done=done))
        background.append(attend(jobs, p_ring, pt_ring))

    for pair in range(MOBA_HEADS // 2):
        moba_pair(pair)
    drain()

    prev = fence()
    m = Map(merge_start, END)
    merged = Split({LAT: [m.sb(f"merged_{s}", [P, KD, NLAT], F32R) for s in ("hi", "lo")]})
    merged.read = prev
    c = Map(ctx_start, ctx_end)
    gates_r = Ring([c.sb(f"gate2_{i}", [P, NLAT]) for i in range(3)])
    sum_r = Ring([c.sb(f"sum2_{i}", [P, NLAT]) for i in range(2)])
    for r in (gates_r, sum_r):
        r.free = [list(prev) for _ in r.free]
    for o in range(KD):
        si, mixed, sfree = sum_r.take()
        t_sum = None
        for branch, (x, kt) in enumerate(((o_a, 2), (o_b, 4), (o_c, 4))):
            (i, bank, t), = linear(X, KD, ONLY_LAT)
            gi, gt, free = gates_r.take()
            tg = act.put(lambda: S.activation(gt[:, :], bank, ACT.Sigmoid), t, free)
            lin.give(i, tg)
            (i, bank, t), = linear(x, kt, ONLY_LAT)
            dst = mixed if branch == 0 else gt
            t2 = dve.put(lambda: V.tensor_tensor(dst[:, :], bank, gt[:, :], ALU.mult), t, tg, sfree)
            lin.give(i, t2)
            if branch:
                t2 = dve.put(lambda: V.tensor_tensor(mixed[:, :], mixed[:, :], gt[:, :], ALU.add), t2, t_sum)
            t_sum = t2
            gates_r.give(gi, t2)
        sum_r.give(si, *put_split(merged, o, LAT, mixed[:, :], t_sum))

    def add_plain(o, outs, sums):
        (i, bank, t), = outs
        h = H[LAT][:, o, :]
        t2 = dve.put(lambda: V.tensor_tensor(h, bank, h, ALU.add), t, h_ready[o, LAT])
        h_ready[o, LAT] = [t2]
        lin.give(i, t2)
        if sums:
            add_squares(sums, o, h, t2, KD - 1, later=True)

    sums = open_sums(LAT)
    for o in range(KD):
        add_plain(o, linear(merged, KD, ONLY_LAT), sums)
    prev = fence()
    rms_norm(sums, "g_ffn")
    sums = open_sums(LAT)
    ffn("ffn2", ONLY_LAT, prev, lambda o, outs, end: add_plain(o, outs, sums if end else None))

    out_sem, stored = [dma_slot(f"stored_out{i}") for i in range(2)], []

    def store(k, ap, t):
        end = sp.dma(out[:, k, :], ap, out_sem[k % 2], t)
        stored.append(end)
        return end

    rms_norm(sums, "g_final", lambda k, x, t: t, store)
    sp.wait(stored)
    assert state["used"] == len(plan) and state["taken"] == state["split"]

    stack.close()


def _blocks(m):
    K, N = m.shape
    return np.ascontiguousarray(m.reshape(K // P, P, N // P, P).transpose(2, 1, 0, 3)).reshape(N // P, P, K)


def _cols(v):
    return np.ascontiguousarray(v.reshape(-1, P).T)


def _buckets(dist):
    d = np.maximum(dist, 0)
    df = np.maximum(d, 1).astype(np.float32)
    large = 16 + (np.log(df / np.float32(16)) / np.float32(np.log(2048 / 16)) * np.float32(16)).astype(np.int32)
    return np.where(d < 16, d, np.minimum(large, 31))


def _one_hot(dist, valid, width):
    hot = np.zeros((33, width), np.float32)
    row = np.where(valid, _buckets(dist), 32)
    hot[row, np.arange(len(dist))] = 1.0
    hot[32, len(dist):] = 1.0
    return hot


def _constants():
    t = np.arange(NLAT)
    nf = RET_DK // 4
    inv = np.float32(10000.0) ** (-np.arange(nf, dtype=np.float32) / np.float32(nf))
    ang = np.concatenate([(t // GRID).astype(np.float32)[:, None] * inv, (t % GRID).astype(np.float32)[:, None] * inv], -1)
    c = {"cos": np.ascontiguousarray(np.cos(ang).T), "sin": np.ascontiguousarray(np.sin(ang).T)}
    c["ident"] = np.eye(P, dtype=np.float32)
    c["dist"] = (np.arange(NLAT + 3 * P)[None, :] - np.arange(P)[:, None] - 3 * P).astype(np.float32)
    mask = np.full((P, 3, BAND), NEG, np.float32)
    for v, n in enumerate((0, 1, 3)):
        for q in range(P):
            qc = n * QB + q % QB
            start = min(max(qc - WIN // 2, 0), GRID - WIN)
            for j in range(BAND):
                if start <= BAND0[n] + j < start + WIN:
                    mask[q, v, j] = 0.0
    c["na_mask"] = mask
    i = np.arange(1023)
    c["hot_w"] = _one_hot(511 - i, (511 - i >= 0) & (511 - i <= 128), 1024)
    i = np.arange(255)
    d = 127 - i
    c["hot_d4"] = _one_hot(4 * d, d >= 0, 256)
    c["hot_d16"] = _one_hot(4 * d, (d >= 0) & (d % 4 == 0), 256)
    i = np.arange(639)
    c["hot_c"] = _one_hot(511 - i, 511 - i >= 0, 640)
    return {k: np.ascontiguousarray(v.astype(np.float32)) for k, v in c.items()}


def kernel(**inputs):
    import concourse.bacc as bacc
    from concourse.bass_utils import run_bass_kernel_spmd

    f = {k: np.asarray(v) for k, v in inputs.items()}
    wts = {"ret_in": _blocks(f["ret_w_in"]), "na_qkv": _blocks(f["na_w_qkv"]), "na_out": _blocks(f["na_w_out"]),
           "in_2": _blocks(f["w_in_2"][0]), "out_2": _blocks(f["w_out_2"][0]),
           "p_a": _blocks(f["p_a_2"][0]), "p_b": _blocks(f["p_b_2"][0]), "p_c": _blocks(f["p_c_2"][0]),
           "w13_0": _blocks(f["ffn_w13"][0]), "w13_1": _blocks(f["ffn_w13"][1]), "w13_2": _blocks(f["w_gu_2"][0]),
           "ret_out": np.stack([_blocks(f["ret_w_out"][RET_DV * h:RET_DV * (h + 1)]) for h in range(RET_HEADS)]),
           **{f"ada_{l}": np.ascontiguousarray(f["ada_w"][l].T).reshape(6 * KD, P, D) for l in range(2)},
           "ada_scale_0": _blocks(f["ada_w"][0][:, D:2 * D])}
    for n, w2 in enumerate((f["ffn_w2"][0], f["ffn_w2"][1], f["w_down_2"][0])):
        for c, (f0, k) in enumerate(FF_CHUNKS):
            wts[f"w2_{n}_{c}"] = _blocks(w2[P * f0:P * (f0 + k)])
    vec = np.concatenate([
        _cols(f["ada_b"]), _cols(f["ln_g"]), _cols(f["ln_b"]), _cols(f["g_mix_2"]), _cols(f["g_ffn_2"]),
        _cols(f["g_final_2"]), f["conv_w_2"][0].reshape(4, LRU_TILES, P).transpose(2, 1, 0).reshape(P, 16),
        _cols(f["conv_b_2"]), _cols(f["lru_ba_2"]), _cols(f["lru_bx_2"]), _cols(f["lru_lam_2"]),
        np.broadcast_to(f["ret_decay"].reshape(1, 8), (P, 8))], 1)
    acts = dict(_constants())
    acts["cond_cols"] = np.ascontiguousarray(np.stack([f["c"][0], f["c_ctx"]]).reshape(2, KD, P).transpose(2, 1, 0))
    acts["cond"] = np.concatenate([f["c"][0], f["c_ctx"]])
    acts["vec"] = np.ascontiguousarray(vec)
    acts["x"] = np.ascontiguousarray(f["x"][0].T.reshape(KD, P, NLAT).transpose(1, 0, 2))
    acts["ctx"] = np.ascontiguousarray(f["ctx"][0].T.reshape(KD, P, NCTX).transpose(1, 0, 2))
    acts["rpb"] = np.ascontiguousarray(f["na_rpb"].reshape(NA_HEADS * RPB_ROWS // 2, 2, RPB_COLS))
    acts["table"] = np.concatenate([f["rel_bias_2"], np.full((1, 20), NEG, np.float32)], 0)
    for n in ("lru_wa", "lru_wx"):
        acts[n] = np.ascontiguousarray(f[n + "_2"][0].reshape(LRU_TILES, 2, 64, 64).transpose(1, 2, 0, 3))
    wts["dist"] = acts.pop("dist")

    nc = bacc.Bacc("TRN2", target_bir_lowering=False, num_devices=1)
    arrays, aps = {}, ({}, {})
    for which, group in enumerate((acts, wts)):
        for name, array in group.items():
            arrays[f"in_{name}"] = array
            aps[which][name] = nc.dram_tensor(f"in_{name}", list(array.shape), mybir.dt.from_np(array.dtype),
                                              kind="ExternalInput").ap()
    out = nc.dram_tensor("out_t", [P, KD, NLAT], F32, kind="ExternalOutput")
    program(nc, aps[0], aps[1], out.ap())
    result = run_bass_kernel_spmd(nc, [arrays], core_ids=[0]).results[0]["out_t"]
    return np.ascontiguousarray(result.transpose(2, 1, 0).reshape(1, NLAT, D))
```
